# Optimizing a Trainium2 kernel written in Bass

```python
import math
import jax, jax.numpy as jnp
from jax import lax
import numpy as np

D_MODEL = 1024
BATCH = 1
SEQ = 2048
DEPTH = 1
DEC_BATCH = 8
DEC_SEQ = 4
PAST_LEN = 16384
PAGE_SIZE = 128

D_MIX = D_MODEL
D_RNN = D_MIX // 2
N_RNN_BLOCKS = 8
RNN_BLOCK = D_RNN // N_RNN_BLOCKS
CONV_W = 4
LRU_C = 8.0
HEAD_DIM = 64
N_HEADS = (D_MIX - D_RNN) // HEAD_DIM
N_KV_HEADS = 2
GQA = N_HEADS // N_KV_HEADS
WINDOW = 128
ATT_BLOCK = WINDOW
N_EXPERTS = 64
TOP_K = 6
N_GROUPS = 8
TOPK_GROUPS = 4
D_EXPERT = D_MODEL // 4
D_SHARED = D_MODEL // 4
ROUTE_SCALE = 2.5
MOE_BLOCK = 128
EPS = 1e-6
NEG = -1e30
SPLITS = (D_RNN, 2 * D_RNN, 2 * D_RNN + N_HEADS * HEAD_DIM,
          2 * D_RNN + N_HEADS * HEAD_DIM + N_KV_HEADS * HEAD_DIM)
D_IN = 2 * D_RNN + (N_HEADS + 2 * N_KV_HEADS) * HEAD_DIM

kernel_name = "hymba_rglru_swa_sink_moe_adaln_step"

def rms_norm(x, g):
    xf = x.astype(jnp.float32)
    y = xf * lax.rsqrt(jnp.mean(xf * xf, axis=-1, keepdims=True) + EPS)
    return (y * g.astype(jnp.float32)).astype(x.dtype)

def adaln(c, w, b):
    mod = jnp.einsum('bd,de->be', jax.nn.silu(c), w) + b
    return jnp.split(mod[:, None, :], 6, axis=-1)

def causal_conv(u, prev, w, b):
    T = u.shape[1]
    up = jnp.concatenate([prev.astype(u.dtype), u], axis=1)
    out = b + up[:, 0:T] * w[0]
    for j in range(1, CONV_W):
        out = out + up[:, j:j + T] * w[j]
    return out, up[:, -(CONV_W - 1):]

def rg_lru(u, h0, wa, ba, wx, bx, lam):
    B, T, _ = u.shape
    ub = u.reshape(B, T, N_RNN_BLOCKS, RNN_BLOCK)
    r = jax.nn.sigmoid(jnp.einsum('btni,nij->btnj', ub, wa).reshape(B, T, D_RNN) + ba)
    i = jax.nn.sigmoid(jnp.einsum('btni,nij->btnj', ub, wx).reshape(B, T, D_RNN) + bx)
    log_a = -LRU_C * r.astype(jnp.float32) * jax.nn.softplus(-lam.astype(jnp.float32))
    a = jnp.exp(log_a)
    b_in = jnp.sqrt(-jnp.expm1(2.0 * log_a)) * (i * u).astype(jnp.float32)

    def step(h, ab):
        h = ab[0] * h + ab[1]
        return h, h

    hT, hs = lax.scan(step, h0.astype(jnp.float32), (jnp.swapaxes(a, 0, 1), jnp.swapaxes(b_in, 0, 1)))
    return jnp.swapaxes(hs, 0, 1).astype(u.dtype), hT.astype(h0.dtype)

def alibi_slopes():
    return jnp.exp2(-8.0 * jnp.arange(1, N_HEADS + 1, dtype=jnp.float32) / N_HEADS)

def attend(q, k, v, q_pos, k_pos, sinks):
    s = jnp.einsum('...qhgd,...khd->...hgqk', q, k).astype(jnp.float32) * (HEAD_DIM ** -0.5)
    dist = q_pos[..., :, None] - k_pos[..., None, :]
    valid = (dist >= 0) & (dist <= WINDOW) & (k_pos[..., None, :] >= 0)
    dist = dist[..., None, None, :, :].astype(jnp.float32)
    valid = valid[..., None, None, :, :]
    s = s - alibi_slopes().reshape(N_KV_HEADS, GQA, 1, 1) * dist
    s = jnp.where(valid, s, NEG)
    sink = jnp.broadcast_to(sinks.astype(jnp.float32).reshape(N_KV_HEADS, GQA, 1, 1), s.shape[:-1] + (1,))
    p = jax.nn.softmax(jnp.concatenate([s, sink], axis=-1), axis=-1)[..., :-1]
    return jnp.einsum('...hgqk,...khd->...qhgd', p.astype(v.dtype), v)

def attn_prompt(q, k, v, sinks):
    B, T = q.shape[:2]
    nb = T // ATT_BLOCK
    qb = q.reshape(B, nb, ATT_BLOCK, N_KV_HEADS, GQA, HEAD_DIM)
    pad = ((0, 0), (ATT_BLOCK, 0), (0, 0), (0, 0))
    kp = jnp.pad(k, pad).reshape(B, nb + 1, ATT_BLOCK, N_KV_HEADS, HEAD_DIM)
    vp = jnp.pad(v, pad).reshape(B, nb + 1, ATT_BLOCK, N_KV_HEADS, HEAD_DIM)
    kb = jnp.concatenate([kp[:, :-1], kp[:, 1:]], axis=2)
    vb = jnp.concatenate([vp[:, :-1], vp[:, 1:]], axis=2)
    q_pos = jnp.arange(T, dtype=jnp.int32).reshape(nb, ATT_BLOCK)
    k_pos = (jnp.arange(nb, dtype=jnp.int32)[:, None] - 1) * ATT_BLOCK + jnp.arange(2 * ATT_BLOCK, dtype=jnp.int32)[None, :]
    o = attend(qb, kb, vb, q_pos, k_pos, sinks)
    return o.reshape(B, T, N_HEADS * HEAD_DIM)

def attn_sample(q, k, v, k_buf, v_buf, sinks):
    B, T = q.shape[:2]
    W = k_buf.shape[1]
    kc = jnp.concatenate([k_buf.astype(k.dtype), k], axis=1)
    vc = jnp.concatenate([v_buf.astype(v.dtype), v], axis=1)
    q_pos = PAST_LEN + jnp.arange(T, dtype=jnp.int32)
    k_pos = PAST_LEN - W + jnp.arange(W + T, dtype=jnp.int32)
    o = attend(q.reshape(B, T, N_KV_HEADS, GQA, HEAD_DIM), kc, vc, q_pos, k_pos, sinks)
    return o.reshape(B, T, N_HEADS * HEAD_DIM), kc[:, -W:], vc[:, -W:]

def route(h, w_r, bias):
    N = h.shape[0]
    s = jax.nn.sigmoid(jnp.einsum('nd,de->ne', h, w_r).astype(jnp.float32))
    sb = s + bias.astype(jnp.float32)
    gscore = lax.top_k(sb.reshape(N, N_GROUPS, N_EXPERTS // N_GROUPS), 2)[0].sum(-1)
    _, gidx = lax.top_k(gscore, TOPK_GROUPS)
    gmask = jnp.any(gidx[:, :, None] == jnp.arange(N_GROUPS)[None, None, :], axis=1)
    emask = jnp.repeat(gmask, N_EXPERTS // N_GROUPS, axis=1)
    _, eidx = lax.top_k(jnp.where(emask, sb, NEG), TOP_K)
    w = jnp.take_along_axis(s, eidx, axis=-1)
    w = w / jnp.sum(w, axis=-1, keepdims=True) * ROUTE_SCALE
    return eidx, w

def routed_experts(h, eidx, gw, w_g, w_u, w_d):
    N = h.shape[0]
    R = N * TOP_K
    e_flat = eidx.reshape(R)
    tok_flat = jnp.repeat(jnp.arange(N, dtype=jnp.int32), TOP_K)
    w_flat = gw.reshape(R)
    counts = jnp.bincount(e_flat, length=N_EXPERTS)
    padded = (counts + MOE_BLOCK - 1) // MOE_BLOCK * MOE_BLOCK
    pad_end = jnp.cumsum(padded)
    pad_start = pad_end - padded
    start = jnp.cumsum(counts) - counts
    order = jnp.argsort(e_flat)
    e_sorted = e_flat[order]
    dest = pad_start[e_sorted] + jnp.arange(R, dtype=jnp.int32) - start[e_sorted]
    n_blocks = -(-R // MOE_BLOCK) + N_EXPERTS
    rows = n_blocks * MOE_BLOCK
    row_tok = jnp.zeros((rows,), jnp.int32).at[dest].set(tok_flat[order])
    row_w = jnp.zeros((rows,), jnp.float32).at[dest].set(w_flat[order])
    blk_e = jnp.minimum(jnp.searchsorted(pad_end, jnp.arange(n_blocks, dtype=jnp.int32) * MOE_BLOCK, side='right'), N_EXPERTS - 1)

    def run_block(args):
        tok, e = args
        xb = h[tok]
        a = xb @ w_g[e]
        b = xb @ w_u[e]
        return (jax.nn.silu(a) * b) @ w_d[e]

    yb = lax.map(run_block, (row_tok.reshape(n_blocks, MOE_BLOCK), blk_e)).reshape(rows, D_MODEL)
    yb = yb * row_w[:, None].astype(yb.dtype)
    return jax.ops.segment_sum(yb, row_tok, num_segments=N)

def block(x, c, P, k_buf, v_buf, conv_prev, h0, prompt):
    B, T, _ = x.shape
    sh1, sc1, g1, sh2, sc2, g2 = adaln(c, P['ada_w'], P['ada_b'])
    h = rms_norm(x, P['norm_mix']) * (1 + sc1) + sh1
    proj = jnp.einsum('btd,de->bte', h, P['w_in'])
    xr, yr, q, k, v = jnp.split(proj, SPLITS, axis=-1)
    u, conv_new = causal_conv(xr, conv_prev, P['conv_w'], P['conv_b'])
    hr, h_new = rg_lru(u, h0, P['gate_a_w'], P['gate_a_b'], P['gate_x_w'], P['gate_x_b'], P['lru_lambda'])
    out_r = hr * jax.nn.gelu(yr)
    q = rms_norm(q.reshape(B, T, N_HEADS, HEAD_DIM), P['q_norm'])
    k = rms_norm(k.reshape(B, T, N_KV_HEADS, HEAD_DIM), P['k_norm'])
    v = v.reshape(B, T, N_KV_HEADS, HEAD_DIM)
    if prompt:
        out_a = attn_prompt(q, k, v, P['attn_sinks'])
        wk = min(WINDOW, T)
        k_new, v_new = k[:, -wk:], v[:, -wk:]
    else:
        out_a, k_new, v_new = attn_sample(q, k, v, k_buf, v_buf, P['attn_sinks'])
    mixed = jnp.einsum('bte,ed->btd', jnp.concatenate([out_r, out_a], axis=-1), P['w_out'])
    x = x + g1 * mixed
    h = (rms_norm(x, P['norm_ffn']) * (1 + sc2) + sh2).reshape(B * T, D_MODEL)
    eidx, gw = route(h, P['router_w'], P['router_bias'])
    routed = routed_experts(h, eidx, gw, P['exp_w_gate'], P['exp_w_up'], P['exp_w_down'])
    shared = (jax.nn.silu(h @ P['sh_w_gate']) * (h @ P['sh_w_up'])) @ P['sh_w_down']
    x = x + g2 * (routed + shared).reshape(B, T, D_MODEL)
    return x, k_new, v_new, conv_new, h_new

def setup_inputs(seed: int = 0) -> dict:
    key = jax.random.key(seed)
    ks = iter(jax.random.split(key, 40))
    f32 = jnp.float32
    nrm = lambda shape, scale: jax.random.normal(next(ks), shape, f32) * scale
    cache_win = min(WINDOW, PAST_LEN)
    u = jax.random.uniform(next(ks), (DEPTH, D_RNN), f32, 0.9, 0.999)
    a0 = u ** (1.0 / LRU_C)
    lam = jnp.log(a0) - jnp.log1p(-a0)
    return {
        'x_prompt': nrm((BATCH, SEQ, D_MODEL), 1.0),
        'x_sample': nrm((DEC_BATCH, DEC_SEQ, D_MODEL), 1.0),
        'c_prompt': nrm((BATCH, D_MODEL), 1.0),
        'c_sample': nrm((DEC_BATCH, D_MODEL), 1.0),
        'cache_k_win': nrm((DEPTH, DEC_BATCH, cache_win, N_KV_HEADS, HEAD_DIM), 1.0),
        'cache_v_win': nrm((DEPTH, DEC_BATCH, cache_win, N_KV_HEADS, HEAD_DIM), 1.0),
        'state_conv': nrm((DEPTH, DEC_BATCH, CONV_W - 1, D_RNN), 1.0),
        'state_rnn': nrm((DEPTH, DEC_BATCH, D_RNN), 0.5),
        'ada_w': nrm((DEPTH, D_MODEL, 6 * D_MODEL), 0.5 * D_MODEL ** -0.5),
        'ada_b': nrm((DEPTH, 6 * D_MODEL), 0.02),
        'norm_mix': 1.0 + nrm((DEPTH, D_MODEL), 0.05),
        'w_in': nrm((DEPTH, D_MODEL, D_IN), D_MODEL ** -0.5),
        'conv_w': nrm((DEPTH, CONV_W, D_RNN), CONV_W ** -0.5),
        'conv_b': nrm((DEPTH, D_RNN), 0.02),
        'gate_a_w': nrm((DEPTH, N_RNN_BLOCKS, RNN_BLOCK, RNN_BLOCK), RNN_BLOCK ** -0.5),
        'gate_a_b': nrm((DEPTH, D_RNN), 0.02),
        'gate_x_w': nrm((DEPTH, N_RNN_BLOCKS, RNN_BLOCK, RNN_BLOCK), RNN_BLOCK ** -0.5),
        'gate_x_b': nrm((DEPTH, D_RNN), 0.02),
        'lru_lambda': lam,
        'q_norm': 1.0 + nrm((DEPTH, HEAD_DIM), 0.05),
        'k_norm': 1.0 + nrm((DEPTH, HEAD_DIM), 0.05),
        'attn_sinks': nrm((DEPTH, N_HEADS), 1.0),
        'w_out': nrm((DEPTH, D_MIX, D_MODEL), D_MIX ** -0.5),
        'norm_ffn': 1.0 + nrm((DEPTH, D_MODEL), 0.05),
        'router_w': nrm((DEPTH, D_MODEL, N_EXPERTS), D_MODEL ** -0.5),
        'router_bias': nrm((DEPTH, N_EXPERTS), 0.01),
        'exp_w_gate': nrm((DEPTH, N_EXPERTS, D_MODEL, D_EXPERT), D_MODEL ** -0.5),
        'exp_w_up': nrm((DEPTH, N_EXPERTS, D_MODEL, D_EXPERT), D_MODEL ** -0.5),
        'exp_w_down': nrm((DEPTH, N_EXPERTS, D_EXPERT, D_MODEL), D_EXPERT ** -0.5),
        'sh_w_gate': nrm((DEPTH, D_MODEL, D_SHARED), D_MODEL ** -0.5),
        'sh_w_up': nrm((DEPTH, D_MODEL, D_SHARED), D_MODEL ** -0.5),
        'sh_w_down': nrm((DEPTH, D_SHARED, D_MODEL), D_SHARED ** -0.5),
    }

def reference(x_prompt, x_sample, c_prompt, c_sample, cache_k_win, cache_v_win, state_conv, state_rnn,
              ada_w, ada_b, norm_mix, w_in, conv_w, conv_b, gate_a_w, gate_a_b, gate_x_w, gate_x_b,
              lru_lambda, q_norm, k_norm, attn_sinks, w_out, norm_ffn, router_w, router_bias,
              exp_w_gate, exp_w_up, exp_w_down, sh_w_gate, sh_w_up, sh_w_down):
    yp, ys = x_prompt, x_sample
    kp_l, vp_l, cp_l, hp_l, ks_l, vs_l, cs_l, hs_l = [], [], [], [], [], [], [], []
    for l in range(DEPTH):
        P = {'ada_w': ada_w[l], 'ada_b': ada_b[l], 'norm_mix': norm_mix[l], 'w_in': w_in[l],
             'conv_w': conv_w[l], 'conv_b': conv_b[l], 'gate_a_w': gate_a_w[l], 'gate_a_b': gate_a_b[l],
             'gate_x_w': gate_x_w[l], 'gate_x_b': gate_x_b[l], 'lru_lambda': lru_lambda[l],
             'q_norm': q_norm[l], 'k_norm': k_norm[l], 'attn_sinks': attn_sinks[l], 'w_out': w_out[l],
             'norm_ffn': norm_ffn[l], 'router_w': router_w[l], 'router_bias': router_bias[l],
             'exp_w_gate': exp_w_gate[l], 'exp_w_up': exp_w_up[l], 'exp_w_down': exp_w_down[l],
             'sh_w_gate': sh_w_gate[l], 'sh_w_up': sh_w_up[l], 'sh_w_down': sh_w_down[l]}
        B = yp.shape[0]
        conv0 = jnp.zeros((B, CONV_W - 1, D_RNN), yp.dtype)
        h0 = jnp.zeros((B, D_RNN), state_rnn.dtype)
        yp, kp, vp, cp, hp = block(yp, c_prompt, P, None, None, conv0, h0, True)
        ys, ks_, vs_, cs_, hs_ = block(ys, c_sample, P, cache_k_win[l], cache_v_win[l], state_conv[l], state_rnn[l], False)
        kp_l.append(kp); vp_l.append(vp); cp_l.append(cp); hp_l.append(hp)
        ks_l.append(ks_); vs_l.append(vs_); cs_l.append(cs_); hs_l.append(hs_)
    return (yp, ys, jnp.stack(kp_l), jnp.stack(vp_l), jnp.stack(cp_l), jnp.stack(hp_l),
            jnp.stack(ks_l), jnp.stack(vs_l), jnp.stack(cs_l), jnp.stack(hs_l))


_drawn_inputs = setup_inputs


def setup_inputs(seed=0):
    import zlib

    import numpy as np

    out = dict(_drawn_inputs(seed))
    spreads = {}
    factors = {'gate_a_b': 7.689, 'gate_x_b': 7.299, 'q_norm': 4.265, 'attn_sinks': 34.365}
    for name, (base, spread) in spreads.items():
        noise = np.random.default_rng([zlib.crc32(name.encode()), seed]).standard_normal(out[name].shape)
        drawn = base * np.exp(spread * noise) if base else spread * noise
        out[name] = __import__('jax').numpy.asarray(drawn.astype(out[name].dtype))
    for name, factor in factors.items():
        out[name] = (out[name] * factor).astype(out[name].dtype)
    return out
```

```python
from contextlib import ExitStack

import concourse.bass as bass
from concourse import mybir

ALU = mybir.AluOpType
ACT = mybir.ActivationFunctionType
AX = mybir.AxisListType
F32 = mybir.dt.float32
I32 = mybir.dt.int32
U32 = mybir.dt.uint32

P = 128
NEG = -1e30
EPS = 1e-6
LRU_C = 8.0
ROUTE_SCALE = 2.5
GELU_C = 0.7978845608028654
GELU_A = 0.044715


def program(nc, x_prompt, x_sample, c_prompt, c_sample, cache_k_win, cache_v_win, state_conv, state_rnn,
            ada_w, ada_b, norm_mix, w_in, conv_w, conv_b, gate_a_w, gate_a_b, gate_x_w, gate_x_b,
            lru_lambda, q_norm, k_norm, attn_sinks, w_out, norm_ffn, router_w, router_bias,
            exp_w_gate, exp_w_up, exp_w_down, sh_w_gate, sh_w_up, sh_w_down,
            y_prompt, y_sample, k_win_prompt, v_win_prompt, conv_prompt, rnn_prompt,
            k_win_sample, v_win_sample, conv_sample, rnn_sample):
    SEQ, D = x_prompt.shape[1], x_prompt.shape[2]
    NS, TS = x_sample.shape[0], x_sample.shape[1]
    KC = D // P
    R = conv_w.shape[2]
    RC = R // P
    HD = q_norm.shape[1]
    NH = attn_sinks.shape[1]
    NKV = cache_k_win.shape[3]
    GQ = NH // NKV
    KVD = NKV * HD
    QD = NH * HD
    QKV = QD + 2 * KVD
    DIN = w_in.shape[2]
    NE = exp_w_gate.shape[1]
    F = exp_w_gate.shape[3]
    NG = 8
    GE = NE // NG
    TG = 4
    TOPK = 6
    NT = SEQ // P
    TAIL = NS * TS
    NTOK = SEQ + TAIL
    HALO = conv_w.shape[1] - 1
    NB = (NTOK * TOPK + NE * (P - 1)) // P
    NB += NB % 2
    NB_MIN = -(-NTOK * TOPK // P)
    NBT = NB + 2
    MOD = 6 * D
    ALL = NT + 1
    assert TAIL <= 32 and KC == 8 and RC == 4 and KVD == P and QD == 4 * P and R == 4 * P and 2 * F == 512

    def dram(name, shape, dt=F32):
        return nc.dram_tensor(name, shape, dt, kind="Internal").ap()

    mod_d = dram("mod_d", [TAIL + 1, MOD])
    mix_d = dram("mix_d", [ALL, P, 2 * RC, P])
    vnew_d = dram("vnew_d", [TAIL, KVD])
    h2_d = dram("h2_d", [NTOK, D])
    xs_d = dram("xs_d", [NTOK, D])
    tok_d = dram("tok_d", [P * NBT, 1], I32)
    blk_d = dram("blk_d", [2 * P, 1], I32)
    y_d = dram("y_d", [NB * P, D])

    with ExitStack() as ctx:
        def sem(name):
            return ctx.enter_context(nc.semaphore(name))

        base = (nc.sbuf_base + 31) // 32 * 32
        KB = 1024
        XW = base + 0
        YW = XW + 58 * KB
        WK = YW + 59 * KB
        end = {"v": WK, "lim": nc.sbuf_usable_end}

        def at(name, shape, off, dt=F32):
            size = 4
            for s in shape[1:]:
                size *= s
            assert off + size <= end["lim"], (name, off, size, end["lim"])
            return nc.alloc_sbuf_tensor_at(name, shape, dt, offset=off), off + (size + 31) // 32 * 32

        o = WK
        ident, o = at("ident", [P, P], o)
        tri, o = at("tri", [P, P], o)
        ones, o = at("ones", [P, P], o)
        mhalf, o = at("mhalf", [P, 16], o)
        epsc, o = at("epsc", [P, 16], o)
        stat, o = at("stat", [P, 4, 40], o)
        idx_all, o = at("idx_all", [P, ALL, 8], o)
        wgt_all, o = at("wgt_all", [P, ALL, 8], o)
        slot_i, o = at("slot_i", [P, ALL, 8], o, I32)
        blkr, o = at("blkr", [1, 2 * P], o, I32)
        gix, o = at("gix", [P, 2, 1], o, I32)
        eix, o = at("eix", [P, 2, 3], o, I32)
        nblk, o = at("nblk", [1, 8], o, I32)
        PERS = o

        ada_wt, _ = at("ada_wt", [P, 2, KC, 512], YW)
        o = end["lim"] - 40 * KB
        o -= o % 32
        cp_t, o = at("cp_t", [P, KC], o)
        cs_t, o = at("cs_t", [P, NS, KC], o)
        cp_h, o = at("cp_h", [P, KC], o)
        cs_h, o = at("cs_h", [P, NS, KC], o)
        csil, o = at("csil", [P, KC, TAIL + 1], o)
        adab, o = at("adab", [TAIL + 1, MOD], o)
        gmix, o = at("gmix", [TAIL + 1, 2, D], o)
        modc, o = at("modc", [TAIL + 1, 2, 512], o)

        win, _ = at("win", [P, KC, DIN], XW)
        o = PERS
        modA, o = at("modA", [P, 2, D], o)
        bias, o = at("bias", [P, NH, 2 * P], o)
        prm, o = at("prm", [P, RC, 40], o)
        gb, o = at("gb", [P, 2 * RC], o)
        lam8, o = at("lam8", [P, RC, 2], o)
        ssq, o = at("ssq", [P, 2], o)
        rst, o = at("rst", [P, 4], o)
        ss10, o = at("ss10", [P, 16], o)
        r10, o = at("r10", [P, 32], o)
        sink, o = at("sink", [P, NH], o)
        mx, o = at("mx", [P, 2, 4, GQ], o)
        esum, o = at("esum", [P, 2, 2, GQ], o)
        hlast, o = at("hlast", [P, RC, 1], o)
        stt, o = at("stt", [P, RC, 36], o)
        xin, o = at("xin", [P, 2, D], o)
        hrow, o = at("hrow", [P, D], o)
        hT, o = at("hT", [P, KC, P], o)
        xrb, o = at("xrb", [P, RC, HALO + P], o)
        u, o = at("u", [P, RC, P], o)
        y_t, o = at("y_t", [P, RC, P], o)
        sq_t, o = at("sq_t", [P, RC, P], o)
        gts, o = at("gts", [P, 2 * RC, P], o)
        a_t, o = at("a_t", [P, RC, P], o)
        th_t, o = at("th_t", [P, RC, P], o)
        b_t, o = at("b_t", [P, RC, P], o)
        outr, o = at("outr", [P, RC, P], o)
        qkv, o = at("qkv", [P, QKV], o)
        qn, o = at("qn", [P, QD + KVD], o)
        qT, o = at("qT", [P, 5, P], o)
        kT, o = at("kT", [P, 2, P], o)
        vb, o = at("vb", [P, 2, KVD], o)
        sc, o = at("sc", [P, 2, GQ, 2 * P], o)
        PT, o = at("PT", [P, GQ, 2, P], o)
        o_small = o
        o = YW + 33 * KB
        gwt, o = at("gwt", [P, 2, RC, P], o)
        prm_r, o = at("prm_r", [40, R], o)
        stt_r, o = at("stt_r", [36, R], o)
        sqj, o = at("sqj", [P, D], o)
        hs_t, o = at("hs_t", [P, RC, P], o)
        orow, o = at("orow", [P, QD], o)
        oT, o = at("oT", [P, RC, P], o)
        qw, o = at("qw", [P, QD + KVD], o)
        ck, o = at("ck", [P, KVD], o)
        qkTt, o = at("qkTt", [P, 5, TAIL], o)
        oTt, o = at("oTt", [P, RC, TAIL], o)
        assert o <= WK, o - WK

        o = YW
        wout, o = at("wout", [P, KC, D], o)
        shgu, o = at("shgu", [P, KC, 2 * F], o)
        shd, o = at("shd", [P, 2, D], o)
        rw, o = at("rw", [P, KC, NE], o)
        assert o <= WK
        o = PERS
        iota, o = at("iota", [P, NE], o)
        mrun, o = at("mrun", [P, NE], o)
        msk_all, o = at("msk_all", [P, ALL, NE], o)
        pos_all, o = at("pos_all", [P, ALL, NE], o)
        keepC = o
        modB, o = at("modB", [P, 3, D], o)
        modG, o = at("modG", [P, D], o)
        mixb, o = at("mixb", [P, 2, 2 * RC, P], o)
        xb, o = at("xb", [P, 2, D], o)
        x2, o = at("x2", [P, 2, D], o)
        h2, o = at("h2", [P, D], o)
        h2T, o = at("h2T", [P, KC, P], o)
        tmpB, o = at("tmpB", [P, D], o)
        sg, o = at("sg", [P, 2, F], o)
        actr, o = at("actr", [P, F], o)
        actT, o = at("actT", [P, 2, P], o)
        xso, o = at("xso", [P, D], o)
        rt_s, o = at("rt_s", [P, NE], o)
        rt_b, o = at("rt_b", [P, NE], o)
        rt_m, o = at("rt_m", [P, NE], o)
        rt_8, o = at("rt_8", [P, NG, 8], o)
        rt_g, o = at("rt_g", [P, 4, 8], o)
        rt_u, o = at("rt_u", [P, 2, 8], o, U32)
        rt_oh, o = at("rt_oh", [P, TOPK, NE], o)
        rt_t, o = at("rt_t", [P, TOPK, NE], o)
        rbias, o = at("rbias", [P, NE], o)
        ssqB, o = at("ssqB", [P, 4], o)
        sqB, o = at("sqB", [P, D], o)
        yzero, o = at("yzero", [P, D], o)


        o = keepC + 16 * KB
        cnt, o = at("cnt", [P, 6, NE], o)
        cnti, o = at("cnti", [P, 2, NE], o, I32)
        ohC, o = at("ohC", [P, TOPK, NE], o)
        slotf, o = at("slotf", [P, ALL, 8], o)
        slotg, o = at("slotg", [P, ALL, 8], o)
        dlow, o = at("dlow", [P, ALL, 8], o, I32)
        dsti, o = at("dsti", [P, ALL, 8], o, I32)
        toki, o = at("toki", [P, ALL], o, I32)
        zer, o = at("zer", [P, NBT], o, I32)
        blkf, o = at("blkf", [P, 2, NE], o)
        blki, o = at("blki", [P, 2], o, I32)
        iotp, o = at("iotp", [P, 2], o)

        wg, _ = at("wg", [P, 2, 3, KC * F], XW)
        o = PERS
        tokt, o = at("tokt", [P, NBT], o, I32)
        xg, o = at("xg", [P, 2, D], o)
        xgT, o = at("xgT", [P, 2, KC, P], o)
        sgD, o = at("sgD", [P, 2, F], o)
        actD, o = at("actD", [P, F], o)
        actDT, o = at("actDT", [P, 2, P], o)
        ysb, o = at("ysb", [P, 2, D], o)
        o = YW
        yg, o = at("yg", [P, 2, TOPK // 2, D], o)
        acc, o = at("acc", [P, 2, D], o)
        xe, o = at("xe", [P, 2, D], o)
        g2b, o = at("g2b", [P, D], o)
        assert o <= WK

        psT = ctx.enter_context(nc.psum_tensor("psT", [P, 1024], F32))
        psP = ctx.enter_context(nc.psum_tensor("psP", [P, 1024], F32))
        psQ = ctx.enter_context(nc.psum_tensor("psQ", [P, 1024], F32))
        psS = ctx.enter_context(nc.psum_tensor("psS", [P, 1024], F32))

        names = """c_in norms_in ada_psum_ready mod_row_ready mod_bank_free csil_ready c_tanh prm_in prm_psum prm_ready sink_in
            qw_in gate_w_zero gate_w_in const_ready bias_ready modA_in win_in tailmod_in
            ssq_ready rstd_ready h_ready hT_psum hT_ready xr_psum xr_ready conv_ready yr_psum y_ready
            gates_psum gates_sum gates_tanh loga_ready a_ready b2_ready bsqrt_ready gelu_in gelu_tanh
            outr_ready qkv1_psum qkv2_psum qkv_ready ss10_ready r10_ready qn_ready v_ready qkT_psum qkT_ready
            s_psum s_read m_ready p_ready pT_psum pT_ready o_psum o_ready oT_psum oT_ready
            lam_exp lam_one lam_ln lam_ready
            kwin_st small_psum small_ready small_st vnew_st smp_ck smp_v smp_q ckT_psum ckT_ready smp_v0 cachecp_st
            wB_in modB_in rbias_in mixed_psum x2_ready ssqB_ready rstdB_ready h2_ready h2T_psum h2T_ready
            router_psum rtanh shup_psum shtanh act_ready actT_psum actT_ready shd_psum xs_ready
            pos_psum msk_ready iota_ready h2_st tailmodB_in mrun_ready iotp_ready y_all rows_used yzero_ready yzero_st
            cnt_psum cnt_read blk_ready blk_st blkr_in zero_st zero_ready dst_ready tok_st tokt_in
            xgT_psum xgT_ready up_psum dtanh dact_ready dactT_psum dactT_ready down_psum ysb_ready
            acc_ready g2_in stageA_end""".split()
        S = {n: sem(n) for n in names}
        slots2 = """ada_in mod_st x_in outr_st oT_st mix_in xB_in xs_st gather_in gu_in dn_in y_st yrow_in xe_in out_st""".split()
        S2 = {n: [sem(f"{n}0"), sem(f"{n}1")] for n in slots2}

        block = ctx.enter_context(nc.Block())
        NCH = MOD // 512
        ada_v = ada_w[0].rearrange("(p k) n -> p k n", k=KC)
        SMP = NT

        def bc(ap, n):
            return ap.unsqueeze(len(ap.shape)).to_broadcast(list(ap.shape) + [n])

        @block.sync
        def _(sp):
            sp.dma_start(cp_t[:], c_prompt[0].rearrange("(p k) -> p k", k=KC)).then_inc(S["c_in"], 16)
            sp.dma_start(cs_t[:], c_sample.rearrange("b (p k) -> p b k", k=KC)).then_inc(S["c_in"], 16)
            for s in range(2):
                sp.dma_start(ada_wt[:, s], ada_v[:, :, s * 512:(s + 1) * 512]).then_inc(S2["ada_in"][s], 16)
            with sp.Fori(1, NCH // 2) as j:
                for s in range(2):
                    sp.wait_ge(S["ada_psum_ready"], 2 * j + s - 1)
                    sp.dma_start(ada_wt[:, s], ada_v[:, :, bass.ds(j * 1024 + s * 512, 512)]).then_inc(S2["ada_in"][s], 16)
            sp.dma_start(xin[:, 0], x_prompt[0, 0:P]).then_inc(S2["x_in"][0], 16)
            sp.dma_start(xin[:, 1], x_prompt[0, P:2 * P]).then_inc(S2["x_in"][1], 16)
            sp.dma_start(win[:], w_in[0].rearrange("(p k) n -> p k n", k=KC)).then_inc(S["win_in"], 16)
            for s in range(2):
                sp.wait_ge(S2["mod_st"][s], 16 * (NCH // 2))
            sp.dma_start(modA[:], mod_d[TAIL:TAIL + 1, 0:2 * D].rearrange("a (m d) -> a m d", m=2)
                         .to_broadcast([P, 2, D])).then_inc(S["modA_in"], 16)
            sp.wait_ge(S["ada_psum_ready"], NCH)
            sp.dma_start(wout[:], w_out[0].rearrange("(c p) n -> p c n", p=P)).then_inc(S["wB_in"], 16)

            def step(i, par, nxt=True, proj=True, att=True, n=P):
                if nxt:
                    sp.wait_ge(S["h_ready"], i + 1)
                    sp.dma_start(xin[:, par], x_prompt[0, bass.ds((i + 2) * P, P)]).then_inc(S2["x_in"][par], 16)
                if proj:
                    sp.wait_ge(S["outr_ready"], i + 1)
                    sp.dma_start(mix_d[i, :, 0:RC, 0:n], outr[:, :, 0:n]).then_inc(S2["outr_st"][0], 16)
                if att:
                    sp.wait_ge(S["oT_ready"], i)
                    sp.dma_start(mix_d[i - 1, :, RC:2 * RC, :], oT[:]).then_inc(S2["oT_st"][0], 16)

            step(0, 0, att=False)
            step(1, 1)
            with sp.Fori(1, NT // 2 - 1) as j:
                for s in range(2):
                    step(2 * j + s, s)
            sp.wait_ge(S["h_ready"], NT - 1)
            sp.dma_start(xin[0:TAIL, 0], x_sample.rearrange("b t d -> (b t) d")).then_inc(S2["x_in"][0], 16)
            step(NT - 2, 0, nxt=False)
            sp.wait_ge(S["h_ready"], NT)
            sp.dma_start(modA[0:TAIL], mod_d[0:TAIL, 0:2 * D].rearrange("a (m d) -> a m d", m=2)).then_inc(S["tailmod_in"], 16)
            step(NT - 1, 1, nxt=False)
            sp.wait_ge(S["qn_ready"], NT)
            sp.dma_start(k_win_prompt[0, 0].rearrange("t h d -> t (h d)"), qn[:, QD:]).then_inc(S["kwin_st"], 16)
            sp.dma_start(v_win_prompt[0, 0].rearrange("t h d -> t (h d)"), qkv[:, QD + KVD:]).then_inc(S["kwin_st"], 16)
            step(NT, 0, nxt=False, n=TAIL)
            sp.wait_ge(S["qn_ready"], NT + 1)
            for out, src in ((k_win_sample, qn[0:TAIL, QD:]), (v_win_sample, qkv[0:TAIL, QD + KVD:])):
                for b in range(NS):
                    sp.dma_start(out[0, b, P - TS:P].rearrange("t h d -> t (h d)"), src[b * TS:(b + 1) * TS]).then_inc(S["kwin_st"], 16)
            sp.dma_start(vnew_d, qkv[0:TAIL, QD + KVD:]).then_inc(S["vnew_st"], 16)
            sp.wait_ge(S["vnew_st"], 16)
            sp.wait_ge(S["smp_v0"], 1)
            with sp.Fori(0, NS) as b:
                sp.wait_ge(S["o_psum"], 2 * (b + SMP))
                sp.dma_start(ck[:], cache_k_win[0, b].rearrange("t h d -> t (h d)")).then_inc(S["smp_ck"], 16)
                sp.dma_start(vb[:, 0], cache_v_win[0, b].rearrange("t h d -> t (h d)")).then_inc(S["smp_v"], 16)
                sp.dma_start(vb[0:TS, 1], vnew_d[bass.ds(b * TS, TS)]).then_inc(S["smp_v"], 16)
            sp.wait_ge(S["small_ready"], 1)
            for dst, a, n in ((conv_prompt[0, 0], 0, HALO), (rnn_prompt[0], HALO, 1),
                              (conv_sample[0].rearrange("b j r -> (b j) r"), HALO + 1, NS * HALO),
                              (rnn_sample[0], HALO + 1 + NS * HALO, NS)):
                sp.dma_start(dst, stt_r[a:a + n]).then_inc(S["small_st"], 16)
            sp.wait_ge(S["oT_ready"], NT + NS)
            sp.dma_start(mix_d[NT, :, RC:2 * RC, 0:TAIL], oTt[:]).then_inc(S2["oT_st"][0], 16)
            sp.wait_ge(S2["oT_st"][0], 16 * (NT + 1))
            sp.wait_ge(S2["outr_st"][0], 16 * (NT + 1))
            sp.wait_ge(S["kwin_st"], 16 * (2 + 2 * NS))
            sp.wait_ge(S["small_st"], 64)
            sp.wait_ge(S["cachecp_st"], 32)

            sp.dma_start(shgu[:, :, 0:F], sh_w_gate[0].rearrange("(p k) f -> p k f", k=KC)).then_inc(S["wB_in"], 16)
            sp.dma_start(shgu[:, :, F:2 * F], sh_w_up[0].rearrange("(p k) f -> p k f", k=KC)).then_inc(S["wB_in"], 16)
            sp.dma_start(shd[:], sh_w_down[0].rearrange("(p j) d -> p j d", j=2)).then_inc(S["wB_in"], 16)
            sp.dma_start(rw[:], router_w[0].rearrange("(p k) e -> p k e", k=KC)).then_inc(S["wB_in"], 16)
            sp.dma_start(modB[:], mod_d[TAIL:TAIL + 1, 2 * D:5 * D].rearrange("a (m d) -> a m d", m=3)
                         .to_broadcast([P, 3, D])).then_inc(S["modB_in"], 16)
            sp.dma_start(modG[:], mod_d[TAIL:TAIL + 1, 5 * D:].to_broadcast([P, D])).then_inc(S["modB_in"], 16)
            sp.dma_start(rbias[:], router_bias.to_broadcast([P, NE])).then_inc(S["rbias_in"], 16)

            def load_b(i, par, n=P, free=True):
                if free:
                    sp.wait_ge(S["x2_ready"], i - 1)
                sp.dma_start(mixb[:, par, :, 0:n], mix_d[i, :, :, 0:n]).then_inc(S2["mix_in"][par], 16)
                src = x_prompt[0, bass.ds(i * P, P)] if n == P else x_sample.rearrange("b t d -> (b t) d")
                sp.dma_start(xb[0:n, par], src).then_inc(S2["xB_in"][par], 16)

            def store_h2(i, n=P):
                sp.wait_ge(S["h2_ready"], i + 1)
                sp.dma_start(h2_d[bass.ds(i * P, n)], h2[0:n]).then_inc(S["h2_st"], 16)

            def store_xs(i, n=P):
                sp.wait_ge(S["xs_ready"], i + 1)
                sp.dma_start(xs_d[bass.ds(i * P, n)], xso[0:n]).then_inc(S2["xs_st"][0], 16)

            load_b(0, 0, free=False)
            load_b(1, 1, free=False)
            sp.wait_ge(S["yzero_ready"], 1)
            sp.dma_start(y_d[NB_MIN * P:].rearrange("(p b) d -> p b d", p=P),
                         yzero[:].unsqueeze(1).to_broadcast([P, NB - NB_MIN, D])).then_inc(S["yzero_st"], 16)
            store_h2(0)
            load_b(2, 0)
            store_h2(1)
            with sp.Fori(1, NT // 2 - 1) as j:
                for s in range(2):
                    load_b(2 * j + s + 1, 1 - s)
                    store_xs(2 * j + s - 2)
                    store_h2(2 * j + s)
            load_b(NT - 1, 1)
            store_xs(NT - 4)
            store_h2(NT - 2)
            sp.wait_ge(S["x2_ready"], NT - 1)
            load_b(NT, 0, TAIL)
            store_xs(NT - 3)
            store_h2(NT - 1)
            sp.wait_ge(S["h2_ready"], NT)
            sp.dma_start(modB[0:TAIL], mod_d[0:TAIL, 2 * D:5 * D].rearrange("a (m d) -> a m d", m=3)).then_inc(S["tailmodB_in"], 16)
            store_xs(NT - 2)
            store_h2(NT, TAIL)
            store_xs(NT - 1)
            sp.dma_start(modG[0:TAIL], mod_d[0:TAIL, 5 * D:]).then_inc(S["tailmodB_in"], 16)
            store_xs(NT, TAIL)

            sp.wait_ge(S["zero_ready"], 1)
            sp.dma_start(tok_d.rearrange("(p b) a -> p (b a)", p=P), zer[:]).then_inc(S["zero_st"], 16)
            sp.wait_ge(S["blk_ready"], 1)
            for h in range(2):
                sp.dma_start(blk_d[h * P:(h + 1) * P], blki[:, h:h + 1]).then_inc(S["blk_st"], 16)
            sp.wait_ge(S["blk_st"], 32)
            sp.dma_start(blkr[:], blk_d.rearrange("b a -> a b")).then_inc(S["blkr_in"], 16)
            sp.wait_ge(S["tok_st"], 16 * TOPK * ALL)
            sp.dma_start(tokt[:], tok_d.rearrange("(p b) a -> p (b a)", p=P)).then_inc(S["tokt_in"], 16)
            sp.wait_ge(S["h2_st"], 16 * ALL)
            sp.wait_ge(S2["xs_st"][0], 16 * ALL)
            sp.wait_ge(S["blkr_in"], 16)

            sp.wait_ge(S["yzero_st"], 16)

            def load_gu(b, s):
                e = sp.value_load(blkr[0:1, bass.ds(b, 1)], min_val=0, max_val=NE - 1)
                for m, w in enumerate((exp_w_gate, exp_w_up)):
                    sp.dma_start(wg[:, s, m], w[0, bass.ds(e, 1)].rearrange("a (p k) f -> p (a k f)", k=KC)).then_inc(S2["gu_in"][s], 16)
                return e

            def load_dn(e, s):
                sp.dma_start(wg[:, s, 2], exp_w_down[0, bass.ds(e, 1)].rearrange("a (p j) d -> p (a j d)", j=2)).then_inc(S2["dn_in"][s], 16)

            def store_y(b, s):
                sp.wait_ge(S["ysb_ready"], b + 1)
                sp.dma_start(y_d[bass.ds(b * P, P)], ysb[:, s]).then_inc(S2["y_st"][s], 16)

            for s in range(2):
                load_dn(load_gu(s, s), s)
            last_pair = sp.value_load(nblk[0:1, 0:1], min_val=0, max_val=NB // 2 - 1)
            with sp.Fori(1, NB // 2) as j:
                with sp.If(j < last_pair + 1):
                    for s in range(2):
                        sp.wait_ge(S["up_psum"], 2 * j + s - 1)
                        e = load_gu(2 * j + s, s)
                        sp.wait_ge(S["down_psum"], 2 * j + s - 1)
                        load_dn(e, s)
                        store_y(2 * j + s - 2, s)
                    sp.nop()
            for s in range(2):
                store_y(last_pair * 2 + s, s)
            for s in range(2):
                sp.wait_ge(S2["y_st"][s], last_pair * 16 + 16)
            sp.sem_inc(S["y_all"], 1)

            sp.dma_start(g2b[:], mod_d[TAIL:TAIL + 1, 5 * D:].to_broadcast([P, D])).then_inc(S["g2_in"], 16)
            y_out = y_prompt[0]

            def load_e(t, s, n=P, free=True):
                if free:
                    sp.wait_ge(S["acc_ready"], t - 1)
                sp.dma_start(xe[0:n, s], xs_d[bass.ds(t * P, n)]).then_inc(S2["xe_in"][s], 16)

            def store_e(t, s, n=P):
                sp.wait_ge(S["acc_ready"], t + 1)
                dst = y_out[bass.ds(t * P, P)] if n == P else y_sample.rearrange("b t d -> (b t) d")
                sp.dma_start(dst, acc[0:n, s]).then_inc(S2["out_st"][s], 16)

            load_e(0, 0, free=False)
            load_e(1, 1, free=False)
            with sp.Fori(0, NT // 2 - 1) as j:
                for s in range(2):
                    store_e(2 * j + s, s)
                    load_e(2 * j + s + 2, s)
            store_e(NT - 2, 0)
            load_e(NT, 0, TAIL)
            store_e(NT - 1, 1)
            sp.dma_start(g2b[0:TAIL], mod_d[0:TAIL, 5 * D:]).then_inc(S["g2_in"], 16)
            store_e(NT, 0, TAIL)
            sp.wait_ge(S2["out_st"][0], 16 * (NT // 2 + 1))
            sp.wait_ge(S2["out_st"][1], 16 * (NT // 2))

        @block.gpsimd
        def _(gp):
            nc.gpsimd.memset(ident[:], 0.0)
            nc.gpsimd.memset(tri[:], 1.0)
            nc.gpsimd.memset(ones[:], 1.0)
            nc.gpsimd.memset(mhalf[:], -0.5)
            nc.gpsimd.memset(epsc[:], EPS)
            nc.gpsimd.iota(hrow[:, 0:2 * P], [[-1, 2 * P]], base=P, channel_multiplier=1, allow_small_or_imprecise_dtypes=True)
            gp.drain()
            nc.gpsimd.affine_select(out=ident[:], in_=ident[:], compare_op=ALU.not_equal, fill=1.0, base=0,
                                    pattern=[[-1, P]], channel_multiplier=1)
            nc.gpsimd.affine_select(out=tri[:], in_=tri[:], compare_op=ALU.is_gt, fill=0.0, base=0,
                                    pattern=[[1, P]], channel_multiplier=-1)
            gp.drain().then_inc(S["const_ready"], 1)
            for h in range(NH):
                nc.gpsimd.tensor_scalar(bias[:, h], hrow[:, 0:2 * P], -(2.0 ** (-8.0 * (h + 1) / NH)), None, ALU.mult)
            gp.drain()
            nc.gpsimd.affine_select(out=bias[:], in_=bias[:], compare_op=ALU.is_ge, fill=NEG, base=P,
                                    pattern=[[0, NH], [-1, 2 * P]], channel_multiplier=1)
            gp.drain()
            nc.gpsimd.affine_select(out=bias[:], in_=bias[:], compare_op=ALU.is_ge, fill=NEG, base=0,
                                    pattern=[[0, NH], [1, 2 * P]], channel_multiplier=-1)
            gp.drain().then_inc(S["bias_ready"], 1)
            gp.dma_start(k_win_sample[0, :, 0:P - TS].rearrange("b t h d -> b (t h d)"),
                         cache_k_win[0, :, TS:P].rearrange("b t h d -> b (t h d)")).then_inc(S["cachecp_st"], 16)
            gp.dma_start(v_win_sample[0, :, 0:P - TS].rearrange("b t h d -> b (t h d)"),
                         cache_v_win[0, :, TS:P].rearrange("b t h d -> b (t h d)")).then_inc(S["cachecp_st"], 16)

            def rstd(i, par, n=P):
                gp.wait_ge(S["ssq_ready"], i + 1)
                nc.gpsimd.tensor_tensor(rst[0:n, 2:3], ssq[0:n, par:par + 1], epsc[0:n, 0:1], ALU.add)
                gp.drain()
                nc.gpsimd.tensor_tensor(rst[0:n, par:par + 1], rst[0:n, 2:3], mhalf[0:n, 0:1], ALU.pow).then_inc(S["rstd_ready"], 1)

            def r10_of(i, n=P):
                gp.wait_ge(S["ss10_ready"], i + 1)
                nc.gpsimd.tensor_tensor(r10[0:n, 16:16 + NH + NKV], ss10[0:n, 0:NH + NKV], epsc[0:n, 0:NH + NKV], ALU.add)
                gp.drain()
                nc.gpsimd.tensor_tensor(r10[0:n, 0:NH + NKV], r10[0:n, 16:16 + NH + NKV], mhalf[0:n, 0:NH + NKV],
                                        ALU.pow).then_inc(S["r10_ready"], 1)

            rstd(0, 0)
            with gp.Fori(0, NT // 2 - 1) as j:
                for s in range(2):
                    rstd(2 * j + s + 1, 1 - s)
                    r10_of(2 * j + s)
            rstd(NT - 1, 1)
            r10_of(NT - 2)
            rstd(NT, 0, TAIL)
            r10_of(NT - 1)
            r10_of(NT, TAIL)

            gp.wait_ge(S["rbias_in"], 16)
            nc.gpsimd.iota(iota[:], [[1, NE]], base=0, channel_multiplier=0, allow_small_or_imprecise_dtypes=True)
            gp.drain().then_inc(S["iota_ready"], 1)

            def rstd_b(i, n=P):
                gp.wait_ge(S["ssqB_ready"], i + 1)
                nc.gpsimd.tensor_tensor(ssqB[0:n, 2:3], ssqB[0:n, 0:1], epsc[0:n, 0:1], ALU.add)
                gp.drain()
                nc.gpsimd.tensor_tensor(ssqB[0:n, 1:2], ssqB[0:n, 2:3], mhalf[0:n, 0:1], ALU.pow).then_inc(S["rstdB_ready"], 1)

            with gp.Fori(0, NT) as i:
                rstd_b(i)
            rstd_b(NT, TAIL)

            nc.gpsimd.memset(zer[:], 0).then_inc(S["zero_ready"], 1)
            nc.gpsimd.iota(toki[:], [[P, ALL]], base=0, channel_multiplier=1)
            nc.gpsimd.iota(iotp[:], [[P, 2]], base=0, channel_multiplier=1, allow_small_or_imprecise_dtypes=True)
            gp.drain().then_inc(S["iotp_ready"], 1)
            gp.wait_ge(S["dst_ready"], 1)
            gp.wait_ge(S["zero_st"], 16)
            for t in range(ALL):
                n = P if t < NT else TAIL
                for k in range(TOPK):
                    nc.gpsimd.indirect_dma_start(tok_d, bass.IndirectOffsetOnAxis(ap=dsti[0:n, t, k:k + 1], axis=0),
                                                 toki[0:n, t:t + 1], None).then_inc(S["tok_st"], 16)

            gp.wait_ge(S["tokt_in"], 16)
            gp.wait_ge(S["h2_st"], 16 * ALL)

            def gather(b, s):
                nc.gpsimd.tensor_copy(gix[:, s], tokt[:, bass.ds(b, 1)])
                gp.drain()
                nc.gpsimd.indirect_dma_start(xg[:, s], None, h2_d, bass.IndirectOffsetOnAxis(ap=gix[:, s], axis=0)
                                             ).then_inc(S2["gather_in"][s], 16)

            for s in range(2):
                gather(s, s)
            gp.wait_ge(S["xgT_psum"], 1)
            gather(2, 0)
            last_pair = gp.value_load(nblk[0:1, 0:1], min_val=0, max_val=NB // 2 - 1)
            with gp.Fori(1, NB // 2) as j:
                with gp.If(j < last_pair + 1):
                    for s in range(2):
                        gp.wait_ge(S["xgT_psum"], 2 * j + s)
                        gather(2 * j + s + 1, 1 - s)
                    gp.nop()

            gp.wait_ge(S["y_all"], 1)

            def rows(t, h, n=P, free=True):
                if free:
                    gp.wait_ge(S["rows_used"], 2 * t + h - 1)
                nc.gpsimd.tensor_copy(eix[0:n, h], slot_i[0:n, t, h * 3:h * 3 + 3])
                gp.drain()
                for k in range(TOPK // 2):
                    nc.gpsimd.indirect_dma_start(yg[0:n, h, k], None, y_d, bass.IndirectOffsetOnAxis(
                        ap=eix[0:n, h, k:k + 1], axis=0)).then_inc(S2["yrow_in"][h], 16)

            rows(0, 0, free=False)
            rows(0, 1, free=False)
            with gp.Fori(1, NT) as t:
                for h in range(2):
                    rows(t, h)
            for h in range(2):
                rows(NT, h, TAIL)

        @block.scalar
        def _(act):
            for a, n, src in ((0, HALO + 1, conv_w[0]), (4, 1, conv_b), (5, 1, gate_a_b), (6, 1, gate_x_b), (7, 1, lru_lambda),
                              (8, NS * HALO, state_conv[0].rearrange("b j r -> (b j) r")), (8 + NS * HALO, NS, state_rnn[0])):
                act.dma_start(prm_r[a:a + n], src).then_inc(S["prm_in"], 16)
            act.dma_start(adab[:], ada_b.to_broadcast([TAIL + 1, MOD])).then_inc(S["norms_in"], 16)
            act.dma_start(gmix[:, 0], norm_mix.to_broadcast([TAIL + 1, D])).then_inc(S["norms_in"], 16)
            act.dma_start(gmix[:, 1], norm_ffn.to_broadcast([TAIL + 1, D])).then_inc(S["norms_in"], 16)
            act.dma_start(sink[:], attn_sinks.to_broadcast([P, NH])).then_inc(S["sink_in"], 16)
            for h in range(NH):
                act.dma_start(qw[:, h * HD:(h + 1) * HD], q_norm.to_broadcast([P, HD])).then_inc(S["qw_in"], 16)
            for h in range(NKV):
                act.dma_start(qw[:, QD + h * HD:QD + (h + 1) * HD], k_norm.to_broadcast([P, HD])).then_inc(S["qw_in"], 16)
            act.wait_ge(S["c_in"], 32)
            nc.scalar.activation(cp_h[:], cp_t[:], ACT.Tanh, scale=0.5)
            nc.scalar.activation(cs_h[:], cs_t[:], ACT.Tanh, scale=0.5).then_inc(S["c_tanh"], 1)
            act.wait_ge(S["gate_w_zero"], 1)
            for g, w in enumerate((gate_a_w, gate_x_w)):
                for two in range(2):
                    act.dma_start(gwt[64 * two:64 * two + 64, g, :, 64 * two:64 * two + 64],
                                  w[0].rearrange("(c two) i j -> two i c j", two=2)[two]).then_inc(S["gate_w_in"], 16)
            with act.Fori(0, NCH // 2) as j:
                for s in range(2):
                    act.wait_ge(S["mod_row_ready"], 2 * j + s + 1)
                    act.dma_start(mod_d[:, bass.ds(j * 1024 + s * 512, 512)], modc[:, s]).then_inc(S2["mod_st"][s], 16)
            act.wait_ge(S["lam_exp"], 1)
            nc.scalar.activation(lam8[:, :, 1], lam8[:, :, 1], ACT.Exp, scale=-1.0).then_inc(S["lam_one"], 1)

            def sumsq(i, par, half, n=P):
                act.wait_ge(S2["x_in"][par], 16 * (half + 1))
                nc.scalar.activation(sqj[0:n], xin[0:n, par], ACT.Square, scale=D ** -0.5, accum_out=ssq[0:n, par:par + 1]).then_inc(S["ssq_ready"], 1)

            def hT_out(i, n=P):
                act.wait_ge(S["hT_psum"], i + 1)
                nc.scalar.activation(hT[:, :, 0:n], psT[:].rearrange("p (k t) -> p k t", k=KC)[:, :, 0:n], ACT.Copy).then_inc(S["hT_ready"], 1)

            def exps(n, h):
                act.wait_ge(S["m_ready"], 2 * n + h + 1)
                nc.scalar.activation(esum[:, h, 1], mx[:, h, 2], ACT.Exp)
                for g in range(GQ):
                    last = nc.scalar.activation(sc[:, h, g], sc[:, h, g], ACT.Exp, bias=mx[:, h, 1, g:g + 1],
                                                accum_out=esum[:, h, 0, g:g + 1])
                last.then_inc(S["p_ready"], 1)

            def pT_out(n, h, first=False):
                act.wait_ge(S["pT_psum"], 2 * n + h + 1)
                if not (first and h == 0):
                    act.wait_ge(S["o_psum"], 2 * n + h)
                nc.scalar.activation(PT[:].rearrange("p g b t -> p (g b t)"), psT[:], ACT.Copy).then_inc(S["pT_ready"], 1)

            def oT_out(n, first=False):
                act.wait_ge(S["oT_psum"], n + 1)
                if not first:
                    act.wait_ge(S2["oT_st"][0], 16 * n)
                nc.scalar.activation(oT[:].rearrange("p c t -> p (c t)"), psS[:, 0:512], ACT.Copy).then_inc(S["oT_ready"], 1)

            def step(i, par, half, proj=True, att=True, nxt=True, first=False, n=P, n_next=P):
                a = i - 1
                if nxt:
                    sumsq(i + 1, 1 - par, half + par, n_next)
                if proj:
                    act.wait_ge(S["xr_psum"], i + 1)
                    if not (isinstance(i, int) and i == 0):
                        act.wait_ge(S["conv_ready"], i)
                    if n == P:
                        nc.scalar.activation(xrb[:, :, HALO:HALO + P], psP[:, 0:512].rearrange("p (c t) -> p c t", c=RC),
                                             ACT.Copy).then_inc(S["xr_ready"], 1)
                    else:
                        for c in range(RC):
                            last = nc.scalar.activation(
                                xrb[:, c, 0:NS * (TS + HALO)].rearrange("p (b t) -> p b t", b=NS)[:, :, HALO:],
                                psP[:, c * P:c * P + n].rearrange("p (b t) -> p b t", b=NS), ACT.Copy)
                        last.then_inc(S["xr_ready"], 1)
                if att:
                    act.wait_ge(S["qkT_psum"], a + 1)
                    nc.scalar.activation(qT[:, 0:4].rearrange("p c t -> p (c t)"), psT[:, 0:512], ACT.Copy)
                    nc.scalar.activation(kT[:, 1 - par], psT[:, 512:640], ACT.Copy).then_inc(S["qkT_ready"], 1)
                if proj:
                    act.wait_ge(S["yr_psum"], i + 1)
                    if not (isinstance(i, int) and i == 0):
                        act.wait_ge(S["outr_ready"], i)
                    yps = psP[:, 512:1024].rearrange("p (c t) -> p c t", c=RC)[:, :, 0:n]
                    nc.scalar.activation(y_t[:, :, 0:n], yps, ACT.Copy)
                    nc.scalar.activation(sq_t[:, :, 0:n], yps, ACT.Square).then_inc(S["y_ready"], 1)
                if att:
                    exps(a, 0)
                if proj:
                    act.wait_ge(S["gates_sum"], i + 1)
                    nc.scalar.activation(gts[:, :, 0:n], gts[:, :, 0:n], ACT.Tanh, scale=0.5).then_inc(S["gates_tanh"], 1)
                if att:
                    pT_out(a, 0, first)
                if proj:
                    act.wait_ge(S["loga_ready"], i + 1)
                    nc.scalar.activation(a_t[:, :, 0:n], b_t[:, :, 0:n], ACT.Exp)
                    nc.scalar.activation(th_t[:, :, 0:n], b_t[:, :, 0:n], ACT.Tanh).then_inc(S["a_ready"], 1)
                if att:
                    exps(a, 1)
                if proj:
                    act.wait_ge(S["gelu_in"], i + 1)
                    nc.scalar.activation(sq_t[:, :, 0:n], sq_t[:, :, 0:n], ACT.Tanh, scale=GELU_C).then_inc(S["gelu_tanh"], 1)
                if att:
                    pT_out(a, 1, first)
                if proj:
                    act.wait_ge(S["b2_ready"], i + 1)
                    nc.scalar.activation(b_t[:, :, 0:n], b_t[:, :, 0:n], ACT.Sqrt).then_inc(S["bsqrt_ready"], 1)
                    act.wait_ge(S["qkv2_psum"], i + 1)
                    if att:
                        act.wait_ge(S["v_ready"], i)
                        act.wait_ge(S["qn_ready"], i)
                    if n != P:
                        act.wait_ge(S["kwin_st"], 32)
                    nc.scalar.activation(qkv[0:n], psQ[0:n, 0:QKV], ACT.Copy).then_inc(S["qkv_ready"], 1)
                if nxt:
                    hT_out(i + 1, n_next)
                if att:
                    oT_out(a, first)

            sumsq(0, 0, 0)
            hT_out(0)
            step(0, 0, 0, att=False)
            step(1, 1, 0, first=True)
            with act.Fori(1, NT // 2 - 1) as j:
                for s in range(2):
                    step(2 * j + s, s, j)
            step(NT - 2, 0, NT // 2 - 1)
            step(NT - 1, 1, NT // 2 - 1, n_next=TAIL)
            step(NT, 0, NT // 2, nxt=False, n=TAIL)
            act.wait_ge(S["qkT_psum"], NT + 1)
            nc.scalar.activation(qkTt[:], psT[:, 0:640].rearrange("p (c t) -> p c t", c=5)[:, :, 0:TAIL], ACT.Copy).then_inc(S["qkT_ready"], 1)
            with act.Fori(0, NS) as b:
                act.wait_ge(S["ckT_psum"], b + 1)
                nc.scalar.activation(kT[:, 0], psP[:, 0:P], ACT.Copy).then_inc(S["ckT_ready"], 1)
                exps(b + SMP, 0)
                pT_out(b + SMP, 0)
                exps(b + SMP, 1)
                pT_out(b + SMP, 1)
                act.wait_ge(S["oT_psum"], b + SMP + 1)
                nc.scalar.activation(oTt[:, :, bass.ds(b * TS, TS)], psS[:, 0:512].rearrange("p (c t) -> p c t", c=RC)[:, :, 0:TS],
                                     ACT.Copy).then_inc(S["oT_ready"], 1)

            def step_b(i, par, half, d0=True, d1=True, d2=True, n0=P, n1=P, n2=P):
                if d2:
                    act.wait_ge(S["pos_psum"], i - 1)
                    nc.scalar.activation(actT[:, :, 0:n2], psP[:, 768:1024].rearrange("p (j t) -> p j t", j=2)[:, :, 0:n2], ACT.Copy)
                    nc.scalar.activation(pos_all[:, i - 2], psP[:, 640:640 + NE], ACT.Copy).then_inc(S["actT_ready"], 1)
                if d1:
                    act.wait_ge(S["h2T_psum"], i)
                    nc.scalar.activation(h2T[:, :, 0:n1], psT[:].rearrange("p (k t) -> p k t", k=KC)[:, :, 0:n1], ACT.Copy).then_inc(S["h2T_ready"], 1)
                    act.wait_ge(S["router_psum"], i)
                    nc.scalar.activation(rt_s[0:n1], psP[0:n1, 512:512 + NE], ACT.Tanh, scale=0.5).then_inc(S["rtanh"], 1)
                if d0:
                    act.wait_ge(S["x2_ready"], i + 1)
                    nc.scalar.activation(sqB[0:n0], x2[0:n0, par], ACT.Square, scale=D ** -0.5, accum_out=ssqB[0:n0, 0:1]).then_inc(S["ssqB_ready"], 1)
                if d1:
                    act.wait_ge(S["shup_psum"], i)
                    nc.scalar.activation(sg[0:n1, 0], psP[0:n1, 0:F], ACT.Tanh, scale=0.5).then_inc(S["shtanh"], 1)

            step_b(0, 0, 0, d1=False, d2=False)
            step_b(1, 1, 0, d2=False)
            with act.Fori(1, NT // 2) as j:
                for s in range(2):
                    step_b(2 * j + s, s, j)
            step_b(NT, 0, 0, n0=TAIL)
            step_b(NT + 1, 1, 0, d0=False, n1=TAIL)
            step_b(NT + 2, 0, 0, d0=False, d1=False, n2=TAIL)

            def x_out(b, s):
                act.wait_ge(S["xgT_psum"], b + 1)
                nc.scalar.activation(xgT[:, s].rearrange("p k t -> p (k t)"), psT[:], ACT.Copy).then_inc(S["xgT_ready"], 1)

            def tanh_d(b, s):
                act.wait_ge(S["up_psum"], b + 1)
                nc.scalar.activation(sgD[:, s], psP[:, s * 512:s * 512 + F], ACT.Tanh, scale=0.5).then_inc(S["dtanh"], 1)

            def a_out(b):
                act.wait_ge(S["dactT_psum"], b + 1)
                nc.scalar.activation(actDT[:].rearrange("p j t -> p (j t)"), psQ[:, 0:F], ACT.Copy).then_inc(S["dactT_ready"], 1)

            x_out(0, 0)
            tanh_d(0, 0)
            x_out(1, 1)
            act.wait_ge(S["blkr_in"], 16)
            last_pair = act.value_load(nblk[0:1, 0:1], min_val=0, max_val=NB // 2 - 1)
            a_out(0)
            tanh_d(1, 1)
            x_out(2, 0)
            with act.Fori(1, NB // 2) as j:
                with act.If(j < last_pair + 1):
                    for s in range(2):
                        a_out(2 * j + s - 1)
                        x_out(2 * j + s + 1, 1 - s)
                        tanh_d(2 * j + s, s)
                    act.nop()
            a_out(last_pair * 2 + 1)

        @block.vector
        def _(dve):
            V = nc.vector
            V.memset(gwt[:], 0.0).then_inc(S["gate_w_zero"], 1)
            dve.sem_inc(S["mod_bank_free"], 2)
            dve.wait_ge(S["c_tanh"], 1)
            V.scalar_tensor_tensor(cp_h[:], cp_h[:], 1.0, cp_t[:], ALU.add, ALU.mult)
            V.scalar_tensor_tensor(cs_h[:], cs_h[:], 1.0, cs_t[:], ALU.add, ALU.mult)
            dve.drain()
            for t in range(TS):
                V.tensor_scalar(csil[:, :, 0:TAIL].rearrange("p k (b t) -> p k b t", t=TS)[:, :, :, t],
                                cs_h[:].rearrange("p b k -> p k b"), 0.5, None, ALU.mult)
            V.tensor_scalar(csil[:, :, TAIL], cp_h[:], 0.5, None, ALU.mult).then_inc(S["csil_ready"], 1)
            dve.wait_ge(S["prm_psum"], 1)
            V.tensor_copy(prm[:], psP[:, 0:RC * 40].rearrange("p (c n) -> p c n", n=40)).then_inc(S["prm_ready"], 1)
            dve.drain()
            V.tensor_copy(gb[:, 0:RC], prm[:, :, 5])
            V.tensor_copy(gb[:, RC:2 * RC], prm[:, :, 6])
            V.tensor_scalar(lam8[:, :, 0], prm[:, :, 7], -1.0, None, ALU.mult)
            dve.drain()
            V.tensor_tensor(lam8[:, :, 1], lam8[:, :, 0], prm[:, :, 7], ALU.max).then_inc(S["lam_exp"], 1)
            dve.wait_ge(S["norms_in"], 48)
            for n in range(NCH):
                dve.wait_ge(S["ada_psum_ready"], n + 1)
                if n >= 2:
                    dve.wait_ge(S2["mod_st"][n % 2], 16 * (n // 2))
                sect = n * 512 // D
                src = psT[0:TAIL + 1, (n % 2) * 512:(n % 2) * 512 + 512]
                if sect in (1, 4):
                    V.tensor_tensor(modc[:, n % 2], src, adab[:, n * 512:(n + 1) * 512], ALU.add)
                    dve.drain()
                    V.scalar_tensor_tensor(modc[:, n % 2], modc[:, n % 2], 1.0,
                                           gmix[:, sect // 4, (n % 2) * 512:(n % 2) * 512 + 512], ALU.add,
                                           ALU.mult).then_inc(S["mod_row_ready"], 1)
                else:
                    V.tensor_tensor(modc[:, n % 2], src, adab[:, n * 512:(n + 1) * 512], ALU.add).then_inc(S["mod_row_ready"], 1)
                dve.drain().then_inc(S["mod_bank_free"], 1)
            dve.wait_ge(S["lam_one"], 1)
            e, z, w, s_ = lam8[:, :, 1], hs_t[:, :, 0], hs_t[:, :, 1], hs_t[:, :, 2]
            V.tensor_scalar(z, e, 2.0, None, ALU.add)
            dve.drain()
            V.reciprocal(z, z)
            dve.drain()
            V.tensor_tensor(z, z, e, ALU.mult)
            dve.drain()
            V.tensor_tensor(w, z, z, ALU.mult)
            V.memset(s_, 1.0 / 17.0)
            for c in (15.0, 13.0, 11.0, 9.0, 7.0, 5.0, 3.0, 1.0):
                dve.drain()
                V.tensor_tensor(s_, s_, w, ALU.mult)
                dve.drain()
                V.tensor_scalar(s_, s_, 1.0 / c, None, ALU.add)
            dve.drain()
            V.scalar_tensor_tensor(s_, s_, 2.0, z, ALU.mult, ALU.mult)
            V.tensor_scalar(lam8[:, :, 0], lam8[:, :, 0], 0.0, None, ALU.max)
            dve.drain()
            V.tensor_tensor(s_, s_, lam8[:, :, 0], ALU.add)
            dve.drain()
            V.tensor_scalar(lam8[:, :, 0], s_, -0.5 * LRU_C, None, ALU.mult)
            V.memset(xrb[:, :, 0:HALO], 0.0)
            V.memset(hlast[:], 0.0)
            dve.drain()

            def h_of(i, par, n=P, first=False):
                dve.wait_ge(S["rstd_ready"], i + 1)
                if not first:
                    dve.wait_ge(S["hT_psum"], i)
                V.scalar_tensor_tensor(hrow[0:n], xin[0:n, par], rst[0:n, par:par + 1], modA[0:n, 1], ALU.mult, ALU.mult)
                dve.drain()
                V.tensor_tensor(hrow[0:n], hrow[0:n], modA[0:n, 0], ALU.add).then_inc(S["h_ready"], 1)

            def conv(i):
                dve.wait_ge(S["xr_ready"], i + 1)
                for c in range(RC):
                    V.tensor_scalar(u[:, c], xrb[:, c, 0:P], prm[:, c, 0:1], prm[:, c, 4:5], ALU.mult, ALU.add)
                for t in range(1, HALO + 1):
                    dve.drain()
                    for c in range(RC):
                        V.scalar_tensor_tensor(u[:, c], xrb[:, c, t:t + P], prm[:, c, t:t + 1], u[:, c], ALU.mult, ALU.add)
                dve.drain()
                V.tensor_copy(xrb[:, :, 0:HALO], xrb[:, :, P:P + HALO])
                dve.drain().then_inc(S["conv_ready"], 1)

            def conv_tail(i):
                def view(ap, t0, n):
                    return ap[:, 0:NS * (TS + HALO)].rearrange("p (b t) -> p b t", b=NS)[:, :, t0:t0 + n]
                dve.wait_ge(S["xr_ready"], i + 1)
                uv = [u[:, c, 0:TAIL].rearrange("p (b t) -> p b t", b=NS) for c in range(RC)]
                for c in range(RC):
                    V.tensor_copy(view(xrb[:, c], 0, HALO), prm[:, c, 8:8 + NS * HALO].rearrange("p (b j) -> p b j", b=NS))
                dve.drain()
                for c in range(RC):
                    V.tensor_scalar(uv[c], view(xrb[:, c], 0, TS), prm[:, c, 0:1], prm[:, c, 4:5], ALU.mult, ALU.add)
                for t in range(1, HALO + 1):
                    dve.drain()
                    for c in range(RC):
                        V.scalar_tensor_tensor(uv[c], view(xrb[:, c], t, TS), prm[:, c, t:t + 1], uv[c], ALU.mult, ALU.add)
                for c in range(RC):
                    V.tensor_copy(stt[:, c, HALO + 1:HALO + 1 + NS * HALO].rearrange("p (b j) -> p b j", b=NS), view(xrb[:, c], TS, HALO))
                dve.drain().then_inc(S["conv_ready"], 1)

            def scores(n, h, first=False):
                dve.wait_ge(S["s_psum"], 2 * n + h + 1)
                hs = slice(GQ * h, GQ * h + GQ)
                s_in = psS[:].rearrange("p (g j) -> p g j", g=GQ)
                if first:
                    V.memset(sc[:, h, :, 0:P], NEG)
                    V.scalar_tensor_tensor(sc[:, h, :, P:], s_in[:, :, P:], HD ** -0.5, bias[:, hs, P:], ALU.mult, ALU.add)
                else:
                    V.scalar_tensor_tensor(sc[:, h], s_in, HD ** -0.5, bias[:, hs], ALU.mult, ALU.add)
                dve.drain().then_inc(S["s_read"], 1)
                V.tensor_reduce(mx[:, h, 0], sc[:, h], AX.X, ALU.max)
                dve.drain()
                V.tensor_tensor(mx[:, h, 0], mx[:, h, 0], sink[:, hs], ALU.max)
                dve.drain()
                V.tensor_scalar(mx[:, h, 1], mx[:, h, 0], -1.0, None, ALU.mult)
                V.tensor_tensor(mx[:, h, 2], sink[:, hs], mx[:, h, 0], ALU.subtract)
                dve.drain().then_inc(S["m_ready"], 1)

            def o_out(n, h):
                dve.wait_ge(S["o_psum"], 2 * n + h + 1)
                V.tensor_tensor(mx[:, h, 3], esum[:, h, 0], esum[:, h, 1], ALU.add)
                dve.drain()
                V.reciprocal(mx[:, h, 3], mx[:, h, 3])
                dve.drain()
                V.tensor_tensor(orow[:, 256 * h:256 * h + 256].rearrange("p (g d) -> p g d", g=GQ),
                                psQ[:, 768:1024].rearrange("p (g d) -> p g d", g=GQ), bc(mx[:, h, 3], HD),
                                ALU.mult).then_inc(S["o_ready"], 1)

            def step(i, par, proj=True, att=True, nxt=True, first=False, n=P, n_next=P):
                a = i - 1
                tail = n != P
                if proj:
                    (conv_tail if tail else conv)(i)
                if att:
                    if not first:
                        dve.wait_ge(S["o_psum"], 2 * a)
                    V.tensor_copy(vb[:, 1 - par], qkv[:, QD + KVD:]).then_inc(S["v_ready"], 1)
                    scores(a, 0, first)
                if nxt:
                    if n_next != P:
                        dve.wait_ge(S["tailmod_in"], 16)
                    h_of(i + 1, 1 - par, n_next)
                if proj:
                    dve.wait_ge(S["gates_psum"], i + 1)
                    V.tensor_tensor(gts[:, :, 0:n], psP[:].rearrange("p (c t) -> p c t", t=P)[:, :, 0:n], bc(gb[:], n),
                                    ALU.add).then_inc(S["gates_sum"], 1)
                    dve.wait_ge(S["y_ready"], i + 1)
                    V.tensor_scalar(sq_t[:, :, 0:n], sq_t[:, :, 0:n], GELU_A, 1.0, ALU.mult, ALU.add)
                    dve.drain()
                    V.tensor_tensor(sq_t[:, :, 0:n], sq_t[:, :, 0:n], y_t[:, :, 0:n], ALU.mult).then_inc(S["gelu_in"], 1)
                    dve.wait_ge(S["gates_tanh"], i + 1)
                    V.scalar_tensor_tensor(b_t[:, :, 0:n], gts[:, 0:RC, 0:n], 1.0, bc(lam8[:, :, 0], n), ALU.add,
                                           ALU.mult).then_inc(S["loga_ready"], 1)
                    V.scalar_tensor_tensor(gts[:, RC:, 0:n], gts[:, RC:, 0:n], 1.0, u[:, :, 0:n], ALU.add, ALU.mult)
                if att:
                    scores(a, 1, first)
                    o_out(a, 0)
                if proj:
                    dve.wait_ge(S["a_ready"], i + 1)
                    V.tensor_scalar(b_t[:, :, 0:n], th_t[:, :, 0:n], -1.0, 1.0, ALU.mult, ALU.add)
                    dve.drain()
                    V.reciprocal(b_t[:, :, 0:n], b_t[:, :, 0:n])
                    dve.drain()
                    V.scalar_tensor_tensor(b_t[:, :, 0:n], th_t[:, :, 0:n], -2.0, b_t[:, :, 0:n], ALU.mult,
                                           ALU.mult).then_inc(S["b2_ready"], 1)
                    dve.wait_ge(S["gelu_tanh"], i + 1)
                    V.scalar_tensor_tensor(sq_t[:, :, 0:n], sq_t[:, :, 0:n], 1.0, y_t[:, :, 0:n], ALU.add, ALU.mult)
                    dve.wait_ge(S["bsqrt_ready"], i + 1)
                    V.scalar_tensor_tensor(b_t[:, :, 0:n], gts[:, RC:, 0:n], 0.5, b_t[:, :, 0:n], ALU.mult, ALU.mult)
                    dve.drain()
                    if tail:
                        at_, bt_, ht_ = (x[:, :, 0:TAIL].rearrange("p c (b t) -> p c b t", b=NS) for x in (a_t, b_t, hs_t))
                        for t in range(TS):
                            prev = prm[:, :, 8 + NS * HALO:8 + NS * HALO + NS] if t == 0 else ht_[:, :, :, t - 1]
                            V.tensor_tensor(ht_[:, :, :, t], at_[:, :, :, t], prev, ALU.mult)
                            dve.drain()
                            V.tensor_tensor(ht_[:, :, :, t], ht_[:, :, :, t], bt_[:, :, :, t], ALU.add)
                            dve.drain()
                        V.tensor_copy(stt[:, :, HALO + 1 + NS * HALO:], ht_[:, :, :, TS - 1])
                    else:
                        for c in range(RC):
                            V.tensor_tensor_scan(hs_t[:, c], a_t[:, c], b_t[:, c], hlast[:, c], ALU.mult, ALU.add)
                        dve.drain()
                        V.tensor_copy(hlast[:], hs_t[:, :, P - 1:P])
                    if att:
                        dve.wait_ge(S2["outr_st"][0], 16 * i)
                    V.scalar_tensor_tensor(outr[:, :, 0:n], sq_t[:, :, 0:n], 0.5, hs_t[:, :, 0:n], ALU.mult, ALU.mult)
                    dve.drain().then_inc(S["outr_ready"], 1)
                if att:
                    o_out(a, 1)
                if proj:
                    dve.wait_ge(S["qkv_ready"], i + 1)
                    if att:
                        dve.wait_ge(S["qkT_psum"], i)
                    if tail:
                        dve.wait_ge(S["kwin_st"], 32)
                    q3 = qkv[0:n, 0:QD + KVD].rearrange("p (h d) -> p h d", d=HD)
                    n3 = qn[0:n].rearrange("p (h d) -> p h d", d=HD)
                    V.scalar_tensor_tensor(qn[0:n], qkv[0:n, 0:QD + KVD], 1.0 / HD, qkv[0:n, 0:QD + KVD], ALU.mult, ALU.mult)
                    dve.drain()
                    V.tensor_reduce(ss10[0:n, 0:NH + NKV], n3, AX.X, ALU.add).then_inc(S["ss10_ready"], 1)
                    dve.wait_ge(S["r10_ready"], i + 1)
                    V.tensor_tensor(q3, q3, bc(r10[0:n, 0:NH + NKV], HD), ALU.mult)
                    dve.drain()
                    for v in range(NKV):
                        V.tensor_tensor(qn[0:n, 0:QD].rearrange("p (g v d) -> p v g d", v=NKV, g=GQ)[:, v],
                                        qkv[0:n, v * GQ * HD:(v + 1) * GQ * HD].rearrange("p (g d) -> p g d", g=GQ),
                                        qw[0:n, v * GQ * HD:(v + 1) * GQ * HD].rearrange("p (g d) -> p g d", g=GQ), ALU.mult)
                    V.tensor_tensor(qn[0:n, QD:], qkv[0:n, QD:QD + KVD], qw[0:n, QD:], ALU.mult).then_inc(S["qn_ready"], 1)

            dve.wait_ge(S["modA_in"], 16)
            dve.wait_ge(S["sink_in"], 16)
            dve.wait_ge(S["bias_ready"], 1)
            dve.wait_ge(S["qw_in"], 16 * (NH + NKV))
            h_of(0, 0, first=True)
            step(0, 0, att=False)
            step(1, 1, first=True)
            with dve.Fori(1, NT // 2 - 1) as j:
                for s in range(2):
                    step(2 * j + s, s)
            step(NT - 2, 0)
            step(NT - 1, 1, n_next=TAIL)
            V.tensor_copy(stt[:, :, 0:HALO], xrb[:, :, 0:HALO])
            V.tensor_copy(stt[:, :, HALO:HALO + 1], hlast[:])
            dve.drain()
            step(NT, 0, nxt=False, n=TAIL)
            dve.wait_ge(S["qkT_psum"], NT + 1)
            dve.wait_ge(S["o_psum"], 2 * NT)
            V.memset(qT[:, 0:4], 0.0)
            V.memset(kT[:, 1], 0.0)
            V.memset(vb[:, 1], 0.0).then_inc(S["smp_v0"], 1)
            dve.wait_ge(S["small_psum"], 1)
            dve.drain()
            V.tensor_copy(stt_r[:], psP[0:36, 512:1024]).then_inc(S["small_ready"], 1)
            dve.wait_ge(S["qkT_ready"], NT + 1)
            with dve.Fori(0, NS) as b:
                dve.wait_ge(S["s_psum"], 2 * (b + SMP))
                V.tensor_copy(qT[:, 0:4, 0:TS], qkTt[:, 0:4, bass.ds(b * TS, TS)])
                V.tensor_copy(kT[:, 1, 0:TS], qkTt[:, 4, bass.ds(b * TS, TS)]).then_inc(S["smp_q"], 1)
                for h in range(2):
                    scores(b + SMP, h)
                for h in range(2):
                    o_out(b + SMP, h)

            dve.wait_ge(S["modB_in"], 32)
            dve.wait_ge(S["rbias_in"], 16)
            V.memset(yzero[:], 0.0).then_inc(S["yzero_ready"], 1)
            V.memset(mrun[:], 0.0)
            V.memset(msk_all[:, NT], 0.0)
            V.memset(idx_all[:], 0.0)
            dve.drain().then_inc(S["mrun_ready"], 1)
            dve.wait_ge(S["iota_ready"], 1)

            def x2_of(i, par, half, n=P, first=False):
                dve.wait_ge(S["mixed_psum"], i + 1)
                dve.wait_ge(S2["xB_in"][par], 16 * half + 16)
                V.tensor_tensor(x2[0:n, par], psQ[0:n], modB[0:n, 0], ALU.mult)
                dve.drain()
                V.tensor_tensor(x2[0:n, par], x2[0:n, par], xb[0:n, par], ALU.add)
                dve.drain().then_inc(S["x2_ready"], 1)

            def h2_of(i, par, n=P, first=False):
                dve.wait_ge(S["rstdB_ready"], i + 1)
                if not first:
                    dve.wait_ge(S["h2_st"], 16 * i)
                    dve.wait_ge(S["h2T_psum"], i)
                V.scalar_tensor_tensor(h2[0:n], x2[0:n, par], ssqB[0:n, 1:2], modB[0:n, 2], ALU.mult, ALU.mult)
                dve.drain()
                V.tensor_tensor(h2[0:n], h2[0:n], modB[0:n, 1], ALU.add).then_inc(S["h2_ready"], 1)

            def shared_act(i, n=P):
                dve.wait_ge(S["shtanh"], i + 1)
                V.scalar_tensor_tensor(sg[0:n, 1], sg[0:n, 0], 1.0, psP[0:n, 0:F], ALU.add, ALU.mult)
                dve.drain()
                V.scalar_tensor_tensor(actr[0:n], sg[0:n, 1], 0.5, psP[0:n, F:2 * F], ALU.mult, ALU.mult).then_inc(S["act_ready"], 1)

            def xs_of(i, par, n=P, first=False):
                dve.wait_ge(S["shd_psum"], i + 1)
                V.tensor_tensor(tmpB[0:n], psS[0:n], modG[0:n], ALU.mult)
                dve.drain()
                if not first:
                    dve.wait_ge(S2["xs_st"][0], 16 * i)
                V.tensor_tensor(xso[0:n], tmpB[0:n], x2[0:n, par], ALU.add).then_inc(S["xs_ready"], 1)
                dve.drain()

            def route(t, n=P):
                dve.wait_ge(S["rtanh"], t + 1)
                V.tensor_scalar(rt_s[0:n], rt_s[0:n], 0.5, 0.5, ALU.mult, ALU.add)
                dve.drain()
                V.tensor_tensor(rt_b[0:n], rt_s[0:n], rbias[0:n], ALU.add)
                dve.drain()
                for g in range(NG):
                    V.max(rt_8[0:n, g], rt_b[0:n, g * GE:(g + 1) * GE])
                dve.drain()
                V.tensor_tensor(rt_g[0:n, 0], rt_8[0:n, :, 0], rt_8[0:n, :, 1], ALU.add)
                dve.drain()
                V.max(rt_g[0:n, 1], rt_g[0:n, 0])
                dve.drain()
                V.max_index(rt_u[0:n, 0], rt_g[0:n, 1], rt_g[0:n, 0])
                dve.drain()
                V.tensor_copy(rt_g[0:n, 2], rt_u[0:n, 0])
                dve.drain()
                g4 = rt_t[0:n, 0, 0:NG * TG].rearrange("p (g k) -> p g k", g=NG)
                V.tensor_tensor(g4, bc(iota[0:n, 0:NG], TG), rt_g[0:n, 2, 0:TG].unsqueeze(1).to_broadcast([n, NG, TG]), ALU.is_equal)
                dve.drain()
                V.tensor_reduce(rt_g[0:n, 3], g4, AX.X, ALU.add)
                dve.drain()
                V.tensor_scalar(rt_g[0:n, 0], rt_g[0:n, 3], -1.0, -NEG, ALU.add, ALU.mult)
                b3 = rt_b[0:n].rearrange("p (g e) -> p g e", g=NG)
                m3 = rt_m[0:n].rearrange("p (g e) -> p g e", g=NG)
                V.tensor_tensor(m3, b3, bc(rt_g[0:n, 3], GE), ALU.mult)
                dve.drain()
                V.tensor_tensor(m3, m3, bc(rt_g[0:n, 0], GE), ALU.add)
                dve.drain()
                V.max(rt_8[0:n, 0], rt_m[0:n])
                dve.drain()
                V.max_index(rt_u[0:n, 1], rt_8[0:n, 0], rt_m[0:n])
                dve.drain()
                V.tensor_copy(idx_all[0:n, t], rt_u[0:n, 1])
                dve.drain()
                V.tensor_tensor(rt_oh[0:n], iota[0:n].unsqueeze(1).to_broadcast([n, TOPK, NE]), bc(idx_all[0:n, t, 0:TOPK], NE), ALU.is_equal)
                dve.drain()
                V.tensor_tensor(rt_t[0:n], rt_oh[0:n], rt_s[0:n].unsqueeze(1).to_broadcast([n, TOPK, NE]), ALU.mult)
                V.tensor_reduce(msk_all[0:n, t], rt_oh[0:n].rearrange("p k e -> p e k"), AX.X, ALU.add).then_inc(S["msk_ready"], 1)
                dve.drain()
                V.tensor_reduce(wgt_all[0:n, t, 0:TOPK], rt_t[0:n], AX.X, ALU.add)
                dve.drain()
                V.tensor_reduce(rt_g[0:n, 1, 0:1], wgt_all[0:n, t, 0:TOPK], AX.X, ALU.add)
                dve.drain()
                V.reciprocal(rt_g[0:n, 1, 1:2], rt_g[0:n, 1, 0:1])
                dve.drain()
                V.tensor_scalar(wgt_all[0:n, t, 0:TOPK], wgt_all[0:n, t, 0:TOPK], rt_g[0:n, 1, 1:2], ROUTE_SCALE, ALU.mult, ALU.mult)
                dve.drain()

            def add_mask(t):
                dve.wait_ge(S["pos_psum"], t + 1)
                V.tensor_tensor(mrun[:], mrun[:], msk_all[:, t], ALU.add)
                dve.drain().then_inc(S["mrun_ready"], 1)

            def step_b(i, par, half, d0=True, d1=True, d2=True, n0=P, n1=P, n2=P, first2=False, last0=False):
                if d2:
                    add_mask(i - 2)
                    xs_of(i - 2, par, n2, first2)
                if d0:
                    x2_of(i, par, half, n0)
                if d1:
                    shared_act(i - 1, n1)
                if d0:
                    h2_of(i, par, n0, first=isinstance(i, int) and i == 0)
                if d1:
                    route(i - 1, n1)

            step_b(0, 0, 0, d1=False, d2=False)
            step_b(1, 1, 0, d2=False)
            step_b(2, 0, 1, first2=True)
            step_b(3, 1, 1)
            with dve.Fori(2, NT // 2) as j:
                for s in range(2):
                    step_b(2 * j + s, s, j)
            dve.wait_ge(S["tailmodB_in"], 16)
            step_b(NT, 0, NT // 2, n0=TAIL)
            step_b(NT + 1, 1, 0, d0=False, n1=TAIL)
            dve.wait_ge(S["tailmodB_in"], 32)
            step_b(NT + 2, 0, 0, d0=False, d1=False, n2=TAIL)

            dve.wait_ge(S["cnt_psum"], 1)
            V.tensor_scalar(cnt[:, 0], psP[:, 0:NE], float(P - 1), None, ALU.add)
            dve.drain()
            V.tensor_copy(cnti[:, 0], cnt[:, 0])
            dve.drain()
            V.tensor_scalar(cnti[:, 1], cnti[:, 0], 7, None, ALU.arith_shift_right)
            dve.drain()
            V.tensor_copy(cnt[:, 1], cnti[:, 1])
            dve.drain()
            V.tensor_tensor_scan(cnt[:, 2], ones[:, 0:NE], cnt[:, 1], 0.0, ALU.mult, ALU.add)
            dve.drain()
            V.tensor_tensor(cnt[:, 3], cnt[:, 2], cnt[:, 1], ALU.subtract)
            dve.wait_ge(S["iotp_ready"], 1)
            for h in range(2):
                V.tensor_scalar(blkf[:, h], cnt[:, 2], iotp[:, h:h + 1], None, ALU.is_le)
            dve.drain()
            V.tensor_scalar(cnt[:, 4], cnt[:, 3], float(P), None, ALU.mult)
            V.tensor_reduce(cnt[:, 5, 0:2], blkf[:], AX.X, ALU.add)
            dve.drain()
            V.tensor_scalar(cnt[:, 5, 0:2], cnt[:, 5, 0:2], float(NE - 1), None, ALU.min)
            V.tensor_tensor(pos_all[:], pos_all[:], cnt[:, 4].unsqueeze(1).to_broadcast([P, ALL, NE]), ALU.add)
            V.tensor_scalar(cnt[0:1, 5, 2:3], cnt[0:1, 2, NE - 1:NE], -1.0, None, ALU.add)
            dve.drain()
            V.tensor_copy(nblk[0:1, 1:2], cnt[0:1, 5, 2:3])
            dve.drain()
            V.tensor_scalar(nblk[0:1, 0:1], nblk[0:1, 1:2], 1, None, ALU.arith_shift_right)
            dve.drain()
            V.tensor_copy(blki[:], cnt[:, 5, 0:2]).then_inc(S["blk_ready"], 1)
            with dve.Fori(0, ALL) as t:
                V.tensor_tensor(ohC[:], iota[:].unsqueeze(1).to_broadcast([P, TOPK, NE]), bc(idx_all[:, t, 0:TOPK], NE), ALU.is_equal)
                dve.drain()
                V.tensor_tensor(ohC[:], ohC[:], pos_all[:, t].unsqueeze(1).to_broadcast([P, TOPK, NE]), ALU.mult)
                dve.drain()
                V.tensor_reduce(slotf[:, t, 0:TOPK], ohC[:], AX.X, ALU.add)
                dve.drain()
            V.memset(slotf[:, :, TOPK:], 0.0)
            dve.drain()
            V.tensor_copy(slot_i[:], slotf[:])
            dve.drain()
            V.tensor_scalar(dsti[:], slot_i[:], 7, None, ALU.arith_shift_right)
            V.tensor_scalar(dlow[:], slot_i[:], P - 1, None, ALU.bitwise_and)
            dve.drain()
            V.tensor_copy(slotf[:], dlow[:])
            V.tensor_copy(slotg[:], dsti[:])
            dve.drain()
            V.scalar_tensor_tensor(slotf[:], slotf[:], float(NBT), slotg[:], ALU.mult, ALU.add)
            dve.drain()
            V.tensor_copy(dsti[:], slotf[:]).then_inc(S["dst_ready"], 1)

            def act_d(b, s, free=True):
                dve.wait_ge(S["dtanh"], b + 1)
                if free:
                    dve.wait_ge(S["dactT_psum"], b)
                V.scalar_tensor_tensor(sgD[:, s], sgD[:, s], 1.0, psP[:, s * 512:s * 512 + F], ALU.add, ALU.mult)
                dve.drain()
                V.scalar_tensor_tensor(actD[:], sgD[:, s], 0.5, psP[:, s * 512 + F:s * 512 + 2 * F], ALU.mult, ALU.mult).then_inc(S["dact_ready"], 1)

            def y_out(b, s, stored=None):
                dve.wait_ge(S["down_psum"], b + 1)
                if stored is not None:
                    dve.wait_ge(S2["y_st"][s], stored)
                V.tensor_copy(ysb[:, s], psS[:]).then_inc(S["ysb_ready"], 1)

            act_d(0, 0, free=False)
            act_d(1, 1)
            y_out(0, 0)
            dve.wait_ge(S["blkr_in"], 16)
            last_pair = dve.value_load(nblk[0:1, 0:1], min_val=0, max_val=NB // 2 - 1)
            with dve.If(last_pair > 0):
                act_d(2, 0)
                y_out(1, 1)
                act_d(3, 1)
                y_out(2, 0, 16)
            with dve.Fori(2, NB // 2) as j:
                with dve.If(j < last_pair + 1):
                    act_d(2 * j, 0)
                    y_out(2 * j - 1, 1, 16 * (j - 1))
                    act_d(2 * j + 1, 1)
                    y_out(2 * j, 0, 16 * j)
            y_out(last_pair * 2 + 1, 1, last_pair * 16)

            def rows_e(t, h, half, n=P):
                dve.wait_ge(S2["yrow_in"][h], 48 * t + 48)
                for k in range(TOPK // 2):
                    w = wgt_all[0:n, t, h * 3 + k:h * 3 + k + 1]
                    if h == 0 and k == 0:
                        V.tensor_scalar(acc[0:n, half], yg[0:n, h, k], w, None, ALU.mult)
                    else:
                        V.scalar_tensor_tensor(acc[0:n, half], yg[0:n, h, k], w, acc[0:n, half], ALU.mult, ALU.add)
                    dve.drain()
                dve.sem_inc(S["rows_used"], 1)

            def out_e(t, s, j, n=P, first=False):
                if not first:
                    dve.wait_ge(S2["out_st"][s], 16 * j)
                rows_e(t, 0, s, n)
                rows_e(t, 1, s, n)
                V.tensor_tensor(acc[0:n, s], acc[0:n, s], g2b[0:n], ALU.mult)
                dve.drain()
                dve.wait_ge(S2["xe_in"][s], 16 * j + 16)
                V.tensor_tensor(acc[0:n, s], acc[0:n, s], xe[0:n, s], ALU.add).then_inc(S["acc_ready"], 1)

            dve.wait_ge(S["g2_in"], 16)
            for s in range(2):
                out_e(s, s, 0, first=True)
            with dve.Fori(1, NT // 2) as j:
                for s in range(2):
                    out_e(2 * j + s, s, j)
            dve.wait_ge(S["g2_in"], 32)
            out_e(NT, 0, NT // 2, n=TAIL)

        @block.tensor
        def _(pe):
            T = nc.tensor
            pe.wait_ge(S["const_ready"], 1)
            pe.wait_ge(S["csil_ready"], 1)
            pe.wait_ge(S["prm_in"], 16 * 7)
            for c in range(RC):
                last = T.transpose(psP[:, c * 40:(c + 1) * 40], prm_r[:, c * P:(c + 1) * P], ident[0:40, 0:40])
            last.then_inc(S["prm_psum"], 1)
            with pe.Fori(0, NCH // 2) as j:
                for s in range(2):
                    pe.wait_ge(S2["ada_in"][s], 16 * j + 16)
                    pe.wait_ge(S["mod_bank_free"], 2 * j + s + 1)
                    for k in range(KC):
                        last = T.matmul(psT[0:TAIL + 1, s * 512:s * 512 + 512], csil[:, k], ada_wt[:, s, k], start=k == 0, stop=k == KC - 1)
                    last.then_inc(S["ada_psum_ready"], 1)
            pe.wait_ge(S["gate_w_in"], 64)

            def h_transpose(i, n=P, first=False):
                pe.wait_ge(S["h_ready"], i + 1)
                if not first:
                    pe.wait_ge(S["hT_ready"], i)
                hv = hrow[0:n].rearrange("p (m k) -> p k m", k=KC)
                for k in range(KC):
                    last = T.transpose(psT[:, k * P:k * P + n], hv[:, k], ident[0:n, 0:n])
                last.then_inc(S["hT_psum"], 1)

            def branch(i, bank, col, n, done, chunks=range(RC)):
                for c in chunks:
                    for k in range(KC):
                        last = T.matmul(psP[:, bank * 512 + c * P:bank * 512 + c * P + n], win[:, k, col + c * P:col + (c + 1) * P],
                                        hT[:, k, 0:n], start=k == 0, stop=k == KC - 1)
                if done is not None:
                    last.then_inc(done, 1)

            def qkv_part(i, c0, c1, n, done):
                for k in range(KC):
                    last = T.matmul(psQ[0:n, c0:c1], hT[:, k, 0:n], win[:, k, 2 * R + c0:2 * R + c1], start=k == 0, stop=k == KC - 1)
                last.then_inc(done, 1)

            def qk_transpose(a, n=P):
                pe.wait_ge(S["qn_ready"], a + 1)
                for g in range(GQ):
                    T.transpose(psT[:, g * P:g * P + n], qn[0:n, g * P:(g + 1) * P], ident[0:n, 0:n])
                T.transpose(psT[:, 4 * P:4 * P + n], qn[0:n, QD:], ident[0:n, 0:n]).then_inc(S["qkT_psum"], 1)

            def qk(n, h, cur, first=False):
                rows = slice(HD * h, HD * h + HD)
                for g in range(GQ):
                    for where, slot in ((0, 1 - cur), (1, cur)):
                        if first and where == 0:
                            continue
                        last = T.matmul(psS[:, g * 256 + where * P:g * 256 + where * P + P], qT[rows, g], kT[rows, slot], start=True, stop=True)
                last.then_inc(S["s_psum"], 1)

            def p_transpose(n, h):
                pe.wait_ge(S["p_ready"], 2 * n + h + 1)
                for g in range(GQ):
                    for b in range(2):
                        last = T.transpose(psT[:, (2 * g + b) * P:(2 * g + b + 1) * P], sc[:, h, g, b * P:(b + 1) * P], ident[:])
                last.then_inc(S["pT_psum"], 1)

            def pv(n, h, cur, first=False):
                pe.wait_ge(S["pT_ready"], 2 * n + h + 1)
                for g in range(GQ):
                    for b, slot in ((0, 1 - cur), (1, cur)):
                        if first and b == 0:
                            continue
                        last = T.matmul(psQ[:, 768 + g * HD:768 + (g + 1) * HD], PT[:, g, b], vb[:, slot, HD * h:HD * h + HD],
                                        start=b == 0 or first, stop=b == 1)
                last.then_inc(S["o_psum"], 1)

            def o_transpose(n):
                pe.wait_ge(S["o_ready"], 2 * n + 2)
                for c in range(RC):
                    last = T.transpose(psS[:, c * P:(c + 1) * P], orow[:, c * P:(c + 1) * P], ident[:])
                last.then_inc(S["oT_psum"], 1)

            def step(i, par, proj=True, att=True, nxt=True, first=False, n=P, n_next=P):
                a, cur = i - 1, 1 - par
                if proj:
                    pe.wait_ge(S["hT_ready"], i + 1)
                    if att:
                        pe.wait_ge(S["gates_sum"], i)
                    branch(i, 0, 0, n, S["xr_psum"])
                if att:
                    qk_transpose(a)
                if proj:
                    branch(i, 1, R, n, None, range(0, 2))
                if att:
                    pe.wait_ge(S["qkT_ready"], a + 1)
                    if not first:
                        pe.wait_ge(S["oT_ready"], a)
                    qk(a, 0, cur, first)
                if proj:
                    branch(i, 1, R, n, S["yr_psum"], range(2, 4))
                    pe.wait_ge(S["conv_ready"], i + 1)
                    pe.wait_ge(S["xr_ready"], i + 1)
                    pe.wait_ge(S["y_ready"], i + 1)
                    for g in range(2):
                        for c in range(RC):
                            last = T.matmul(psP[:, (g * RC + c) * P:(g * RC + c) * P + n], gwt[:, g, c], u[:, c, 0:n], start=True, stop=True)
                    last.then_inc(S["gates_psum"], 1)
                if att:
                    p_transpose(a, 0)
                    pe.wait_ge(S["s_read"], 2 * a + 1)
                    qk(a, 1, cur, first)
                    pe.wait_ge(S["v_ready"], a + 1)
                    if not first:
                        pe.wait_ge(S["o_ready"], 2 * a)
                    pv(a, 0, cur, first)
                if proj:
                    if att:
                        pe.wait_ge(S["qkv_ready"], i)
                    qkv_part(i, 0, 512, n, S["qkv1_psum"])
                if att:
                    pe.wait_ge(S["pT_ready"], 2 * a + 1)
                    p_transpose(a, 1)
                if proj:
                    if att:
                        pe.wait_ge(S["o_ready"], 2 * a + 1)
                    qkv_part(i, 512, QKV, n, S["qkv2_psum"])
                if nxt:
                    if att:
                        pe.wait_ge(S["pT_ready"], 2 * a + 2)
                    h_transpose(i + 1, n_next)
                if att:
                    pe.wait_ge(S["o_ready"], 2 * a + 1)
                    if proj:
                        pe.wait_ge(S["qkv_ready"], i + 1)
                    pv(a, 1, cur, first)
                    o_transpose(a)

            pe.wait_ge(S["prm_ready"], 1)
            pe.wait_ge(S["mod_row_ready"], NCH)
            h_transpose(0, first=True)
            pe.wait_ge(S["win_in"], 16)
            step(0, 0, att=False)
            step(1, 1, first=True)
            with pe.Fori(1, NT // 2 - 1) as j:
                for s in range(2):
                    step(2 * j + s, s)
            step(NT - 2, 0)
            step(NT - 1, 1, n_next=TAIL)
            step(NT, 0, nxt=False, n=TAIL)
            qk_transpose(NT, TAIL)
            pe.wait_ge(S["outr_ready"], NT + 1)
            for c in range(RC):
                last = T.transpose(psP[0:36, 512 + c * P:512 + (c + 1) * P], stt[:, c], ident[:])
            last.then_inc(S["small_psum"], 1)
            with pe.Fori(0, NS) as b:
                pe.wait_ge(S["smp_ck"], 16 * b + 16)
                T.transpose(psP[:, 0:P], ck[:], ident[:]).then_inc(S["ckT_psum"], 1)
                pe.wait_ge(S["ckT_ready"], b + 1)
                pe.wait_ge(S["smp_q"], b + 1)
                pe.wait_ge(S["oT_ready"], b + SMP)
                qk(b + SMP, 0, 1)
                p_transpose(b + SMP, 0)
                pe.wait_ge(S["s_read"], 2 * (b + SMP) + 1)
                qk(b + SMP, 1, 1)
                pe.wait_ge(S["smp_v"], 32 * b + 32)
                pe.wait_ge(S["o_ready"], 2 * (b + SMP))
                pv(b + SMP, 0, 1)
                pe.wait_ge(S["pT_ready"], 2 * (b + SMP) + 1)
                p_transpose(b + SMP, 1)
                pe.wait_ge(S["o_ready"], 2 * (b + SMP) + 1)
                pv(b + SMP, 1, 1)
                o_transpose(b + SMP)

            def mixed(i, par, h, half, n, first=False):
                if h == 0:
                    pe.wait_ge(S2["mix_in"][par], 16 * half + 16)
                    if not first:
                        pe.wait_ge(S["x2_ready"], i)
                for c in range(2 * RC):
                    last = T.matmul(psQ[0:n, h * 512:h * 512 + 512], mixb[:, par, c, 0:n], wout[:, c, h * 512:h * 512 + 512],
                                    start=c == 0, stop=c == 2 * RC - 1)
                if h == 1:
                    last.then_inc(S["mixed_psum"], 1)

            def step_b(i, par, half, d0=True, d1=True, d2=True, n0=P, n1=P, n2=P, first0=False, first1=False):
                if d0:
                    mixed(i, par, 0, half, n0, first0)
                if d2:
                    pe.wait_ge(S["act_ready"], i - 1)
                    pe.wait_ge(S["rtanh"], i - 1)
                    av = actr[0:n2].rearrange("p (m j) -> p j m", j=2)
                    for jj in range(2):
                        T.transpose(psP[:, 768 + jj * P:768 + jj * P + n2], av[:, jj], ident[0:n2, 0:n2])
                    pe.wait_ge(S["msk_ready"], i - 1)
                    pe.wait_ge(S["mrun_ready"], i - 1)
                    T.matmul(psP[:, 640:640 + NE], tri[:], msk_all[:, i - 2], start=True, stop=False)
                    T.matmul(psP[:, 640:640 + NE], ones[:], mrun[:], start=False, stop=True).then_inc(S["pos_psum"], 1)
                if d1:
                    pe.wait_ge(S["h2_ready"], i)
                    if not first1:
                        pe.wait_ge(S["h2T_ready"], i - 1)
                    hv = h2[0:n1].rearrange("p (m k) -> p k m", k=KC)
                    for k in range(KC):
                        last = T.transpose(psT[:, k * P:k * P + n1], hv[:, k], ident[0:n1, 0:n1])
                    last.then_inc(S["h2T_psum"], 1)
                if d0:
                    mixed(i, par, 1, half, n0)
                if d2:
                    pe.wait_ge(S["actT_ready"], i - 1)
                    if not (isinstance(i, int) and i == 2):
                        pe.wait_ge(S["xs_ready"], i - 2)
                    for h in range(2):
                        for jj in range(2):
                            last = T.matmul(psS[0:n2, h * 512:h * 512 + 512], actT[:, jj, 0:n2], shd[:, jj, h * 512:h * 512 + 512],
                                            start=jj == 0, stop=jj == 1)
                    last.then_inc(S["shd_psum"], 1)
                if d1:
                    pe.wait_ge(S["h2T_ready"], i)
                    if not first1:
                        pe.wait_ge(S["act_ready"], i - 1)
                    for k in range(KC):
                        last = T.matmul(psP[0:n1, 512:512 + NE], h2T[:, k, 0:n1], rw[:, k], start=k == 0, stop=k == KC - 1)
                    last.then_inc(S["router_psum"], 1)
                    for k in range(KC):
                        last = T.matmul(psP[0:n1, 0:2 * F], h2T[:, k, 0:n1], shgu[:, k], start=k == 0, stop=k == KC - 1)
                    last.then_inc(S["shup_psum"], 1)

            pe.wait_ge(S["wB_in"], 16 * 5)
            step_b(0, 0, 0, d1=False, d2=False, first0=True)
            step_b(1, 1, 0, d2=False, first1=True)
            step_b(2, 0, 1)
            step_b(3, 1, 1)
            with pe.Fori(2, NT // 2) as j:
                for s in range(2):
                    step_b(2 * j + s, s, j)
            step_b(NT, 0, NT // 2, n0=TAIL)
            step_b(NT + 1, 1, 0, d0=False, n1=TAIL)
            step_b(NT + 2, 0, 0, d0=False, d1=False, n2=TAIL)
            pe.wait_ge(S["mrun_ready"], ALL + 1)
            pe.wait_ge(S["act_ready"], ALL)
            T.matmul(psP[:, 0:NE], ones[:], mrun[:], start=True, stop=True).then_inc(S["cnt_psum"], 1)

            def x_tr(b, s, pairs):
                pe.wait_ge(S2["gather_in"][s], pairs)
                xv = xg[:, s].rearrange("p (m k) -> p k m", k=KC)
                for k in range(KC):
                    last = T.transpose(psT[:, k * P:(k + 1) * P], xv[:, k], ident[:])
                last.then_inc(S["xgT_psum"], 1)

            def up(b, s, j, free=True):
                pe.wait_ge(S2["gu_in"][s], 32 * j + 32)
                pe.wait_ge(S["xgT_ready"], b + 1)
                if free:
                    pe.wait_ge(S["dact_ready"], b - 1)
                for m in range(2):
                    for k in range(KC):
                        last = T.matmul(psP[:, s * 512 + m * F:s * 512 + (m + 1) * F], xgT[:, s, k], wg[:, s, m, k * F:(k + 1) * F],
                                        start=k == 0, stop=k == KC - 1)
                last.then_inc(S["up_psum"], 1)

            def a_tr(b):
                pe.wait_ge(S["dact_ready"], b + 1)
                av = actD[:].rearrange("p (m j) -> p j m", j=2)
                for jj in range(2):
                    last = T.transpose(psQ[:, jj * P:(jj + 1) * P], av[:, jj], ident[:])
                last.then_inc(S["dactT_psum"], 1)

            def down(b, s, j, free=True):
                pe.wait_ge(S2["dn_in"][s], 16 * j + 16)
                pe.wait_ge(S["dactT_ready"], b + 1)
                if free:
                    pe.wait_ge(S["ysb_ready"], b)
                for h in range(2):
                    for jj in range(2):
                        last = T.matmul(psS[:, h * 512:h * 512 + 512], actDT[:, jj], wg[:, s, 2, jj * D + h * 512:jj * D + h * 512 + 512],
                                        start=jj == 0, stop=jj == 1)
                last.then_inc(S["down_psum"], 1)

            x_tr(0, 0, 16)
            up(0, 0, 0, free=False)
            pe.wait_ge(S["xgT_ready"], 1)
            x_tr(1, 1, 16)
            up(1, 1, 0, free=False)
            a_tr(0)
            pe.wait_ge(S["xgT_ready"], 2)
            x_tr(2, 0, 32)
            down(0, 0, 0, free=False)
            pe.wait_ge(S["blkr_in"], 16)
            last_pair = pe.value_load(nblk[0:1, 0:1], min_val=0, max_val=NB // 2 - 1)
            with pe.Fori(1, NB // 2) as j:
                with pe.If(j < last_pair + 1):
                    for s in range(2):
                        b = 2 * j + s
                        up(b, s, j)
                        a_tr(b - 1)
                        x_tr(b + 1, 1 - s, 16 * (j + 1 + s))
                        down(b - 1, 1 - s, j - 1 + s)
            a_tr(last_pair * 2 + 1)
            down(last_pair * 2 + 1, 1, last_pair)


_INS = ["x_prompt", "x_sample", "c_prompt", "c_sample", "cache_k_win", "cache_v_win", "state_conv",
        "state_rnn", "ada_w", "ada_b", "norm_mix", "w_in", "conv_w", "conv_b", "gate_a_w", "gate_a_b",
        "gate_x_w", "gate_x_b", "lru_lambda", "q_norm", "k_norm", "attn_sinks", "w_out", "norm_ffn",
        "router_w", "router_bias", "exp_w_gate", "exp_w_up", "exp_w_down", "sh_w_gate", "sh_w_up",
        "sh_w_down"]
_OUTS = [(1, 2048, 1024), (8, 4, 1024), (1, 1, 128, 2, 64), (1, 1, 128, 2, 64), (1, 1, 3, 512), (1, 1, 512),
         (1, 8, 128, 2, 64), (1, 8, 128, 2, 64), (1, 8, 3, 512), (1, 8, 512)]


def kernel(**inputs):
    import numpy as _np
    import concourse.bacc as _bacc
    from concourse import mybir as _mybir
    from concourse.bass_utils import run_bass_kernel_spmd as _run

    nc = _bacc.Bacc("TRN2", target_bir_lowering=False, num_devices=1)
    arrays, args = {}, []
    for name in _INS:
        a = _np.ascontiguousarray(inputs[name])
        arrays[f"in_{name}_dram"] = a
        args.append(nc.dram_tensor(f"in_{name}_dram", a.shape, _mybir.dt.from_np(a.dtype), kind="ExternalInput").ap())
    for i, shape in enumerate(_OUTS):
        args.append(nc.dram_tensor(f"out_{i}_dram", shape, _mybir.dt.float32, kind="ExternalOutput").ap())
    program(nc, *args)
    r = _run(nc, [arrays], core_ids=[0])
    return tuple(r.results[0][f"out_{i}_dram"] for i in range(len(_OUTS)))
```

```python
from contextlib import ExitStack

import concourse.bass as bass
from concourse import mybir

ALU = mybir.AluOpType
ACT = mybir.ActivationFunctionType
AX = mybir.AxisListType
F32 = mybir.dt.float32
I32 = mybir.dt.int32
U32 = mybir.dt.uint32

P = 128
NEG = -1e30
EPS = 1e-6
LRU_C = 8.0
ROUTE_SCALE = 2.5
GELU_C = 0.7978845608028654
GELU_A = 0.044715


def program(nc, x_prompt, x_sample, c_prompt, c_sample, cache_k_win, cache_v_win, state_conv, state_rnn,
            ada_w, ada_b, norm_mix, w_in, conv_w, conv_b, gate_a_w, gate_a_b, gate_x_w, gate_x_b,
            lru_lambda, q_norm, k_norm, attn_sinks, w_out, norm_ffn, router_w, router_bias,
            exp_w_gate, exp_w_up, exp_w_down, sh_w_gate, sh_w_up, sh_w_down,
            y_prompt, y_sample, k_win_prompt, v_win_prompt, conv_prompt, rnn_prompt,
            k_win_sample, v_win_sample, conv_sample, rnn_sample):
    SEQ, D = x_prompt.shape[1], x_prompt.shape[2]
    NS, TS = x_sample.shape[0], x_sample.shape[1]
    KC = D // P
    R = conv_w.shape[2]
    RC = R // P
    HD = q_norm.shape[1]
    NH = attn_sinks.shape[1]
    NKV = cache_k_win.shape[3]
    GQ = NH // NKV
    KVD = NKV * HD
    QD = NH * HD
    QKV = QD + 2 * KVD
    DIN = w_in.shape[2]
    NE = exp_w_gate.shape[1]
    F = exp_w_gate.shape[3]
    NG = 8
    GE = NE // NG
    TG = 4
    TOPK = 6
    NT = SEQ // P
    TAIL = NS * TS
    NTOK = SEQ + TAIL
    HALO = conv_w.shape[1] - 1
    NB = (NTOK * TOPK + NE * (P - 1)) // P
    NB += NB % 2
    LB = -(-NTOK // P)
    SLOTS = 4
    NBT = NB + 4
    MOD = 6 * D
    ALL = NT + 1
    assert TAIL <= 32 and KC == 8 and RC == 4 and KVD == P and QD == 4 * P and R == 4 * P and 2 * F == 512
    assert NE * LB < 9 * P and NE % SLOTS == 0 and NS == 8 and TS == 4 and GQ * TS <= 32

    def dram(name, shape, dt=F32):
        return nc.dram_tensor(name, shape, dt, kind="Internal").ap()

    mod_d = dram("mod_d", [TAIL + 1, MOD])
    mix_d = dram("mix_d", [ALL, P, 2 * RC, P])
    h2_d = dram("h2_d", [NTOK + P, D])
    x2_d = dram("x2_d", [NTOK, D])
    acc_d = dram("acc_d", [NTOK + P, D])
    LROWS = 9 * P
    list_d = dram("list_d", [LROWS * P, 2])
    blk_d = dram("blk_d", [2 * P, 2], I32)

    with ExitStack() as ctx:
        def sem(name):
            return ctx.enter_context(nc.semaphore(name))

        base = (nc.sbuf_base + 31) // 32 * 32
        KB = 1024
        XW = base + 0
        YW = XW + 58 * KB
        WK = YW + 59 * KB
        end = {"v": WK, "lim": nc.sbuf_usable_end}

        def at(name, shape, off, dt=F32):
            size = 4
            for s in shape[1:]:
                size *= s
            assert off + size <= end["lim"], (name, off, size, end["lim"])
            return nc.alloc_sbuf_tensor_at(name, shape, dt, offset=off), off + (size + 31) // 32 * 32

        o = WK
        ident, o = at("ident", [P, P], o)
        tri, o = at("tri", [P, P], o)
        ones, o = at("ones", [P, P], o)
        mhalf, o = at("mhalf", [P, 16], o)
        epsc, o = at("epsc", [P, 16], o)
        stat, o = at("stat", [P, 4, 40], o)
        blkr, o = at("blkr", [1, 2 * P, 2], o, I32)
        strt, o = at("strt", [1, NE], o, I32)
        nblk, o = at("nblk", [1, 8], o, I32)
        pid, o = at("pid", [P, 8], o, I32)
        smc, o = at("smc", [P, 16], o)
        gsel, o = at("gsel", [P, 2, GQ], o)
        gtmp, o = at("gtmp", [P, 2, NH], o)
        jdist, o = at("jdist", [P, P + TAIL], o)
        PERS = o

        ada_wt, _ = at("ada_wt", [P, 2, KC, 512], YW)
        o = end["lim"] - 40 * KB
        o -= o % 32
        cp_t, o = at("cp_t", [P, KC], o)
        cs_t, o = at("cs_t", [P, NS, KC], o)
        cp_h, o = at("cp_h", [P, KC], o)
        cs_h, o = at("cs_h", [P, NS, KC], o)
        csil, o = at("csil", [P, KC, TAIL + 1], o)
        adab, o = at("adab", [TAIL + 1, MOD], o)
        gmix, o = at("gmix", [TAIL + 1, 2, D], o)
        modc, o = at("modc", [TAIL + 1, 2, 512], o)

        win, _ = at("win", [P, KC, DIN], XW)
        o = PERS
        modA, o = at("modA", [P, 2, D], o)
        bias, o = at("bias", [P, NH, 2 * P], o)
        prm, o = at("prm", [P, RC, 40], o)
        gb, o = at("gb", [P, 2 * RC], o)
        lam8, o = at("lam8", [P, RC, 2], o)
        ssq, o = at("ssq", [P, 2], o)
        rst, o = at("rst", [P, 4], o)
        ss10, o = at("ss10", [P, 16], o)
        r10, o = at("r10", [P, 32], o)
        sink, o = at("sink", [P, NH], o)
        mx, o = at("mx", [P, 2, 4, GQ], o)
        esum, o = at("esum", [P, 2, 2, GQ], o)
        hlast, o = at("hlast", [P, RC, 1], o)
        stt, o = at("stt", [P, RC, 36], o)
        xin, o = at("xin", [P, 2, D], o)
        o_hrow = o
        hrow, o = at("hrow", [P, D], o)
        o_hT = o
        hT, o = at("hT", [P, KC, P], o)
        o_xrb = o
        xrb, o = at("xrb", [P, RC, HALO + P], o)
        u, o = at("u", [P, RC, P], o)
        y_t, o = at("y_t", [P, RC, P], o)
        sq_t, o = at("sq_t", [P, RC, P], o)
        gts, o = at("gts", [P, 2 * RC, P], o)
        a_t, o = at("a_t", [P, RC, P], o)
        th_t, o = at("th_t", [P, RC, P], o)
        b_t, o = at("b_t", [P, RC, P], o)
        outr, o = at("outr", [P, RC, P], o)
        qkv, o = at("qkv", [P, QKV], o)
        qn, o = at("qn", [P, QD + KVD], o)
        qT, o = at("qT", [P, 5, P], o)
        kT, o = at("kT", [P, 2, P], o)
        vb, o = at("vb", [P, 2, KVD], o)
        o_sc = o
        sc, o = at("sc", [P, 2, GQ, 2 * P], o)
        o_PT = o
        PT, o = at("PT", [P, GQ, 2, P], o)
        endA = o
        lini, _ = at("lini", [P, P, 2], o_xrb)
        zrow, _ = at("zrow", [P, D], o_hT)
        o = YW + 33 * KB
        gwt, o = at("gwt", [P, 2, RC, P], o)
        prm_r, o = at("prm_r", [40, R], o)
        stt_r, o = at("stt_r", [36, R], o)
        sqj, o = at("sqj", [P, D], o)
        hs_t, o = at("hs_t", [P, RC, P], o)
        orow, o = at("orow", [P, QD], o)
        oT, o = at("oT", [P, RC, P], o)
        qw, o = at("qw", [P, QD + KVD], o)
        assert o <= WK, o - WK

        wout, _ = at("wout", [P, KC, D], YW)
        o = XW
        shgu, o = at("shgu", [P, KC, 2 * F], o)
        shd, o = at("shd", [P, 2, D], o)
        rw, o = at("rw", [P, KC, NE], o)
        modB, o = at("modB", [P, 3, D], o)
        rbias, o = at("rbias", [P, NE], o)
        ck8, o = at("ck8", [P, NS, KVD], o)
        vb8, o = at("vb8", [P, NS, KVD], o)
        kT8, o = at("kT8", [P, NS, P], o)
        kTn, o = at("kTn", [P, TAIL], o)
        qTs, o = at("qTs", [P, NS, 32], o)
        biasS, o = at("biasS", [P, 2, NKV, P + TAIL], o)
        orowS, o = at("orowS", [P, 2, KVD], o)
        oTs, o = at("oTs", [P, GQ, TAIL], o)
        assert o <= YW, o - YW
        scS, _ = at("scS", [P, 2, NKV, P + TAIL], o_sc)
        PTs, _ = at("PTs", [P, 2 * NKV, P], o_PT)
        PTn, _ = at("PTn", [TAIL, 2 * NKV, P], o_hrow)
        distS, o = at("distS", [P, 2, P + TAIL], o_hT)
        penS, o = at("penS", [P, 2, P + TAIL], o)
        penT, o = at("penT", [P, 2, P + TAIL], o)
        mxS, o = at("mxS", [P, 6, 2, NKV], o)
        o = PERS
        iota, o = at("iota", [P, NE], o)
        mrun, o = at("mrun", [P, NE], o)
        msk_all, o = at("msk_all", [P, ALL, NE], o)
        pos_all, o = at("pos_all", [P, ALL, NE], o)
        tokf, o = at("tokf", [P, ALL], o)
        iotp, o = at("iotp", [P, 2], o)
        idxf, o = at("idxf", [P, 8], o)
        wgt, o = at("wgt", [P, 8], o)
        posk, o = at("posk", [P, 2, 2, 8], o)
        entry, o = at("entry", [P, 2, TOPK, 2], o)
        dstf, o = at("dstf", [P, 2, 8], o)
        dsti, o = at("dsti", [P, 2, 8], o, I32)
        keepC = o
        mixb, o = at("mixb", [P, 2, 2 * RC, P], o)
        xb, o = at("xb", [P, 2, D], o)
        x2, o = at("x2", [P, 2, D], o)
        h2, o = at("h2", [P, D], o)
        h2T, o = at("h2T", [P, KC, P], o)
        sg, o = at("sg", [P, 2, F], o)
        actr, o = at("actr", [P, F], o)
        actT, o = at("actT", [P, 2, P], o)
        sho, o = at("sho", [P, 2, D], o)
        rt_s, o = at("rt_s", [P, NE], o)
        rt_b, o = at("rt_b", [P, NE], o)
        rt_m, o = at("rt_m", [P, NE], o)
        rt_8, o = at("rt_8", [P, NG, 8], o)
        rt_g, o = at("rt_g", [P, 4, 8], o)
        rt_u, o = at("rt_u", [P, 2, 8], o, U32)
        rt_oh, o = at("rt_oh", [P, TOPK, NE], o)
        rt_t, o = at("rt_t", [P, TOPK, NE], o)
        ssqB, o = at("ssqB", [P, 4], o)
        sqB, o = at("sqB", [P, D], o)

        cnt, o = at("cnt", [P, 6, NE], o)
        cnti, o = at("cnti", [P, 2, NE], o, I32)
        blkf, o = at("blkf", [P, 4, NE], o)
        blki, o = at("blki", [P, 2, 2], o, I32)
        bsum, o = at("bsum", [P, 4, 2], o)

        wg, o = at("wg", [P, SLOTS, 3, KC * F], XW)
        assert o <= WK
        o = PERS
        lent, o = at("lent", [P, 2, 2], o)
        gix, o = at("gix", [P, 2, 1], o, I32)
        six, o = at("six", [P, 2, 1], o, I32)
        tok_all, o = at("tok_all", [P, NBT], o, I32)
        w_all, o = at("w_all", [P, NBT], o)
        xg, o = at("xg", [P, 2, D], o)
        xgT, o = at("xgT", [P, 2, KC, P], o)
        sgD, o = at("sgD", [P, 2, F], o)
        actD, o = at("actD", [P, F], o)
        actDT, o = at("actDT", [P, 2, P], o)
        ysb, o = at("ysb", [P, 2, D], o)
        o = YW
        acc, o = at("acc", [P, 4, D], o)
        xe, o = at("xe", [P, 4, D], o)
        g2b, o = at("g2b", [P, 2, D], o)
        ye, o = at("ye", [P, 4, D], o)
        assert o <= WK

        psT = ctx.enter_context(nc.psum_tensor("psT", [P, 1024], F32))
        psP = ctx.enter_context(nc.psum_tensor("psP", [P, 1024], F32))
        psQ = ctx.enter_context(nc.psum_tensor("psQ", [P, 1024], F32))
        psS = ctx.enter_context(nc.psum_tensor("psS", [P, 1024], F32))

        names = """c_in norms_in ada_psum_ready mod_row_ready mod_bank_free csil_ready c_tanh prm_in prm_psum prm_ready sink_in
            qw_in gate_w_zero gate_w_in const_ready bias_ready modA_in win_in tailmod_in
            ssq_ready rstd_ready h_ready hT_psum hT_ready xr_psum xr_ready conv_ready yr_psum y_ready
            gates_psum gates_sum gates_tanh loga_ready a_ready b2_ready bsqrt_ready gelu_in gelu_tanh
            outr_ready qkv1_psum qkv2_psum qkv_ready ss10_ready r10_ready qn_ready v_ready qkT_psum qkT_ready
            s_psum s_read m_ready p_ready pT_psum pT_ready o_psum o_ready oT_psum oT_ready
            lam_exp lam_one             kwin_st small_psum small_ready small_st cachecp_st init_st             smp_in smp_q0 ckT_psum ckT_ready smp_s smp_m smp_p smp_pT smp_pTo smp_o smp_or smp_oT smp_oTo smp_oT_st
            wB_in modB_in rbias_in mixed_psum x2_ready ssqB_ready rstdB_ready h2_ready h2T_psum h2T_ready
            router_psum rtanh shup_psum shtanh act_ready actT_ready shd_psum sh_ready
            pos_psum msk_ready iota_ready tailmodB_in mrun_ready entry_ready pid_ready
            cnt_psum blk_ready blk_st blkr_in w_in lent_used
            xgT_psum xgT_ready up_psum dtanh dact_ready dactT_psum dactT_ready down_psum ysb_ready
            outr_st oT_st ye_ready g2_in add_st""".split()
        S = {n: sem(n) for n in names}
        slots2 = """ada_in mod_st x_in mix_in xB_in x2_st h2_st sh_st list_st lent_in gather_in""".split()
        S2 = {n: [sem(f"{n}0"), sem(f"{n}1")] for n in slots2}
        S4 = {n: [sem(f"{n}{k}") for k in range(4)] for n in ("xe_in", "out_st")}

        block = ctx.enter_context(nc.Block())
        NCH = MOD // 512
        ada_v = ada_w[0].rearrange("(p k) n -> p k n", k=KC)
        SMP = NT

        def bc(ap, n):
            return ap.unsqueeze(len(ap.shape)).to_broadcast(list(ap.shape) + [n])

        @block.sync
        def _(sp):
            sp.dma_start(cp_t[:], c_prompt[0].rearrange("(p k) -> p k", k=KC)).then_inc(S["c_in"], 16)
            sp.dma_start(cs_t[:], c_sample.rearrange("b (p k) -> p b k", k=KC)).then_inc(S["c_in"], 16)
            for s in range(2):
                sp.dma_start(ada_wt[:, s], ada_v[:, :, s * 512:(s + 1) * 512]).then_inc(S2["ada_in"][s], 16)
            with sp.Fori(1, NCH // 2) as j:
                for s in range(2):
                    sp.wait_ge(S["ada_psum_ready"], 2 * j + s - 1)
                    sp.dma_start(ada_wt[:, s], ada_v[:, :, bass.ds(j * 1024 + s * 512, 512)]).then_inc(S2["ada_in"][s], 16)
            sp.dma_start(xin[:, 0], x_prompt[0, 0:P]).then_inc(S2["x_in"][0], 16)
            sp.dma_start(xin[:, 1], x_prompt[0, P:2 * P]).then_inc(S2["x_in"][1], 16)
            sp.dma_start(win[:], w_in[0].rearrange("(p k) n -> p k n", k=KC)).then_inc(S["win_in"], 16)
            for s in range(2):
                sp.wait_ge(S2["mod_st"][s], 16 * (NCH // 2))
            sp.dma_start(modA[:], mod_d[TAIL:TAIL + 1, 0:2 * D].rearrange("a (m d) -> a m d", m=2)
                         .to_broadcast([P, 2, D])).then_inc(S["modA_in"], 16)
            sp.wait_ge(S["ada_psum_ready"], NCH)
            sp.dma_start(wout[:], w_out[0].rearrange("(c p) n -> p c n", p=P)).then_inc(S["wB_in"], 16)

            def step(i, par, nxt=True, proj=True, att=True, n=P):
                if nxt:
                    sp.wait_ge(S["h_ready"], i + 1)
                    sp.dma_start(xin[:, par], x_prompt[0, bass.ds((i + 2) * P, P)]).then_inc(S2["x_in"][par], 16)
                if proj:
                    sp.wait_ge(S["outr_ready"], i + 1)
                    sp.dma_start(mix_d[i, :, 0:RC, 0:n], outr[:, :, 0:n]).then_inc(S["outr_st"], 16)
                if att:
                    sp.wait_ge(S["oT_ready"], i)
                    sp.dma_start(mix_d[i - 1, :, RC:2 * RC, :], oT[:]).then_inc(S["oT_st"], 16)

            step(0, 0, att=False)
            step(1, 1)
            with sp.Fori(1, NT // 2 - 1) as j:
                for s in range(2):
                    step(2 * j + s, s)
            sp.wait_ge(S["h_ready"], NT - 1)
            sp.dma_start(xin[0:TAIL, 0], x_sample.rearrange("b t d -> (b t) d")).then_inc(S2["x_in"][0], 16)
            step(NT - 2, 0, nxt=False)
            sp.wait_ge(S["h_ready"], NT)
            sp.dma_start(modA[0:TAIL], mod_d[0:TAIL, 0:2 * D].rearrange("a (m d) -> a m d", m=2)).then_inc(S["tailmod_in"], 16)
            step(NT - 1, 1, nxt=False)
            sp.wait_ge(S["qn_ready"], NT)
            sp.dma_start(k_win_prompt[0, 0].rearrange("t h d -> t (h d)"), qn[:, QD:]).then_inc(S["kwin_st"], 16)
            sp.dma_start(v_win_prompt[0, 0].rearrange("t h d -> t (h d)"), qkv[:, QD + KVD:]).then_inc(S["kwin_st"], 16)
            sp.wait_ge(S["qkv2_psum"], NT + 1)
            sp.dma_start(ck8[:], cache_k_win[0].rearrange("b t h d -> t b (h d)")).then_inc(S["smp_in"], 16)
            sp.dma_start(vb8[:], cache_v_win[0].rearrange("b t h d -> t b (h d)")).then_inc(S["smp_in"], 16)
            sp.dma_start(modB[:], mod_d[TAIL:TAIL + 1, 2 * D:5 * D].rearrange("a (m d) -> a m d", m=3)
                         .to_broadcast([P, 3, D])).then_inc(S["modB_in"], 16)
            sp.dma_start(shgu[:, :, 0:F], sh_w_gate[0].rearrange("(p k) f -> p k f", k=KC)).then_inc(S["wB_in"], 16)
            sp.dma_start(shgu[:, :, F:2 * F], sh_w_up[0].rearrange("(p k) f -> p k f", k=KC)).then_inc(S["wB_in"], 16)
            sp.dma_start(shd[:], sh_w_down[0].rearrange("(p j) d -> p j d", j=2)).then_inc(S["wB_in"], 16)
            sp.dma_start(rw[:], router_w[0].rearrange("(p k) e -> p k e", k=KC)).then_inc(S["wB_in"], 16)
            sp.dma_start(rbias[:], router_bias.to_broadcast([P, NE])).then_inc(S["rbias_in"], 16)
            step(NT, 0, nxt=False, n=TAIL)
            sp.wait_ge(S["qn_ready"], NT + 1)
            for out, src in ((k_win_sample, qn[0:TAIL, QD:]), (v_win_sample, qkv[0:TAIL, QD + KVD:])):
                for b in range(NS):
                    sp.dma_start(out[0, b, P - TS:P].rearrange("t h d -> t (h d)"), src[b * TS:(b + 1) * TS]).then_inc(S["kwin_st"], 16)
            sp.wait_ge(S["small_ready"], 1)
            for dst, a, n in ((conv_prompt[0, 0], 0, HALO), (rnn_prompt[0], HALO, 1),
                              (conv_sample[0].rearrange("b j r -> (b j) r"), HALO + 1, NS * HALO),
                              (rnn_sample[0], HALO + 1 + NS * HALO, NS)):
                sp.dma_start(dst, stt_r[a:a + n]).then_inc(S["small_st"], 16)
            sp.wait_ge(S["oT_st"], 16 * NT)
            sp.wait_ge(S["outr_st"], 16 * (NT + 1))
            sp.wait_ge(S["kwin_st"], 16 * (2 + 2 * NS))

            def load_b(i, par, n=P, free=True):
                if free:
                    sp.wait_ge(S["x2_ready"], i - 1)
                sp.dma_start(mixb[:, par, :, 0:n], mix_d[i, :, :, 0:n]).then_inc(S2["mix_in"][par], 16)
                src = x_prompt[0, bass.ds(i * P, P)] if n == P else x_sample.rearrange("b t d -> (b t) d")
                sp.dma_start(xb[0:n, par], src).then_inc(S2["xB_in"][par], 16)

            def store_h2(i, par, n=P):
                sp.wait_ge(S["x2_ready"], i + 1)
                sp.dma_start(x2_d[bass.ds(i * P, n)], x2[0:n, par]).then_inc(S2["x2_st"][par], 16)
                sp.wait_ge(S["h2_ready"], i + 1)
                sp.dma_start(h2_d[bass.ds(i * P, n)], h2[0:n]).then_inc(S2["h2_st"][par], 16)

            def store_sh(i, par, n=P):
                sp.wait_ge(S["sh_ready"], i + 1)
                sp.dma_start(acc_d[bass.ds(i * P, n)], sho[0:n, par]).then_inc(S2["sh_st"][par], 16)

            load_b(0, 0, free=False)
            load_b(1, 1, free=False)
            store_h2(0, 0)
            load_b(2, 0)
            store_h2(1, 1)
            with sp.Fori(1, NT // 2 - 1) as j:
                for s in range(2):
                    load_b(2 * j + s + 1, 1 - s)
                    store_sh(2 * j + s - 2, s)
                    store_h2(2 * j + s, s)
            load_b(NT - 1, 1)
            store_sh(NT - 4, 0)
            store_h2(NT - 2, 0)
            sp.wait_ge(S["x2_ready"], NT - 1)
            sp.wait_ge(S["smp_oT_st"], 16 * 2 * GQ)
            load_b(NT, 0, TAIL)
            store_sh(NT - 3, 1)
            store_h2(NT - 1, 1)
            sp.dma_start(modB[0:TAIL], mod_d[0:TAIL, 2 * D:5 * D].rearrange("a (m d) -> a m d", m=3)).then_inc(S["tailmodB_in"], 16)
            store_sh(NT - 2, 0)
            store_h2(NT, 0, TAIL)
            store_sh(NT - 1, 1)
            store_sh(NT, 0, TAIL)

            def load_w(e, s):
                for m, w in enumerate((exp_w_gate, exp_w_up)):
                    sp.dma_start(wg[:, s, m], w[0, bass.ds(e, 1)].rearrange("a (p k) f -> p (a k f)", k=KC)).then_inc(S["w_in"], 16)
                sp.dma_start(wg[:, s, 2], exp_w_down[0, bass.ds(e, 1)].rearrange("a (p j) d -> p (a j d)", j=2)).then_inc(S["w_in"], 16)

            load_w(0, 0)
            sp.wait_ge(S["blk_ready"], 1)
            for h in range(2):
                sp.dma_start(blk_d[h * P:(h + 1) * P], blki[:, h]).then_inc(S["blk_st"], 16)
            sp.wait_ge(S["blk_st"], 32)
            sp.dma_start(blkr[:], blk_d.unsqueeze(0)).then_inc(S["blkr_in"], 16)
            for e in range(1, SLOTS):
                sp.wait_ge(S["w_in"], 48 * e)
                load_w(e, e)
            with sp.Fori(1, NE // SLOTS) as q:
                for s in range(SLOTS):
                    e = sp.snap(q * SLOTS + s)
                    sp.wait_ge(S["w_in"], e * 48)
                    free = sp.value_load(strt[0:1, bass.ds(q * SLOTS + s - SLOTS + 1, 1)], min_val=1, max_val=NB + 1)
                    sp.wait_ge(S["down_psum"], free)
                    load_w(e, s)
            sp.wait_ge(S["w_in"], 48 * NE)

            y_out = y_prompt[0]

            def load_e(t, s, n=P, free=True):
                if free:
                    sp.wait_ge(S["ye_ready"], t - 3)
                sp.dma_start(xe[0:n, s], x2_d[bass.ds(t * P, n)]).then_inc(S4["xe_in"][s], 16)
                sp.dma_start(acc[0:n, s], acc_d[bass.ds(t * P, n)]).then_inc(S4["xe_in"][s], 16)

            last_pair = sp.value_load(nblk[0:1, 0:1], min_val=0, max_val=NB // 2 - 1)
            sp.wait_ge(S["add_st"], last_pair * 32 + 32)
            sp.dma_start(g2b[:, 0], mod_d[TAIL:TAIL + 1, 5 * D:].to_broadcast([P, D])).then_inc(S["g2_in"], 16)
            sp.dma_start(g2b[0:TAIL, 1], mod_d[0:TAIL, 5 * D:]).then_inc(S["g2_in"], 16)
            for s in range(4):
                load_e(s, s, free=False)
            with sp.Fori(1, NT // 4) as q:
                for s in range(4):
                    load_e(4 * q + s, s)
            load_e(NT, 0, TAIL)
            for s in range(4):
                sp.wait_ge(S4["out_st"][s], 16 * (NT // 4 + (s == 0)))
            for n in ("small_st", "cachecp_st"):
                sp.wait_ge(S[n], 64 if n == "small_st" else 32)

        @block.gpsimd
        def _(gp):
            nc.gpsimd.memset(ident[:], 0.0)
            nc.gpsimd.memset(tri[:], 1.0)
            nc.gpsimd.memset(ones[:], 1.0)
            nc.gpsimd.memset(mhalf[:], -0.5)
            nc.gpsimd.memset(epsc[:], EPS)
            nc.gpsimd.iota(hrow[:, 0:2 * P], [[-1, 2 * P]], base=P, channel_multiplier=1, allow_small_or_imprecise_dtypes=True)
            gp.drain()
            nc.gpsimd.affine_select(out=ident[:], in_=ident[:], compare_op=ALU.not_equal, fill=1.0, base=0,
                                    pattern=[[-1, P]], channel_multiplier=1)
            nc.gpsimd.affine_select(out=tri[:], in_=tri[:], compare_op=ALU.is_gt, fill=0.0, base=0,
                                    pattern=[[1, P]], channel_multiplier=-1)
            gp.drain().then_inc(S["const_ready"], 1)
            for h in range(NH):
                nc.gpsimd.tensor_scalar(bias[:, h], hrow[:, 0:2 * P], -(2.0 ** (-8.0 * (h + 1) / NH)), None, ALU.mult)
            gp.drain()
            nc.gpsimd.affine_select(out=bias[:], in_=bias[:], compare_op=ALU.is_ge, fill=NEG, base=P,
                                    pattern=[[0, NH], [-1, 2 * P]], channel_multiplier=1)
            gp.drain()
            nc.gpsimd.affine_select(out=bias[:], in_=bias[:], compare_op=ALU.is_ge, fill=NEG, base=0,
                                    pattern=[[0, NH], [1, 2 * P]], channel_multiplier=-1)
            gp.drain().then_inc(S["bias_ready"], 1)
            nc.gpsimd.memset(lini[:], 0.0)
            nc.gpsimd.memset(zrow[:], 0.0)
            nc.gpsimd.iota(pid[:, 0:1], [[1, 1]], base=0, channel_multiplier=1)
            nc.gpsimd.iota(jdist[:, 0:P], [[-1, P]], base=P, channel_multiplier=0, allow_small_or_imprecise_dtypes=True)
            nc.gpsimd.iota(jdist[:, P:], [[-1, TAIL]], base=0, channel_multiplier=0, allow_small_or_imprecise_dtypes=True)
            gp.drain().then_inc(S["pid_ready"], 1)
            nc.gpsimd.iota(lini[:, :, 0], [[1, P]], base=NTOK, channel_multiplier=0, allow_small_or_imprecise_dtypes=True)
            gp.drain()
            gp.dma_start(list_d.rearrange("(p b c) a -> p b c a", p=P, c=P), lini[:].unsqueeze(1).to_broadcast([P, 9, P, 2])
                         ).then_inc(S["init_st"], 16)
            gp.dma_start(h2_d[NTOK:], zrow[:]).then_inc(S["init_st"], 16)
            gp.dma_start(acc_d[NTOK:], zrow[:]).then_inc(S["init_st"], 16)
            gp.dma_start(k_win_sample[0, :, 0:P - TS].rearrange("b t h d -> b (t h d)"),
                         cache_k_win[0, :, TS:P].rearrange("b t h d -> b (t h d)")).then_inc(S["cachecp_st"], 16)
            gp.dma_start(v_win_sample[0, :, 0:P - TS].rearrange("b t h d -> b (t h d)"),
                         cache_v_win[0, :, TS:P].rearrange("b t h d -> b (t h d)")).then_inc(S["cachecp_st"], 16)

            def rstd(i, par, n=P):
                gp.wait_ge(S["ssq_ready"], i + 1)
                nc.gpsimd.tensor_tensor(rst[0:n, 2:3], ssq[0:n, par:par + 1], epsc[0:n, 0:1], ALU.add)
                gp.drain()
                nc.gpsimd.tensor_tensor(rst[0:n, par:par + 1], rst[0:n, 2:3], mhalf[0:n, 0:1], ALU.pow).then_inc(S["rstd_ready"], 1)

            def r10_of(i, n=P):
                gp.wait_ge(S["ss10_ready"], i + 1)
                nc.gpsimd.tensor_tensor(r10[0:n, 16:16 + NH + NKV], ss10[0:n, 0:NH + NKV], epsc[0:n, 0:NH + NKV], ALU.add)
                gp.drain()
                nc.gpsimd.tensor_tensor(r10[0:n, 0:NH + NKV], r10[0:n, 16:16 + NH + NKV], mhalf[0:n, 0:NH + NKV],
                                        ALU.pow).then_inc(S["r10_ready"], 1)

            rstd(0, 0)
            with gp.Fori(0, NT // 2 - 1) as j:
                for s in range(2):
                    rstd(2 * j + s + 1, 1 - s)
                    r10_of(2 * j + s)
            rstd(NT - 1, 1)
            r10_of(NT - 2)
            rstd(NT, 0, TAIL)
            r10_of(NT - 1)
            r10_of(NT, TAIL)

            gp.wait_ge(S["r10_ready"], NT + 1)
            gp.wait_ge(S["smp_s"], 1)
            nc.gpsimd.iota(iota[:], [[1, NE]], base=0, channel_multiplier=0, allow_small_or_imprecise_dtypes=True)
            nc.gpsimd.iota(tokf[:], [[P, ALL]], base=0, channel_multiplier=1, allow_small_or_imprecise_dtypes=True)
            nc.gpsimd.iota(iotp[:], [[P, 2]], base=0, channel_multiplier=1, allow_small_or_imprecise_dtypes=True)
            gp.drain().then_inc(S["iota_ready"], 1)
            gp.wait_ge(S["init_st"], 48)
            gp.nop()

            def rstd_b(i, n=P):
                gp.wait_ge(S["ssqB_ready"], i + 1)
                nc.gpsimd.tensor_tensor(ssqB[0:n, 2:3], ssqB[0:n, 0:1], epsc[0:n, 0:1], ALU.add)
                gp.drain()
                nc.gpsimd.tensor_tensor(ssqB[0:n, 1:2], ssqB[0:n, 2:3], mhalf[0:n, 0:1], ALU.pow).then_inc(S["rstdB_ready"], 1)

            def enlist(i, par, n=P):
                gp.wait_ge(S["entry_ready"], i + 1)
                nc.gpsimd.tensor_tensor(dstf[0:n, par, 0:TOPK], posk[0:n, par, 0, 0:TOPK], posk[0:n, par, 1, 0:TOPK], ALU.add)
                gp.drain()
                nc.gpsimd.tensor_copy(dsti[0:n, par, 0:TOPK], dstf[0:n, par, 0:TOPK])
                gp.drain()
                for k in range(TOPK):
                    nc.gpsimd.indirect_dma_start(list_d, bass.IndirectOffsetOnAxis(ap=dsti[0:n, par, k:k + 1], axis=0),
                                                 entry[0:n, par, k], None).then_inc(S2["list_st"][par], 16)

            rstd_b(0)
            rstd_b(1)
            with gp.Fori(1, NT // 2) as j:
                for s in range(2):
                    rstd_b(2 * j + s)
                    enlist(2 * j + s - 2, s)
            rstd_b(NT, TAIL)
            enlist(NT - 2, 0)
            enlist(NT - 1, 1)
            enlist(NT, 0, TAIL)

            def gather(b, s, half):
                gp.wait_ge(S2["lent_in"][s], 16 * half + 16)
                nc.gpsimd.tensor_copy(tok_all[:, bass.ds(b, 1)], lent[:, s, 0:1])
                nc.gpsimd.tensor_copy(gix[:, s], lent[:, s, 0:1])
                nc.gpsimd.tensor_copy(w_all[:, bass.ds(b, 1)], lent[:, s, 1:2])
                gp.drain().then_inc(S["lent_used"], 1)
                nc.gpsimd.indirect_dma_start(xg[:, s], None, h2_d, bass.IndirectOffsetOnAxis(ap=gix[:, s], axis=0)
                                             ).then_inc(S2["gather_in"][s], 16)

            def add_rows(b, s, first=False):
                if not first:
                    gp.wait_ge(S["add_st"], 16 * b)
                gp.wait_ge(S["ysb_ready"], b + 1)
                nc.gpsimd.tensor_copy(six[:, s], tok_all[:, bass.ds(b, 1)])
                gp.drain()
                nc.gpsimd.indirect_dma_start(acc_d, bass.IndirectOffsetOnAxis(ap=six[:, s], axis=0), ysb[:, s], None,
                                             compute_op=ALU.add).then_inc(S["add_st"], 16)

            for s in range(2):
                for par in range(2):
                    gp.wait_ge(S2["h2_st"][par], 16 * (NT // 2 + 1 - par))
                gather(s, s, 0)
            for b in range(2, 5):
                gp.wait_ge(S["xgT_psum"], b - 1)
                gather(b, b % 2, b // 2)
            for par in range(2):
                gp.wait_ge(S2["sh_st"][par], 16 * (NT // 2 + 1 - par))
            add_rows(0, 0, first=True)
            last_pair = gp.value_load(nblk[0:1, 0:1], min_val=0, max_val=NB // 2 - 1)
            with gp.Fori(1, NB // 2) as j:
                with gp.If(j < last_pair + 1):
                    for s in range(2):
                        gp.wait_ge(S["xgT_psum"], 2 * j + s + 2)
                        gather(2 * j + s + 3, 1 - s, j + 1 + s)
                        add_rows(2 * j + s - 1, 1 - s)
            add_rows(last_pair * 2 + 1, 1)

        @block.scalar
        def _(act):
            for a, n, src in ((0, HALO + 1, conv_w[0]), (4, 1, conv_b), (5, 1, gate_a_b), (6, 1, gate_x_b), (7, 1, lru_lambda),
                              (8, NS * HALO, state_conv[0].rearrange("b j r -> (b j) r")), (8 + NS * HALO, NS, state_rnn[0])):
                act.dma_start(prm_r[a:a + n], src).then_inc(S["prm_in"], 16)
            act.dma_start(adab[:], ada_b.to_broadcast([TAIL + 1, MOD])).then_inc(S["norms_in"], 16)
            act.dma_start(gmix[:, 0], norm_mix.to_broadcast([TAIL + 1, D])).then_inc(S["norms_in"], 16)
            act.dma_start(gmix[:, 1], norm_ffn.to_broadcast([TAIL + 1, D])).then_inc(S["norms_in"], 16)
            act.dma_start(sink[:], attn_sinks.to_broadcast([P, NH])).then_inc(S["sink_in"], 16)
            for h in range(NH):
                act.dma_start(qw[:, h * HD:(h + 1) * HD], q_norm.to_broadcast([P, HD])).then_inc(S["qw_in"], 16)
            for h in range(NKV):
                act.dma_start(qw[:, QD + h * HD:QD + (h + 1) * HD], k_norm.to_broadcast([P, HD])).then_inc(S["qw_in"], 16)
            act.wait_ge(S["c_in"], 32)
            nc.scalar.activation(cp_h[:], cp_t[:], ACT.Tanh, scale=0.5)
            nc.scalar.activation(cs_h[:], cs_t[:], ACT.Tanh, scale=0.5).then_inc(S["c_tanh"], 1)
            act.wait_ge(S["gate_w_zero"], 1)
            for g, w in enumerate((gate_a_w, gate_x_w)):
                for two in range(2):
                    act.dma_start(gwt[64 * two:64 * two + 64, g, :, 64 * two:64 * two + 64],
                                  w[0].rearrange("(c two) i j -> two i c j", two=2)[two]).then_inc(S["gate_w_in"], 16)
            with act.Fori(0, NCH // 2) as j:
                for s in range(2):
                    act.wait_ge(S["mod_row_ready"], 2 * j + s + 1)
                    act.dma_start(mod_d[:, bass.ds(j * 1024 + s * 512, 512)], modc[:, s]).then_inc(S2["mod_st"][s], 16)
            act.wait_ge(S["lam_exp"], 1)
            nc.scalar.activation(lam8[:, :, 1], lam8[:, :, 1], ACT.Exp, scale=-1.0).then_inc(S["lam_one"], 1)

            def sumsq(i, par, half, n=P):
                act.wait_ge(S2["x_in"][par], 16 * (half + 1))
                nc.scalar.activation(sqj[0:n], xin[0:n, par], ACT.Square, scale=D ** -0.5, accum_out=ssq[0:n, par:par + 1]).then_inc(S["ssq_ready"], 1)

            def hT_out(i, n=P):
                act.wait_ge(S["hT_psum"], i + 1)
                nc.scalar.activation(hT[:, :, 0:n], psT[:].rearrange("p (k t) -> p k t", k=KC)[:, :, 0:n], ACT.Copy).then_inc(S["hT_ready"], 1)

            def exps(n, h):
                act.wait_ge(S["m_ready"], 2 * n + h + 1)
                nc.scalar.activation(esum[:, h, 1], mx[:, h, 2], ACT.Exp)
                for g in range(GQ):
                    last = nc.scalar.activation(sc[:, h, g], sc[:, h, g], ACT.Exp, bias=mx[:, h, 1, g:g + 1],
                                                accum_out=esum[:, h, 0, g:g + 1])
                last.then_inc(S["p_ready"], 1)

            def pT_out(n, h, first=False):
                act.wait_ge(S["pT_psum"], 2 * n + h + 1)
                if not (first and h == 0):
                    act.wait_ge(S["o_psum"], 2 * n + h)
                nc.scalar.activation(PT[:].rearrange("p g b t -> p (g b t)"), psT[:], ACT.Copy).then_inc(S["pT_ready"], 1)

            def oT_out(n, first=False):
                act.wait_ge(S["oT_psum"], n + 1)
                if not first:
                    act.wait_ge(S["oT_st"], 16 * n)
                nc.scalar.activation(oT[:].rearrange("p c t -> p (c t)"), psS[:, 0:512], ACT.Copy).then_inc(S["oT_ready"], 1)

            def step(i, par, half, proj=True, att=True, nxt=True, first=False, n=P, n_next=P):
                a = i - 1
                if nxt:
                    sumsq(i + 1, 1 - par, half + par, n_next)
                if proj:
                    act.wait_ge(S["xr_psum"], i + 1)
                    if not (isinstance(i, int) and i == 0):
                        act.wait_ge(S["conv_ready"], i)
                    if n == P:
                        nc.scalar.activation(xrb[:, :, HALO:HALO + P], psP[:, 0:512].rearrange("p (c t) -> p c t", c=RC),
                                             ACT.Copy).then_inc(S["xr_ready"], 1)
                    else:
                        for c in range(RC):
                            last = nc.scalar.activation(
                                xrb[:, c, 0:NS * (TS + HALO)].rearrange("p (b t) -> p b t", b=NS)[:, :, HALO:],
                                psP[:, c * P:c * P + n].rearrange("p (b t) -> p b t", b=NS), ACT.Copy)
                        last.then_inc(S["xr_ready"], 1)
                if att:
                    act.wait_ge(S["qkT_psum"], a + 1)
                    nc.scalar.activation(qT[:, 0:4].rearrange("p c t -> p (c t)"), psT[:, 0:512], ACT.Copy)
                    nc.scalar.activation(kT[:, 1 - par], psT[:, 512:640], ACT.Copy).then_inc(S["qkT_ready"], 1)
                if proj:
                    act.wait_ge(S["yr_psum"], i + 1)
                    if not (isinstance(i, int) and i == 0):
                        act.wait_ge(S["outr_ready"], i)
                    yps = psP[:, 512:1024].rearrange("p (c t) -> p c t", c=RC)[:, :, 0:n]
                    nc.scalar.activation(y_t[:, :, 0:n], yps, ACT.Copy)
                    nc.scalar.activation(sq_t[:, :, 0:n], yps, ACT.Square).then_inc(S["y_ready"], 1)
                if att:
                    exps(a, 0)
                if proj:
                    act.wait_ge(S["gates_sum"], i + 1)
                    nc.scalar.activation(gts[:, :, 0:n], gts[:, :, 0:n], ACT.Tanh, scale=0.5).then_inc(S["gates_tanh"], 1)
                if att:
                    pT_out(a, 0, first)
                if proj:
                    act.wait_ge(S["loga_ready"], i + 1)
                    nc.scalar.activation(a_t[:, :, 0:n], b_t[:, :, 0:n], ACT.Exp)
                    nc.scalar.activation(th_t[:, :, 0:n], b_t[:, :, 0:n], ACT.Tanh).then_inc(S["a_ready"], 1)
                if att:
                    exps(a, 1)
                if proj:
                    act.wait_ge(S["gelu_in"], i + 1)
                    nc.scalar.activation(sq_t[:, :, 0:n], sq_t[:, :, 0:n], ACT.Tanh, scale=GELU_C).then_inc(S["gelu_tanh"], 1)
                if att:
                    pT_out(a, 1, first)
                if proj:
                    act.wait_ge(S["b2_ready"], i + 1)
                    nc.scalar.activation(b_t[:, :, 0:n], b_t[:, :, 0:n], ACT.Sqrt).then_inc(S["bsqrt_ready"], 1)
                    act.wait_ge(S["qkv2_psum"], i + 1)
                    if att:
                        act.wait_ge(S["v_ready"], i)
                        act.wait_ge(S["qn_ready"], i)
                    if n != P:
                        act.wait_ge(S["kwin_st"], 32)
                    nc.scalar.activation(qkv[0:n], psQ[0:n, 0:QKV], ACT.Copy).then_inc(S["qkv_ready"], 1)
                if nxt:
                    hT_out(i + 1, n_next)
                if att:
                    oT_out(a, first)

            sumsq(0, 0, 0)
            hT_out(0)
            step(0, 0, 0, att=False)
            step(1, 1, 0, first=True)
            with act.Fori(1, NT // 2 - 1) as j:
                for s in range(2):
                    step(2 * j + s, s, j)
            step(NT - 2, 0, NT // 2 - 1)
            step(NT - 1, 1, NT // 2 - 1, n_next=TAIL)
            step(NT, 0, NT // 2, nxt=False, n=TAIL)
            act.wait_ge(S["smp_q0"], 1)
            act.wait_ge(S["qkT_psum"], NT + 1)
            nc.scalar.activation(kTn[:], psT[:, 4 * P:4 * P + TAIL], ACT.Copy)
            for g in range(GQ):
                last = nc.scalar.activation(qTs[:, :, g * TS:(g + 1) * TS], psT[:, g * P:g * P + TAIL].rearrange("p (b t) -> p b t", b=NS),
                                            ACT.Copy)
            last.then_inc(S["qkT_ready"], 1)
            act.wait_ge(S["ckT_psum"], 1)
            nc.scalar.activation(kT8[:].rearrange("p b t -> p (b t)"), psP[:], ACT.Copy).then_inc(S["ckT_ready"], 1)
            act.wait_ge(S["smp_m"], 1)
            nc.scalar.activation(mxS[:, 4], mxS[:, 2], ACT.Exp)
            for half in range(2):
                for h in range(NKV):
                    last = nc.scalar.activation(scS[:, half, h], scS[:, half, h], ACT.Exp, bias=mxS[:, 1, half, h:h + 1],
                                                accum_out=mxS[:, 3, half, h:h + 1])
            last.then_inc(S["smp_p"], 1)
            act.wait_ge(S["smp_pT"], 1)
            nc.scalar.activation(PTs[:].rearrange("p c t -> p (c t)"), psT[:, 0:512], ACT.Copy)
            nc.scalar.activation(PTn[:].rearrange("p c t -> p (c t)"), psT[0:TAIL, 512:1024], ACT.Copy).then_inc(S["smp_pTo"], 1)
            act.wait_ge(S["smp_oT"], 1)
            for g in range(GQ):
                last = nc.scalar.activation(oTs[:, g].rearrange("p (b t) -> p b t", b=NS),
                                            psT[:, 0:2 * P].rearrange("p (b r) -> p b r", b=NS)[:, :, g * TS:(g + 1) * TS], ACT.Copy)
            last.then_inc(S["smp_oTo"], 1)
            act.wait_ge(S["smp_oTo"], 1)
            for g in range(GQ):
                for h in range(NKV):
                    head = h * GQ + g
                    act.dma_start(mix_d[NT, (head % 2) * HD:(head % 2) * HD + HD, RC + head // 2, 0:TAIL],
                                  oTs[h * HD:(h + 1) * HD, g]).then_inc(S["smp_oT_st"], 16)

            def step_b(i, par, half, d0=True, d1=True, d2=True, n0=P, n1=P, n2=P, st=None):
                if d2:
                    act.wait_ge(S["pos_psum"], i - 1)
                    nc.scalar.activation(actT[:, :, 0:n2], psP[:, 768:1024].rearrange("p (j t) -> p j t", j=2)[:, :, 0:n2], ACT.Copy)
                    nc.scalar.activation(pos_all[:, i - 2], psP[:, 640:640 + NE], ACT.Copy).then_inc(S["actT_ready"], 1)
                if d1:
                    act.wait_ge(S["h2T_psum"], i)
                    nc.scalar.activation(h2T[:, :, 0:n1], psT[:].rearrange("p (k t) -> p k t", k=KC)[:, :, 0:n1], ACT.Copy).then_inc(S["h2T_ready"], 1)
                    act.wait_ge(S["router_psum"], i)
                    nc.scalar.activation(rt_s[0:n1], psP[0:n1, 512:512 + NE], ACT.Tanh, scale=0.5).then_inc(S["rtanh"], 1)
                if d0:
                    act.wait_ge(S["x2_ready"], i + 1)
                    nc.scalar.activation(sqB[0:n0], x2[0:n0, par], ACT.Square, scale=D ** -0.5, accum_out=ssqB[0:n0, 0:1]).then_inc(S["ssqB_ready"], 1)
                if d1:
                    act.wait_ge(S["shup_psum"], i)
                    nc.scalar.activation(sg[0:n1, 0], psP[0:n1, 0:F], ACT.Tanh, scale=0.5).then_inc(S["shtanh"], 1)
                if d2:
                    act.wait_ge(S["shd_psum"], i - 1)
                    if st is not None:
                        act.wait_ge(S2["sh_st"][par], st)
                    nc.scalar.activation(sho[0:n2, par], psS[0:n2], ACT.Copy).then_inc(S["sh_ready"], 1)

            step_b(0, 0, 0, d1=False, d2=False)
            step_b(1, 1, 0, d2=False)
            step_b(2, 0, 1)
            step_b(3, 1, 1)
            with act.Fori(2, NT // 2) as j:
                for s in range(2):
                    step_b(2 * j + s, s, j, st=16 * j - 16)
            step_b(NT, 0, 0, n0=TAIL, st=8 * NT - 16)
            step_b(NT + 1, 1, 0, d0=False, n1=TAIL, st=8 * NT - 16)
            step_b(NT + 2, 0, 0, d0=False, d1=False, n2=TAIL, st=8 * NT)

            def x_out(b, s):
                act.wait_ge(S["xgT_psum"], b + 1)
                nc.scalar.activation(xgT[:, s].rearrange("p k t -> p (k t)"), psT[:], ACT.Copy).then_inc(S["xgT_ready"], 1)

            def tanh_d(b, s):
                act.wait_ge(S["up_psum"], b + 1)
                nc.scalar.activation(sgD[:, s], psP[:, s * 512:s * 512 + F], ACT.Tanh, scale=0.5).then_inc(S["dtanh"], 1)

            def a_out(b):
                act.wait_ge(S["dactT_psum"], b + 1)
                nc.scalar.activation(actDT[:].rearrange("p j t -> p (j t)"), psQ[:, 0:F], ACT.Copy).then_inc(S["dactT_ready"], 1)

            def load_list(b, s, free=True):
                row = act.value_load(blkr[0:1, bass.ds(b, 1), 1:2], min_val=0, max_val=NE * LB)
                if free:
                    act.wait_ge(S["lent_used"], b - 1)
                act.dma_start(lent[:, s], list_d[bass.ds(row * P, P)]).then_inc(S2["lent_in"][s], 16)

            act.wait_ge(S["blkr_in"], 16)
            for par in range(2):
                act.wait_ge(S2["list_st"][par], 16 * TOPK * (NT // 2 + 1 - par))
            load_list(0, 0, free=False)
            load_list(1, 1, free=False)
            load_list(2, 0)
            load_list(3, 1)
            x_out(0, 0)
            tanh_d(0, 0)
            load_list(4, 0)
            x_out(1, 1)
            load_list(5, 1)
            last_pair = act.value_load(nblk[0:1, 0:1], min_val=0, max_val=NB // 2 - 1)
            a_out(0)
            tanh_d(1, 1)
            x_out(2, 0)
            with act.Fori(1, NB // 2) as j:
                with act.If(j < last_pair + 1):
                    for s in range(2):
                        a_out(2 * j + s - 1)
                        load_list(2 * j + s + 4, s)
                        x_out(2 * j + s + 1, 1 - s)
                        tanh_d(2 * j + s, s)
            a_out(last_pair * 2 + 1)

            def store_e(t, s, n=P):
                act.wait_ge(S["ye_ready"], t + 1)
                dst = y_prompt[0, bass.ds(t * P, P)] if n == P else y_sample.rearrange("b t d -> (b t) d")
                act.dma_start(dst, ye[0:n, s]).then_inc(S4["out_st"][s], 16)

            with act.Fori(0, NT // 4) as q:
                for s in range(4):
                    store_e(4 * q + s, s)
            store_e(NT, 0, TAIL)

        @block.vector
        def _(dve):
            V = nc.vector
            V.memset(gwt[:], 0.0).then_inc(S["gate_w_zero"], 1)
            dve.sem_inc(S["mod_bank_free"], 2)
            dve.wait_ge(S["c_tanh"], 1)
            V.scalar_tensor_tensor(cp_h[:], cp_h[:], 1.0, cp_t[:], ALU.add, ALU.mult)
            V.scalar_tensor_tensor(cs_h[:], cs_h[:], 1.0, cs_t[:], ALU.add, ALU.mult)
            dve.drain()
            for t in range(TS):
                V.tensor_scalar(csil[:, :, 0:TAIL].rearrange("p k (b t) -> p k b t", t=TS)[:, :, :, t],
                                cs_h[:].rearrange("p b k -> p k b"), 0.5, None, ALU.mult)
            V.tensor_scalar(csil[:, :, TAIL], cp_h[:], 0.5, None, ALU.mult).then_inc(S["csil_ready"], 1)
            dve.wait_ge(S["prm_psum"], 1)
            V.tensor_copy(prm[:], psP[:, 0:RC * 40].rearrange("p (c n) -> p c n", n=40)).then_inc(S["prm_ready"], 1)
            dve.drain()
            V.tensor_copy(gb[:, 0:RC], prm[:, :, 5])
            V.tensor_copy(gb[:, RC:2 * RC], prm[:, :, 6])
            V.tensor_scalar(lam8[:, :, 0], prm[:, :, 7], -1.0, None, ALU.mult)
            dve.drain()
            V.tensor_tensor(lam8[:, :, 1], lam8[:, :, 0], prm[:, :, 7], ALU.max).then_inc(S["lam_exp"], 1)
            dve.wait_ge(S["norms_in"], 48)
            for n in range(NCH):
                dve.wait_ge(S["ada_psum_ready"], n + 1)
                if n >= 2:
                    dve.wait_ge(S2["mod_st"][n % 2], 16 * (n // 2))
                sect = n * 512 // D
                src = psT[0:TAIL + 1, (n % 2) * 512:(n % 2) * 512 + 512]
                if sect in (1, 4):
                    V.tensor_tensor(modc[:, n % 2], src, adab[:, n * 512:(n + 1) * 512], ALU.add)
                    dve.drain()
                    V.scalar_tensor_tensor(modc[:, n % 2], modc[:, n % 2], 1.0,
                                           gmix[:, sect // 4, (n % 2) * 512:(n % 2) * 512 + 512], ALU.add,
                                           ALU.mult).then_inc(S["mod_row_ready"], 1)
                else:
                    V.tensor_tensor(modc[:, n % 2], src, adab[:, n * 512:(n + 1) * 512], ALU.add).then_inc(S["mod_row_ready"], 1)
                dve.drain().then_inc(S["mod_bank_free"], 1)
            dve.wait_ge(S["pid_ready"], 1)
            V.tensor_scalar(pid[:, 1:2], pid[:, 0:1], TS - 1, None, ALU.bitwise_and)
            V.tensor_scalar(pid[:, 2:3], pid[:, 0:1], 5, None, ALU.arith_shift_right)
            V.tensor_scalar(pid[:, 3:4], pid[:, 0:1], 2, None, ALU.arith_shift_right)
            for h in range(NH):
                V.memset(gtmp[:, 0, h:h + 1], -(2.0 ** (-8.0 * (h + 1) / NH)))
            dve.drain()
            V.tensor_scalar(pid[:, 4:5], pid[:, 3:4], GQ - 1, None, ALU.bitwise_and)
            V.tensor_copy(smc[:, 0:1], pid[:, 1:2])
            V.tensor_copy(smc[:, 10:11], pid[:, 2:3])
            dve.drain()
            V.tensor_copy(smc[:, 9:10], pid[:, 4:5])
            V.scalar_tensor_tensor(smc[:, 1:2], smc[:, 10:11], float(TS), smc[:, 0:1], ALU.mult, ALU.add)
            dve.drain()
            V.tensor_scalar(smc[:, 2:3], smc[:, 1:2], float(TS * NS // 2), None, ALU.add)
            for g in range(GQ):
                V.tensor_scalar(gsel[:, 0, g:g + 1], smc[:, 9:10], float(g), None, ALU.is_equal)
            dve.wait_ge(S["sink_in"], 16)
            dve.drain()
            gs = gsel[:, 0].unsqueeze(1).to_broadcast([P, NKV, GQ])
            for k, src in ((0, gtmp[:, 0]), (1, sink[:])):
                V.tensor_tensor(gtmp[:, k].rearrange("p (h g) -> p h g", h=NKV), src.rearrange("p (h g) -> p h g", h=NKV), gs, ALU.mult)
                dve.drain()
                V.tensor_reduce(smc[:, 3 + 2 * k:5 + 2 * k], gtmp[:, k].rearrange("p (h g) -> p h g", h=NKV), AX.X, ALU.add)
            dve.wait_ge(S["lam_one"], 1)
            e, z, w, s_ = lam8[:, :, 1], hs_t[:, :, 0], hs_t[:, :, 1], hs_t[:, :, 2]
            V.tensor_scalar(z, e, 2.0, None, ALU.add)
            dve.drain()
            V.reciprocal(z, z)
            dve.drain()
            V.tensor_tensor(z, z, e, ALU.mult)
            dve.drain()
            V.tensor_tensor(w, z, z, ALU.mult)
            V.memset(s_, 1.0 / 17.0)
            for c in (15.0, 13.0, 11.0, 9.0, 7.0, 5.0, 3.0, 1.0):
                dve.drain()
                V.tensor_tensor(s_, s_, w, ALU.mult)
                dve.drain()
                V.tensor_scalar(s_, s_, 1.0 / c, None, ALU.add)
            dve.drain()
            V.scalar_tensor_tensor(s_, s_, 2.0, z, ALU.mult, ALU.mult)
            V.tensor_scalar(lam8[:, :, 0], lam8[:, :, 0], 0.0, None, ALU.max)
            dve.drain()
            V.tensor_tensor(s_, s_, lam8[:, :, 0], ALU.add)
            dve.drain()
            V.tensor_scalar(lam8[:, :, 0], s_, -0.5 * LRU_C, None, ALU.mult)
            dve.wait_ge(S["init_st"], 48)
            V.memset(xrb[:, :, 0:HALO], 0.0)
            V.memset(hlast[:], 0.0)
            dve.drain()

            def h_of(i, par, n=P, first=False):
                dve.wait_ge(S["rstd_ready"], i + 1)
                if not first:
                    dve.wait_ge(S["hT_psum"], i)
                V.scalar_tensor_tensor(hrow[0:n], xin[0:n, par], rst[0:n, par:par + 1], modA[0:n, 1], ALU.mult, ALU.mult)
                dve.drain()
                V.tensor_tensor(hrow[0:n], hrow[0:n], modA[0:n, 0], ALU.add).then_inc(S["h_ready"], 1)

            def conv(i):
                dve.wait_ge(S["xr_ready"], i + 1)
                for c in range(RC):
                    V.tensor_scalar(u[:, c], xrb[:, c, 0:P], prm[:, c, 0:1], prm[:, c, 4:5], ALU.mult, ALU.add)
                for t in range(1, HALO + 1):
                    dve.drain()
                    for c in range(RC):
                        V.scalar_tensor_tensor(u[:, c], xrb[:, c, t:t + P], prm[:, c, t:t + 1], u[:, c], ALU.mult, ALU.add)
                dve.drain()
                V.tensor_copy(xrb[:, :, 0:HALO], xrb[:, :, P:P + HALO])
                dve.drain().then_inc(S["conv_ready"], 1)

            def conv_tail(i):
                def view(ap, t0, n):
                    return ap[:, 0:NS * (TS + HALO)].rearrange("p (b t) -> p b t", b=NS)[:, :, t0:t0 + n]
                dve.wait_ge(S["xr_ready"], i + 1)
                uv = [u[:, c, 0:TAIL].rearrange("p (b t) -> p b t", b=NS) for c in range(RC)]
                for c in range(RC):
                    V.tensor_copy(view(xrb[:, c], 0, HALO), prm[:, c, 8:8 + NS * HALO].rearrange("p (b j) -> p b j", b=NS))
                dve.drain()
                for c in range(RC):
                    V.tensor_scalar(uv[c], view(xrb[:, c], 0, TS), prm[:, c, 0:1], prm[:, c, 4:5], ALU.mult, ALU.add)
                for t in range(1, HALO + 1):
                    dve.drain()
                    for c in range(RC):
                        V.scalar_tensor_tensor(uv[c], view(xrb[:, c], t, TS), prm[:, c, t:t + 1], uv[c], ALU.mult, ALU.add)
                for c in range(RC):
                    V.tensor_copy(stt[:, c, HALO + 1:HALO + 1 + NS * HALO].rearrange("p (b j) -> p b j", b=NS), view(xrb[:, c], TS, HALO))
                dve.drain().then_inc(S["conv_ready"], 1)

            def scores(n, h, first=False):
                dve.wait_ge(S["s_psum"], 2 * n + h + 1)
                hs = slice(GQ * h, GQ * h + GQ)
                s_in = psS[:].rearrange("p (g j) -> p g j", g=GQ)
                if first:
                    V.memset(sc[:, h, :, 0:P], NEG)
                    V.scalar_tensor_tensor(sc[:, h, :, P:], s_in[:, :, P:], HD ** -0.5, bias[:, hs, P:], ALU.mult, ALU.add)
                else:
                    V.scalar_tensor_tensor(sc[:, h], s_in, HD ** -0.5, bias[:, hs], ALU.mult, ALU.add)
                dve.drain().then_inc(S["s_read"], 1)
                V.tensor_reduce(mx[:, h, 0], sc[:, h], AX.X, ALU.max)
                dve.drain()
                V.tensor_tensor(mx[:, h, 0], mx[:, h, 0], sink[:, hs], ALU.max)
                dve.drain()
                V.tensor_scalar(mx[:, h, 1], mx[:, h, 0], -1.0, None, ALU.mult)
                V.tensor_tensor(mx[:, h, 2], sink[:, hs], mx[:, h, 0], ALU.subtract)
                dve.drain().then_inc(S["m_ready"], 1)

            def o_out(n, h):
                dve.wait_ge(S["o_psum"], 2 * n + h + 1)
                V.tensor_tensor(mx[:, h, 3], esum[:, h, 0], esum[:, h, 1], ALU.add)
                dve.drain()
                V.reciprocal(mx[:, h, 3], mx[:, h, 3])
                dve.drain()
                V.tensor_tensor(orow[:, 256 * h:256 * h + 256].rearrange("p (g d) -> p g d", g=GQ),
                                psQ[:, 768:1024].rearrange("p (g d) -> p g d", g=GQ), bc(mx[:, h, 3], HD),
                                ALU.mult).then_inc(S["o_ready"], 1)

            def step(i, par, proj=True, att=True, nxt=True, first=False, n=P, n_next=P):
                a = i - 1
                tail = n != P
                if proj:
                    (conv_tail if tail else conv)(i)
                if att:
                    if not first:
                        dve.wait_ge(S["o_psum"], 2 * a)
                    V.tensor_copy(vb[:, 1 - par], qkv[:, QD + KVD:]).then_inc(S["v_ready"], 1)
                    scores(a, 0, first)
                if nxt:
                    if n_next != P:
                        dve.wait_ge(S["tailmod_in"], 16)
                    h_of(i + 1, 1 - par, n_next)
                if proj:
                    dve.wait_ge(S["gates_psum"], i + 1)
                    V.tensor_tensor(gts[:, :, 0:n], psP[:].rearrange("p (c t) -> p c t", t=P)[:, :, 0:n], bc(gb[:], n),
                                    ALU.add).then_inc(S["gates_sum"], 1)
                    dve.wait_ge(S["y_ready"], i + 1)
                    V.tensor_scalar(sq_t[:, :, 0:n], sq_t[:, :, 0:n], GELU_A, 1.0, ALU.mult, ALU.add)
                    dve.drain()
                    V.tensor_tensor(sq_t[:, :, 0:n], sq_t[:, :, 0:n], y_t[:, :, 0:n], ALU.mult).then_inc(S["gelu_in"], 1)
                    dve.wait_ge(S["gates_tanh"], i + 1)
                    V.scalar_tensor_tensor(b_t[:, :, 0:n], gts[:, 0:RC, 0:n], 1.0, bc(lam8[:, :, 0], n), ALU.add,
                                           ALU.mult).then_inc(S["loga_ready"], 1)
                    V.scalar_tensor_tensor(gts[:, RC:, 0:n], gts[:, RC:, 0:n], 1.0, u[:, :, 0:n], ALU.add, ALU.mult)
                if att:
                    scores(a, 1, first)
                    o_out(a, 0)
                if proj:
                    dve.wait_ge(S["a_ready"], i + 1)
                    V.tensor_scalar(b_t[:, :, 0:n], th_t[:, :, 0:n], -1.0, 1.0, ALU.mult, ALU.add)
                    dve.drain()
                    V.reciprocal(b_t[:, :, 0:n], b_t[:, :, 0:n])
                    dve.drain()
                    V.scalar_tensor_tensor(b_t[:, :, 0:n], th_t[:, :, 0:n], -2.0, b_t[:, :, 0:n], ALU.mult,
                                           ALU.mult).then_inc(S["b2_ready"], 1)
                    dve.wait_ge(S["gelu_tanh"], i + 1)
                    V.scalar_tensor_tensor(sq_t[:, :, 0:n], sq_t[:, :, 0:n], 1.0, y_t[:, :, 0:n], ALU.add, ALU.mult)
                    dve.wait_ge(S["bsqrt_ready"], i + 1)
                    V.scalar_tensor_tensor(b_t[:, :, 0:n], gts[:, RC:, 0:n], 0.5, b_t[:, :, 0:n], ALU.mult, ALU.mult)
                    dve.drain()
                    if tail:
                        at_, bt_, ht_ = (x[:, :, 0:TAIL].rearrange("p c (b t) -> p c b t", b=NS) for x in (a_t, b_t, hs_t))
                        for t in range(TS):
                            prev = prm[:, :, 8 + NS * HALO:8 + NS * HALO + NS] if t == 0 else ht_[:, :, :, t - 1]
                            V.tensor_tensor(ht_[:, :, :, t], at_[:, :, :, t], prev, ALU.mult)
                            dve.drain()
                            V.tensor_tensor(ht_[:, :, :, t], ht_[:, :, :, t], bt_[:, :, :, t], ALU.add)
                            dve.drain()
                        V.tensor_copy(stt[:, :, HALO + 1 + NS * HALO:], ht_[:, :, :, TS - 1])
                    else:
                        for c in range(RC):
                            V.tensor_tensor_scan(hs_t[:, c], a_t[:, c], b_t[:, c], hlast[:, c], ALU.mult, ALU.add)
                        dve.drain()
                        V.tensor_copy(hlast[:], hs_t[:, :, P - 1:P])
                    if att:
                        dve.wait_ge(S["outr_st"], 16 * i)
                    V.scalar_tensor_tensor(outr[:, :, 0:n], sq_t[:, :, 0:n], 0.5, hs_t[:, :, 0:n], ALU.mult, ALU.mult)
                    dve.drain().then_inc(S["outr_ready"], 1)
                if att:
                    o_out(a, 1)
                if proj:
                    dve.wait_ge(S["qkv_ready"], i + 1)
                    if att:
                        dve.wait_ge(S["qkT_psum"], i)
                    if tail:
                        dve.wait_ge(S["kwin_st"], 32)
                    q3 = qkv[0:n, 0:QD + KVD].rearrange("p (h d) -> p h d", d=HD)
                    n3 = qn[0:n].rearrange("p (h d) -> p h d", d=HD)
                    V.scalar_tensor_tensor(qn[0:n], qkv[0:n, 0:QD + KVD], 1.0 / HD, qkv[0:n, 0:QD + KVD], ALU.mult, ALU.mult)
                    dve.drain()
                    V.tensor_reduce(ss10[0:n, 0:NH + NKV], n3, AX.X, ALU.add).then_inc(S["ss10_ready"], 1)
                    dve.wait_ge(S["r10_ready"], i + 1)
                    V.tensor_tensor(q3, q3, bc(r10[0:n, 0:NH + NKV], HD), ALU.mult)
                    dve.drain()
                    for v in range(NKV):
                        V.tensor_tensor(qn[0:n, 0:QD].rearrange("p (g v d) -> p v g d", v=NKV, g=GQ)[:, v],
                                        qkv[0:n, v * GQ * HD:(v + 1) * GQ * HD].rearrange("p (g d) -> p g d", g=GQ),
                                        qw[0:n, v * GQ * HD:(v + 1) * GQ * HD].rearrange("p (g d) -> p g d", g=GQ), ALU.mult)
                    V.tensor_tensor(qn[0:n, QD:], qkv[0:n, QD:QD + KVD], qw[0:n, QD:], ALU.mult).then_inc(S["qn_ready"], 1)

            dve.wait_ge(S["modA_in"], 16)
            dve.wait_ge(S["sink_in"], 16)
            dve.wait_ge(S["bias_ready"], 1)
            dve.wait_ge(S["qw_in"], 16 * (NH + NKV))
            h_of(0, 0, first=True)
            step(0, 0, att=False)
            step(1, 1, first=True)
            with dve.Fori(1, NT // 2 - 1) as j:
                for s in range(2):
                    step(2 * j + s, s)
            step(NT - 2, 0)
            step(NT - 1, 1, n_next=TAIL)
            V.tensor_copy(stt[:, :, 0:HALO], xrb[:, :, 0:HALO])
            V.tensor_copy(stt[:, :, HALO:HALO + 1], hlast[:])
            dve.drain()
            step(NT, 0, nxt=False, n=TAIL)
            dve.wait_ge(S["smp_in"], 32)
            V.memset(qTs[:], 0.0).then_inc(S["smp_q0"], 1)
            V.tensor_scalar(distS[:, :, 0:P], jdist[:, 0:P].unsqueeze(1).to_broadcast([P, 2, P]), smc[:, 0:1], None, ALU.add)
            for half in range(2):
                V.tensor_scalar(distS[:, half, P:], jdist[:, P:], smc[:, 1 + half:2 + half], None, ALU.add)
            dve.drain()
            V.tensor_scalar(penS[:, :, 0:P], distS[:, :, 0:P], float(P), NEG, ALU.is_gt, ALU.mult)
            V.tensor_scalar(penS[:, :, P:], distS[:, :, P:], smc[:, 0:1], NEG, ALU.is_gt, ALU.mult)
            V.tensor_scalar(penT[:], distS[:], 0.0, NEG, ALU.is_lt, ALU.mult)
            dve.drain()
            V.tensor_tensor(penS[:], penS[:], penT[:], ALU.add)
            dve.drain()
            for h in range(NKV):
                V.scalar_tensor_tensor(biasS[:, :, h], distS[:], smc[:, 3 + h:4 + h], penS[:], ALU.mult, ALU.add)
            dve.wait_ge(S["small_psum"], 1)
            V.tensor_copy(stt_r[:], psQ[0:36, 0:512]).then_inc(S["small_ready"], 1)
            dve.drain()
            dve.wait_ge(S["smp_s"], 1)
            sS = psS[:].rearrange("p (h a j) -> p a h j", a=2, h=NKV)[:, :, :, 0:P + TAIL]
            for half in range(2):
                V.scalar_tensor_tensor(scS[:, half], sS[:, half], HD ** -0.5, biasS[:, half], ALU.mult, ALU.add)
            dve.drain()
            V.tensor_reduce(mxS[:, 0], scS[:], AX.X, ALU.max)
            dve.drain()
            snk = smc[:, 5:7].unsqueeze(1).to_broadcast([P, 2, NKV])
            V.tensor_tensor(mxS[:, 0], mxS[:, 0], snk, ALU.max)
            dve.drain()
            V.tensor_scalar(mxS[:, 1], mxS[:, 0], -1.0, None, ALU.mult)
            V.tensor_tensor(mxS[:, 2], snk, mxS[:, 0], ALU.subtract)
            dve.drain().then_inc(S["smp_m"], 1)
            dve.wait_ge(S["smp_p"], 1)
            V.tensor_tensor(mxS[:, 5], mxS[:, 3], mxS[:, 4], ALU.add)
            dve.drain()
            V.reciprocal(mxS[:, 5], mxS[:, 5])
            dve.drain()
            dve.wait_ge(S["smp_o"], 1)
            V.tensor_tensor(orowS[:].rearrange("p a (h d) -> p (a h) d", h=NKV), psQ[:, 768:1024].rearrange("p (c d) -> p c d", c=2 * NKV),
                            bc(mxS[:, 5].rearrange("p a h -> p (a h)"), HD), ALU.mult).then_inc(S["smp_or"], 1)

            dve.wait_ge(S["modB_in"], 16)
            dve.wait_ge(S["rbias_in"], 16)
            dve.wait_ge(S["iota_ready"], 1)
            V.memset(mrun[:], 0.0)
            V.memset(msk_all[:, NT], 0.0)
            dve.drain().then_inc(S["mrun_ready"], 1)

            def x2_of(i, par, half, n=P, st=None):
                dve.wait_ge(S["mixed_psum"], i + 1)
                dve.wait_ge(S2["xB_in"][par], 16 * half + 16)
                if st is not None:
                    dve.wait_ge(S2["x2_st"][par], st)
                V.tensor_tensor(x2[0:n, par], psQ[0:n], modB[0:n, 0], ALU.mult)
                dve.drain()
                V.tensor_tensor(x2[0:n, par], x2[0:n, par], xb[0:n, par], ALU.add)
                dve.drain().then_inc(S["x2_ready"], 1)

            def h2_of(i, par, half, n=P, first=False):
                dve.wait_ge(S["rstdB_ready"], i + 1)
                if not first:
                    dve.wait_ge(S2["h2_st"][1 - par], 16 * (half + par))
                    dve.wait_ge(S["h2T_psum"], i)
                V.scalar_tensor_tensor(h2[0:n], x2[0:n, par], ssqB[0:n, 1:2], modB[0:n, 2], ALU.mult, ALU.mult)
                dve.drain()
                V.tensor_tensor(h2[0:n], h2[0:n], modB[0:n, 1], ALU.add).then_inc(S["h2_ready"], 1)

            def shared_act(i, n=P):
                dve.wait_ge(S["shtanh"], i + 1)
                V.scalar_tensor_tensor(sg[0:n, 1], sg[0:n, 0], 1.0, psP[0:n, 0:F], ALU.add, ALU.mult)
                dve.drain()
                V.scalar_tensor_tensor(actr[0:n], sg[0:n, 1], 0.5, psP[0:n, F:2 * F], ALU.mult, ALU.mult).then_inc(S["act_ready"], 1)

            def route(t, n=P):
                dve.wait_ge(S["rtanh"], t + 1)
                V.tensor_scalar(rt_s[0:n], rt_s[0:n], 0.5, 0.5, ALU.mult, ALU.add)
                dve.drain()
                V.tensor_tensor(rt_b[0:n], rt_s[0:n], rbias[0:n], ALU.add)
                dve.drain()
                for g in range(NG):
                    V.max(rt_8[0:n, g], rt_b[0:n, g * GE:(g + 1) * GE])
                dve.drain()
                V.tensor_tensor(rt_g[0:n, 0], rt_8[0:n, :, 0], rt_8[0:n, :, 1], ALU.add)
                dve.drain()
                V.max(rt_g[0:n, 1], rt_g[0:n, 0])
                dve.drain()
                V.max_index(rt_u[0:n, 0], rt_g[0:n, 1], rt_g[0:n, 0])
                dve.drain()
                V.tensor_copy(rt_g[0:n, 2], rt_u[0:n, 0])
                dve.drain()
                g4 = rt_t[0:n, 0, 0:NG * TG].rearrange("p (g k) -> p g k", g=NG)
                V.tensor_tensor(g4, bc(iota[0:n, 0:NG], TG), rt_g[0:n, 2, 0:TG].unsqueeze(1).to_broadcast([n, NG, TG]), ALU.is_equal)
                dve.drain()
                V.tensor_reduce(rt_g[0:n, 3], g4, AX.X, ALU.add)
                dve.drain()
                V.tensor_scalar(rt_g[0:n, 0], rt_g[0:n, 3], -1.0, -NEG, ALU.add, ALU.mult)
                b3 = rt_b[0:n].rearrange("p (g e) -> p g e", g=NG)
                m3 = rt_m[0:n].rearrange("p (g e) -> p g e", g=NG)
                V.tensor_tensor(m3, b3, bc(rt_g[0:n, 3], GE), ALU.mult)
                dve.drain()
                V.tensor_tensor(m3, m3, bc(rt_g[0:n, 0], GE), ALU.add)
                dve.drain()
                V.max(rt_8[0:n, 0], rt_m[0:n])
                dve.drain()
                V.max_index(rt_u[0:n, 1], rt_8[0:n, 0], rt_m[0:n])
                dve.drain()
                V.tensor_copy(idxf[0:n], rt_u[0:n, 1])
                dve.drain()
                V.tensor_tensor(rt_oh[0:n], iota[0:n].unsqueeze(1).to_broadcast([n, TOPK, NE]), bc(idxf[0:n, 0:TOPK], NE), ALU.is_equal)
                dve.drain()
                V.tensor_tensor(rt_t[0:n], rt_oh[0:n], rt_s[0:n].unsqueeze(1).to_broadcast([n, TOPK, NE]), ALU.mult)
                V.tensor_reduce(msk_all[0:n, t], rt_oh[0:n].rearrange("p k e -> p e k"), AX.X, ALU.add).then_inc(S["msk_ready"], 1)
                dve.drain()
                V.tensor_reduce(wgt[0:n, 0:TOPK], rt_t[0:n], AX.X, ALU.add)
                dve.drain()
                V.tensor_reduce(rt_g[0:n, 1, 0:1], wgt[0:n, 0:TOPK], AX.X, ALU.add)
                dve.drain()
                V.reciprocal(rt_g[0:n, 1, 1:2], rt_g[0:n, 1, 0:1])
                dve.drain()
                V.tensor_scalar(wgt[0:n, 0:TOPK], wgt[0:n, 0:TOPK], rt_g[0:n, 1, 1:2], ROUTE_SCALE, ALU.mult, ALU.mult)
                dve.drain()

            def add_mask(t):
                dve.wait_ge(S["pos_psum"], t + 1)
                V.tensor_tensor(mrun[:], mrun[:], msk_all[:, t], ALU.add)
                dve.drain().then_inc(S["mrun_ready"], 1)

            def entries(t, par, st, n=P):
                dve.wait_ge(S["actT_ready"], t + 1)
                V.tensor_tensor(rt_t[0:n], rt_oh[0:n], pos_all[0:n, t].unsqueeze(1).to_broadcast([n, TOPK, NE]), ALU.mult)
                dve.drain()
                if st is not None:
                    dve.wait_ge(S2["list_st"][par], st)
                V.tensor_reduce(posk[0:n, par, 0, 0:TOPK], rt_t[0:n], AX.X, ALU.add)
                V.tensor_scalar(posk[0:n, par, 1, 0:TOPK], idxf[0:n, 0:TOPK], float(LB * P), None, ALU.mult)
                V.tensor_copy(entry[0:n, par, :, 0], tokf[0:n, bass.ds(t, 1)].to_broadcast([n, TOPK]))
                V.tensor_copy(entry[0:n, par, :, 1], wgt[0:n, 0:TOPK])
                dve.drain().then_inc(S["entry_ready"], 1)

            def step_b(i, par, half, d0=True, d1=True, d2=True, n0=P, n1=P, n2=P, st=None, lst=None):
                if d2:
                    add_mask(i - 2)
                if d0:
                    x2_of(i, par, half, n0, st)
                if d2:
                    entries(i - 2, par, lst, n2)
                if d1:
                    shared_act(i - 1, n1)
                if d0:
                    h2_of(i, par, half, n0, first=isinstance(i, int) and i == 0)
                if d1:
                    route(i - 1, n1)

            LT = 16 * TOPK
            step_b(0, 0, 0, d1=False, d2=False)
            step_b(1, 1, 0, d2=False)
            step_b(2, 0, 1, st=16)
            step_b(3, 1, 1, st=16)
            with dve.Fori(2, NT // 2) as j:
                for s in range(2):
                    step_b(2 * j + s, s, j, st=16 * j, lst=LT * j - LT)
            dve.wait_ge(S["tailmodB_in"], 16)
            step_b(NT, 0, NT // 2, n0=TAIL, st=8 * NT, lst=LT * (NT // 2 - 1))
            step_b(NT + 1, 1, 0, d0=False, n1=TAIL, lst=LT * (NT // 2 - 1))
            step_b(NT + 2, 0, 0, d0=False, d1=False, n2=TAIL, lst=LT * (NT // 2))

            dve.wait_ge(S["cnt_psum"], 1)
            V.tensor_scalar(cnt[:, 0], psP[:, 0:NE], float(P - 1), None, ALU.add)
            dve.drain()
            V.tensor_copy(cnti[:, 0], cnt[:, 0])
            dve.drain()
            V.tensor_scalar(cnti[:, 1], cnti[:, 0], 7, None, ALU.arith_shift_right)
            dve.drain()
            V.tensor_copy(cnt[:, 1], cnti[:, 1])
            dve.drain()
            V.tensor_tensor_scan(cnt[:, 2], ones[:, 0:NE], cnt[:, 1], 0.0, ALU.mult, ALU.add)
            dve.drain()
            V.tensor_tensor(cnt[:, 3], cnt[:, 2], cnt[:, 1], ALU.subtract)
            V.tensor_scalar(cnt[:, 5], iota[:], float(LB), None, ALU.mult)
            dve.drain()
            for h in range(2):
                V.tensor_scalar(blkf[:, h], cnt[:, 2], iotp[:, h:h + 1], None, ALU.is_le)
                V.tensor_scalar(blkf[:, 2 + h], cnt[:, 3], iotp[:, h:h + 1], None, ALU.is_le)
            V.tensor_tensor(cnt[:, 5], cnt[:, 5], cnt[:, 3], ALU.subtract)
            V.tensor_scalar(cnt[:, 0], cnt[:, 3], 1.0, None, ALU.add)
            V.tensor_scalar(cnt[0:1, 4, 0:1], cnt[0:1, 2, NE - 1:NE], -1.0, None, ALU.add)
            dve.drain()
            V.tensor_copy(strt[:], cnt[0:1, 0])
            V.tensor_copy(nblk[0:1, 1:2], cnt[0:1, 4, 0:1])
            V.tensor_tensor(blkf[:, 2:4], blkf[:, 2:4], blkf[:, 0:2], ALU.subtract)
            V.tensor_reduce(bsum[:, 0], blkf[:, 0:2], AX.X, ALU.add)
            dve.drain()
            V.tensor_scalar(nblk[0:1, 0:1], nblk[0:1, 1:2], 1, None, ALU.arith_shift_right)
            V.tensor_scalar(bsum[:, 0], bsum[:, 0], float(NE - 1), None, ALU.min)
            V.tensor_tensor(blkf[:, 2:4], blkf[:, 2:4], cnt[:, 5].unsqueeze(1).to_broadcast([P, 2, NE]), ALU.mult)
            V.tensor_scalar(bsum[:, 1], iotp[:], -1.0, float(NE * LB), ALU.mult, ALU.add)
            dve.drain()
            V.tensor_reduce(bsum[:, 2], blkf[:, 2:4], AX.X, ALU.add)
            V.tensor_tensor(bsum[:, 1], bsum[:, 1], blkf[:, 0:2, NE - 1], ALU.mult)
            dve.drain()
            V.tensor_tensor(bsum[:, 2], bsum[:, 2], iotp[:], ALU.add)
            dve.drain()
            V.tensor_tensor(bsum[:, 2], bsum[:, 2], bsum[:, 1], ALU.add)
            V.tensor_copy(blki[:, :, 0], bsum[:, 0])
            dve.drain()
            V.tensor_copy(blki[:, :, 1], bsum[:, 2])
            dve.drain().then_inc(S["blk_ready"], 1)

            def act_d(b, s, free=True):
                dve.wait_ge(S["dtanh"], b + 1)
                if free:
                    dve.wait_ge(S["dactT_psum"], b)
                V.scalar_tensor_tensor(sgD[:, s], sgD[:, s], 1.0, psP[:, s * 512:s * 512 + F], ALU.add, ALU.mult)
                dve.drain()
                V.scalar_tensor_tensor(actD[:], sgD[:, s], 0.5, psP[:, s * 512 + F:s * 512 + 2 * F], ALU.mult, ALU.mult).then_inc(S["dact_ready"], 1)

            def y_out(b, s, stored=None):
                dve.wait_ge(S["down_psum"], b + 2)
                if stored is not None:
                    dve.wait_ge(S["add_st"], stored)
                V.tensor_scalar(ysb[:, s], psS[:], w_all[:, bass.ds(b, 1)], None, ALU.mult).then_inc(S["ysb_ready"], 1)

            act_d(0, 0, free=False)
            act_d(1, 1)
            y_out(0, 0)
            dve.wait_ge(S["blkr_in"], 16)
            last_pair = dve.value_load(nblk[0:1, 0:1], min_val=0, max_val=NB // 2 - 1)
            with dve.If(last_pair > 0):
                act_d(2, 0)
                y_out(1, 1)
                act_d(3, 1)
                y_out(2, 0, 16)
            with dve.Fori(2, NB // 2) as j:
                with dve.If(j < last_pair + 1):
                    act_d(2 * j, 0)
                    y_out(2 * j - 1, 1, 32 * j - 32)
                    act_d(2 * j + 1, 1)
                    y_out(2 * j, 0, 32 * j - 16)
            y_out(last_pair * 2 + 1, 1, last_pair * 32)

            def out_e(t, s, q, n=P, stored=True, g=0):
                dve.wait_ge(S4["xe_in"][s], 32 * q + 32)
                V.tensor_tensor(acc[0:n, s], acc[0:n, s], g2b[0:n, g], ALU.mult)
                dve.drain()
                if stored:
                    dve.wait_ge(S4["out_st"][s], 16 * q)
                V.tensor_tensor(ye[0:n, s], acc[0:n, s], xe[0:n, s], ALU.add).then_inc(S["ye_ready"], 1)

            dve.wait_ge(S["g2_in"], 32)
            for s in range(4):
                out_e(s, s, 0, stored=False)
            with dve.Fori(1, NT // 4) as q:
                for s in range(4):
                    out_e(4 * q + s, s, q)
            out_e(NT, 0, NT // 4, n=TAIL, g=1)

        @block.tensor
        def _(pe):
            T = nc.tensor
            pe.wait_ge(S["const_ready"], 1)
            pe.wait_ge(S["csil_ready"], 1)
            pe.wait_ge(S["prm_in"], 16 * 7)
            for c in range(RC):
                last = T.transpose(psP[:, c * 40:(c + 1) * 40], prm_r[:, c * P:(c + 1) * P], ident[0:40, 0:40])
            last.then_inc(S["prm_psum"], 1)
            with pe.Fori(0, NCH // 2) as j:
                for s in range(2):
                    pe.wait_ge(S2["ada_in"][s], 16 * j + 16)
                    pe.wait_ge(S["mod_bank_free"], 2 * j + s + 1)
                    for k in range(KC):
                        last = T.matmul(psT[0:TAIL + 1, s * 512:s * 512 + 512], csil[:, k], ada_wt[:, s, k], start=k == 0, stop=k == KC - 1)
                    last.then_inc(S["ada_psum_ready"], 1)
            pe.wait_ge(S["gate_w_in"], 64)
            pe.sem_inc(S["down_psum"], 1)

            def h_transpose(i, n=P, first=False):
                pe.wait_ge(S["h_ready"], i + 1)
                if not first:
                    pe.wait_ge(S["hT_ready"], i)
                hv = hrow[0:n].rearrange("p (m k) -> p k m", k=KC)
                for k in range(KC):
                    last = T.transpose(psT[:, k * P:k * P + n], hv[:, k], ident[0:n, 0:n])
                last.then_inc(S["hT_psum"], 1)

            def branch(i, bank, col, n, done, chunks=range(RC)):
                for c in chunks:
                    for k in range(KC):
                        last = T.matmul(psP[:, bank * 512 + c * P:bank * 512 + c * P + n], win[:, k, col + c * P:col + (c + 1) * P],
                                        hT[:, k, 0:n], start=k == 0, stop=k == KC - 1)
                if done is not None:
                    last.then_inc(done, 1)

            def qkv_part(i, c0, c1, n, done):
                for k in range(KC):
                    last = T.matmul(psQ[0:n, c0:c1], hT[:, k, 0:n], win[:, k, 2 * R + c0:2 * R + c1], start=k == 0, stop=k == KC - 1)
                last.then_inc(done, 1)

            def qk_transpose(a, n=P):
                pe.wait_ge(S["qn_ready"], a + 1)
                for g in range(GQ):
                    T.transpose(psT[:, g * P:g * P + n], qn[0:n, g * P:(g + 1) * P], ident[0:n, 0:n])
                T.transpose(psT[:, 4 * P:4 * P + n], qn[0:n, QD:], ident[0:n, 0:n]).then_inc(S["qkT_psum"], 1)

            def qk(n, h, cur, first=False):
                rows = slice(HD * h, HD * h + HD)
                for g in range(GQ):
                    for where, slot in ((0, 1 - cur), (1, cur)):
                        if first and where == 0:
                            continue
                        last = T.matmul(psS[:, g * 256 + where * P:g * 256 + where * P + P], qT[rows, g], kT[rows, slot], start=True, stop=True)
                last.then_inc(S["s_psum"], 1)

            def p_transpose(n, h):
                pe.wait_ge(S["p_ready"], 2 * n + h + 1)
                for g in range(GQ):
                    for b in range(2):
                        last = T.transpose(psT[:, (2 * g + b) * P:(2 * g + b + 1) * P], sc[:, h, g, b * P:(b + 1) * P], ident[:])
                last.then_inc(S["pT_psum"], 1)

            def pv(n, h, cur, first=False):
                pe.wait_ge(S["pT_ready"], 2 * n + h + 1)
                for g in range(GQ):
                    for b, slot in ((0, 1 - cur), (1, cur)):
                        if first and b == 0:
                            continue
                        last = T.matmul(psQ[:, 768 + g * HD:768 + (g + 1) * HD], PT[:, g, b], vb[:, slot, HD * h:HD * h + HD],
                                        start=b == 0 or first, stop=b == 1)
                last.then_inc(S["o_psum"], 1)

            def o_transpose(n):
                pe.wait_ge(S["o_ready"], 2 * n + 2)
                for c in range(RC):
                    last = T.transpose(psS[:, c * P:(c + 1) * P], orow[:, c * P:(c + 1) * P], ident[:])
                last.then_inc(S["oT_psum"], 1)

            def step(i, par, proj=True, att=True, nxt=True, first=False, n=P, n_next=P):
                a, cur = i - 1, 1 - par
                if proj:
                    pe.wait_ge(S["hT_ready"], i + 1)
                    if att:
                        pe.wait_ge(S["gates_sum"], i)
                    branch(i, 0, 0, n, S["xr_psum"])
                if att:
                    qk_transpose(a)
                if proj:
                    branch(i, 1, R, n, None, range(0, 2))
                if att:
                    pe.wait_ge(S["qkT_ready"], a + 1)
                    if not first:
                        pe.wait_ge(S["oT_ready"], a)
                    qk(a, 0, cur, first)
                if proj:
                    branch(i, 1, R, n, S["yr_psum"], range(2, 4))
                    pe.wait_ge(S["conv_ready"], i + 1)
                    pe.wait_ge(S["xr_ready"], i + 1)
                    pe.wait_ge(S["y_ready"], i + 1)
                    for g in range(2):
                        for c in range(RC):
                            last = T.matmul(psP[:, (g * RC + c) * P:(g * RC + c) * P + n], gwt[:, g, c], u[:, c, 0:n], start=True, stop=True)
                    last.then_inc(S["gates_psum"], 1)
                if att:
                    p_transpose(a, 0)
                    pe.wait_ge(S["s_read"], 2 * a + 1)
                    qk(a, 1, cur, first)
                    pe.wait_ge(S["v_ready"], a + 1)
                    if not first:
                        pe.wait_ge(S["o_ready"], 2 * a)
                    pv(a, 0, cur, first)
                if proj:
                    if att:
                        pe.wait_ge(S["qkv_ready"], i)
                    qkv_part(i, 0, 512, n, S["qkv1_psum"])
                if att:
                    pe.wait_ge(S["pT_ready"], 2 * a + 1)
                    p_transpose(a, 1)
                if proj:
                    if att:
                        pe.wait_ge(S["o_ready"], 2 * a + 1)
                    qkv_part(i, 512, QKV, n, S["qkv2_psum"])
                if nxt:
                    if att:
                        pe.wait_ge(S["pT_ready"], 2 * a + 2)
                    h_transpose(i + 1, n_next)
                if att:
                    pe.wait_ge(S["o_ready"], 2 * a + 1)
                    if proj:
                        pe.wait_ge(S["qkv_ready"], i + 1)
                    pv(a, 1, cur, first)
                    o_transpose(a)

            pe.wait_ge(S["prm_ready"], 1)
            pe.wait_ge(S["mod_row_ready"], NCH)
            h_transpose(0, first=True)
            pe.wait_ge(S["win_in"], 16)
            step(0, 0, att=False)
            step(1, 1, first=True)
            with pe.Fori(1, NT // 2 - 1) as j:
                for s in range(2):
                    step(2 * j + s, s)
            step(NT - 2, 0)
            step(NT - 1, 1, n_next=TAIL)
            step(NT, 0, nxt=False, n=TAIL)
            qk_transpose(NT, TAIL)
            pe.wait_ge(S["outr_ready"], NT + 1)
            pe.wait_ge(S["qkv_ready"], NT + 1)
            for c in range(RC):
                last = T.transpose(psQ[0:36, c * P:(c + 1) * P], stt[:, c], ident[:])
            last.then_inc(S["small_psum"], 1)
            pe.wait_ge(S["smp_in"], 32)
            pe.wait_ge(S["gates_sum"], NT + 1)
            for b in range(NS):
                last = T.transpose(psP[:, b * P:(b + 1) * P], ck8[:, b], ident[:])
            last.then_inc(S["ckT_psum"], 1)
            pe.wait_ge(S["qkT_ready"], NT + 1)
            pe.wait_ge(S["ckT_ready"], 1)
            pe.wait_ge(S["oT_ready"], NT)
            for b in range(NS):
                half, q = divmod(b, 4)
                for h in range(NKV):
                    rows, col = slice(HD * h, HD * h + HD), h * 512 + half * 256
                    T.matmul(psS[32 * q:32 * q + 32, col:col + P], qTs[rows, b], kT8[rows, b], start=True, stop=True)
                    last = T.matmul(psS[32 * q:32 * q + 32, col + P:col + P + TAIL], qTs[rows, b], kTn[rows], start=True, stop=True)
            last.then_inc(S["smp_s"], 1)
            pe.wait_ge(S["smp_p"], 1)
            for c in range(2 * NKV):
                half, h = divmod(c, NKV)
                T.transpose(psT[:, c * P:(c + 1) * P], scS[:, half, h, 0:P], ident[:])
                last = T.transpose(psT[0:TAIL, 512 + c * P:512 + (c + 1) * P], scS[:, half, h, P:], ident[:])
            last.then_inc(S["smp_pT"], 1)
            pe.wait_ge(S["smp_pTo"], 1)
            pe.wait_ge(S["o_ready"], 2 * NT)
            for b in range(NS):
                half, q = divmod(b, 4)
                for h in range(NKV):
                    c = half * NKV + h
                    out = psQ[32 * q:32 * q + 32, 768 + c * HD:768 + (c + 1) * HD]
                    T.matmul(out, PTs[:, c, 32 * q:32 * q + 32], vb8[:, b, HD * h:HD * h + HD], start=True, stop=False)
                    last = T.matmul(out, PTn[:, c, 32 * q:32 * q + 32], qkv[0:TAIL, QD + KVD + HD * h:QD + KVD + HD * h + HD],
                                    start=False, stop=True)
            last.then_inc(S["smp_o"], 1)
            pe.wait_ge(S["smp_or"], 1)
            for half in range(2):
                last = T.transpose(psT[:, half * P:(half + 1) * P], orowS[:, half], ident[:])
            last.then_inc(S["smp_oT"], 1)
            pe.wait_ge(S["small_ready"], 1)
            pe.wait_ge(S["smp_oTo"], 1)

            def mixed(i, par, h, half, n, first=False):
                if h == 0:
                    pe.wait_ge(S2["mix_in"][par], 16 * half + 16)
                    if not first:
                        pe.wait_ge(S["x2_ready"], i)
                for c in range(2 * RC):
                    last = T.matmul(psQ[0:n, h * 512:h * 512 + 512], mixb[:, par, c, 0:n], wout[:, c, h * 512:h * 512 + 512],
                                    start=c == 0, stop=c == 2 * RC - 1)
                if h == 1:
                    last.then_inc(S["mixed_psum"], 1)

            def step_b(i, par, half, d0=True, d1=True, d2=True, n0=P, n1=P, n2=P, first0=False, first1=False):
                if d0:
                    mixed(i, par, 0, half, n0, first0)
                if d2:
                    pe.wait_ge(S["act_ready"], i - 1)
                    pe.wait_ge(S["rtanh"], i - 1)
                    av = actr[0:n2].rearrange("p (m j) -> p j m", j=2)
                    for jj in range(2):
                        T.transpose(psP[:, 768 + jj * P:768 + jj * P + n2], av[:, jj], ident[0:n2, 0:n2])
                    pe.wait_ge(S["msk_ready"], i - 1)
                    pe.wait_ge(S["mrun_ready"], i - 1)
                    T.matmul(psP[:, 640:640 + NE], tri[:], msk_all[:, i - 2], start=True, stop=False)
                    T.matmul(psP[:, 640:640 + NE], ones[:], mrun[:], start=False, stop=True).then_inc(S["pos_psum"], 1)
                if d1:
                    pe.wait_ge(S["h2_ready"], i)
                    if not first1:
                        pe.wait_ge(S["h2T_ready"], i - 1)
                    hv = h2[0:n1].rearrange("p (m k) -> p k m", k=KC)
                    for k in range(KC):
                        last = T.transpose(psT[:, k * P:k * P + n1], hv[:, k], ident[0:n1, 0:n1])
                    last.then_inc(S["h2T_psum"], 1)
                if d0:
                    mixed(i, par, 1, half, n0)
                if d2:
                    pe.wait_ge(S["actT_ready"], i - 1)
                    if not (isinstance(i, int) and i == 2):
                        pe.wait_ge(S["sh_ready"], i - 2)
                    for h in range(2):
                        for jj in range(2):
                            last = T.matmul(psS[0:n2, h * 512:h * 512 + 512], actT[:, jj, 0:n2], shd[:, jj, h * 512:h * 512 + 512],
                                            start=jj == 0, stop=jj == 1)
                    last.then_inc(S["shd_psum"], 1)
                if d1:
                    pe.wait_ge(S["h2T_ready"], i)
                    if not first1:
                        pe.wait_ge(S["act_ready"], i - 1)
                    for k in range(KC):
                        last = T.matmul(psP[0:n1, 512:512 + NE], h2T[:, k, 0:n1], rw[:, k], start=k == 0, stop=k == KC - 1)
                    last.then_inc(S["router_psum"], 1)
                    for k in range(KC):
                        last = T.matmul(psP[0:n1, 0:2 * F], h2T[:, k, 0:n1], shgu[:, k], start=k == 0, stop=k == KC - 1)
                    last.then_inc(S["shup_psum"], 1)

            pe.wait_ge(S["wB_in"], 16 * 5)
            step_b(0, 0, 0, d1=False, d2=False, first0=True)
            step_b(1, 1, 0, d2=False, first1=True)
            step_b(2, 0, 1)
            step_b(3, 1, 1)
            with pe.Fori(2, NT // 2) as j:
                for s in range(2):
                    step_b(2 * j + s, s, j)
            step_b(NT, 0, NT // 2, n0=TAIL)
            step_b(NT + 1, 1, 0, d0=False, n1=TAIL)
            step_b(NT + 2, 0, 0, d0=False, d1=False, n2=TAIL)
            pe.wait_ge(S["mrun_ready"], ALL + 1)
            pe.wait_ge(S["act_ready"], ALL)
            T.matmul(psP[:, 0:NE], ones[:], mrun[:], start=True, stop=True).then_inc(S["cnt_psum"], 1)

            def x_tr(b, s, pairs):
                pe.wait_ge(S2["gather_in"][s], pairs)
                xv = xg[:, s].rearrange("p (m k) -> p k m", k=KC)
                for k in range(KC):
                    last = T.transpose(psT[:, k * P:(k + 1) * P], xv[:, k], ident[:])
                last.then_inc(S["xgT_psum"], 1)

            def up(b, s, free=True):
                e = pe.value_load(blkr[0:1, bass.ds(b, 1), 0:1], min_val=0, max_val=NE - 1)
                pe.wait_ge(S["w_in"], e * 48 + 48)
                pe.wait_ge(S["xgT_ready"], b + 1)
                if free:
                    pe.wait_ge(S["dact_ready"], b - 1)
                for k in range(KC):
                    last = T.matmul(psP[:, s * 512:s * 512 + 2 * F], xgT[:, s, k], wg[:, bass.ds(e % SLOTS, 1), 0:2, k * F:(k + 1) * F],
                                    start=k == 0, stop=k == KC - 1)
                last.then_inc(S["up_psum"], 1)

            def a_tr(b):
                pe.wait_ge(S["dact_ready"], b + 1)
                av = actD[:].rearrange("p (m j) -> p j m", j=2)
                for jj in range(2):
                    last = T.transpose(psQ[:, jj * P:(jj + 1) * P], av[:, jj], ident[:])
                last.then_inc(S["dactT_psum"], 1)

            def down(b, free=True):
                e = pe.value_load(blkr[0:1, bass.ds(b, 1), 0:1], min_val=0, max_val=NE - 1)
                pe.wait_ge(S["dactT_ready"], b + 1)
                if free:
                    pe.wait_ge(S["ysb_ready"], b)
                for h in range(2):
                    for jj in range(2):
                        last = T.matmul(psS[:, h * 512:h * 512 + 512], actDT[:, jj],
                                        wg[:, bass.ds(e % SLOTS, 1), 2, jj * D + h * 512:jj * D + h * 512 + 512], start=jj == 0, stop=jj == 1)
                last.then_inc(S["down_psum"], 1)

            pe.wait_ge(S["blkr_in"], 16)
            x_tr(0, 0, 16)
            up(0, 0, free=False)
            pe.wait_ge(S["xgT_ready"], 1)
            x_tr(1, 1, 16)
            up(1, 1, free=False)
            a_tr(0)
            pe.wait_ge(S["xgT_ready"], 2)
            x_tr(2, 0, 32)
            down(0, free=False)
            last_pair = pe.value_load(nblk[0:1, 0:1], min_val=0, max_val=NB // 2 - 1)
            with pe.Fori(1, NB // 2) as j:
                with pe.If(j < last_pair + 1):
                    for s in range(2):
                        b = 2 * j + s
                        up(b, s)
                        a_tr(b - 1)
                        x_tr(b + 1, 1 - s, 16 * (j + 1 + s))
                        down(b - 1)
            a_tr(last_pair * 2 + 1)
            down(last_pair * 2 + 1)


_INS = ["x_prompt", "x_sample", "c_prompt", "c_sample", "cache_k_win", "cache_v_win", "state_conv",
        "state_rnn", "ada_w", "ada_b", "norm_mix", "w_in", "conv_w", "conv_b", "gate_a_w", "gate_a_b",
        "gate_x_w", "gate_x_b", "lru_lambda", "q_norm", "k_norm", "attn_sinks", "w_out", "norm_ffn",
        "router_w", "router_bias", "exp_w_gate", "exp_w_up", "exp_w_down", "sh_w_gate", "sh_w_up",
        "sh_w_down"]
_OUTS = [(1, 2048, 1024), (8, 4, 1024), (1, 1, 128, 2, 64), (1, 1, 128, 2, 64), (1, 1, 3, 512), (1, 1, 512),
         (1, 8, 128, 2, 64), (1, 8, 128, 2, 64), (1, 8, 3, 512), (1, 8, 512)]


def kernel(**inputs):
    import numpy as _np
    import concourse.bacc as _bacc
    from concourse import mybir as _mybir
    from concourse.bass_utils import run_bass_kernel_spmd as _run

    nc = _bacc.Bacc("TRN2", target_bir_lowering=False, num_devices=1)
    arrays, args = {}, []
    for name in _INS:
        a = _np.ascontiguousarray(inputs[name])
        arrays[f"in_{name}_dram"] = a
        args.append(nc.dram_tensor(f"in_{name}_dram", a.shape, _mybir.dt.from_np(a.dtype), kind="ExternalInput").ap())
    for i, shape in enumerate(_OUTS):
        args.append(nc.dram_tensor(f"out_{i}_dram", shape, _mybir.dt.float32, kind="ExternalOutput").ap())
    program(nc, *args)
    r = _run(nc, [arrays], core_ids=[0])
    return tuple(r.results[0][f"out_{i}_dram"] for i in range(len(_OUTS)))
```

```python
from contextlib import ExitStack

import concourse.bass as bass
from concourse import mybir

ALU = mybir.AluOpType
ACT = mybir.ActivationFunctionType
AX = mybir.AxisListType
F32 = mybir.dt.float32
I32 = mybir.dt.int32
U32 = mybir.dt.uint32
R32 = mybir.dt.float32r

P = 128
NEG = -1e30
EPS = 1e-6
LRU_C = 8.0
ROUTE_SCALE = 2.5
GELU_C = 0.7978845608028654
GELU_A = 0.044715


def program(nc, x_prompt, x_sample, c_prompt, c_sample, cache_k_win, cache_v_win, state_conv, state_rnn,
            ada_w, ada_b, norm_mix, w_in, conv_w, conv_b, gate_a_w, gate_a_b, gate_x_w, gate_x_b,
            lru_lambda, q_norm, k_norm, attn_sinks, w_out, norm_ffn, router_w, router_bias,
            exp_w_gate, exp_w_up, exp_w_down, sh_w_gate, sh_w_up, sh_w_down,
            y_prompt, y_sample, k_win_prompt, v_win_prompt, conv_prompt, rnn_prompt,
            k_win_sample, v_win_sample, conv_sample, rnn_sample):
    SEQ, D = x_prompt.shape[1], x_prompt.shape[2]
    NS, TS = x_sample.shape[0], x_sample.shape[1]
    KC = D // P
    R = conv_w.shape[2]
    RC = R // P
    HD = q_norm.shape[1]
    NH = attn_sinks.shape[1]
    NKV = cache_k_win.shape[3]
    GQ = NH // NKV
    KVD = NKV * HD
    QD = NH * HD
    QKV = QD + 2 * KVD
    DIN = w_in.shape[2]
    NE = exp_w_gate.shape[1]
    F = exp_w_gate.shape[3]
    NG = 8
    GE = NE // NG
    TG = 4
    TOPK = 6
    NT = SEQ // P
    TAIL = NS * TS
    NTOK = SEQ + TAIL
    HALO = conv_w.shape[1] - 1
    NB = (NTOK * TOPK + NE * (P - 1)) // P
    NB += NB % 2
    LB = -(-NTOK // P)
    NBT = NB + 4
    MOD = 6 * D
    ALL = NT + 1
    assert TAIL <= 32 and KC == 8 and RC == 4 and KVD == P and QD == 4 * P and R == 4 * P and 2 * F == 512
    assert NE * LB < 9 * P and NS == 8 and TS == 4 and GQ * TS <= 32

    def dram(name, shape, dt=F32):
        return nc.dram_tensor(name, shape, dt, kind="Internal").ap()

    mod_d = dram("mod_d", [TAIL + 1, MOD])
    mix_d = dram("mix_d", [ALL, P, 2 * RC, P])
    h2_d = dram("h2_d", [NTOK + P, D])
    x2_d = dram("x2_d", [NTOK, D])
    acc_d = dram("acc_d", [NTOK + P, D])
    LROWS = 9 * P
    list_d = dram("list_d", [LROWS * P, 2], I32)
    blk_d = dram("blk_d", [2 * P, 4], I32)

    with ExitStack() as ctx:
        def sem(name):
            return ctx.enter_context(nc.semaphore(name))

        base = (nc.sbuf_base + 31) // 32 * 32
        KB = 1024
        XW = base + 0
        YW = XW + 58 * KB
        WK = YW + 59 * KB
        end = {"v": WK, "lim": nc.sbuf_usable_end}

        def at(name, shape, off, dt=F32):
            size = 4
            for s in shape[1:]:
                size *= s
            assert off + size <= end["lim"], (name, off, size, end["lim"])
            return nc.alloc_sbuf_tensor_at(name, shape, dt, offset=off), off + (size + 31) // 32 * 32

        o = WK
        ident, o = at("ident", [P, P], o)
        tri, o = at("tri", [P, P], o)
        ones, o = at("ones", [P, P], o)
        mhalf, o = at("mhalf", [P, 16], o)
        epsc, o = at("epsc", [P, 16], o)
        stat, o = at("stat", [P, 4, 40], o)
        blkr, o = at("blkr", [1, 2 * P, 4], o, I32)
        nord, o = at("nord", [1, 8], o, I32)
        nblk, o = at("nblk", [1, 8], o, I32)
        pid, o = at("pid", [P, 8], o, I32)
        smc, o = at("smc", [P, 16], o)
        gsel, o = at("gsel", [P, 2, GQ], o)
        gtmp, o = at("gtmp", [P, 2, NH], o)
        jdist, o = at("jdist", [P, P + TAIL], o)
        PERS = o

        ada_wt, _ = at("ada_wt", [P, 2, KC, 512], YW)
        o = end["lim"] - 40 * KB
        o -= o % 32
        cp_t, o = at("cp_t", [P, KC], o)
        cs_t, o = at("cs_t", [P, NS, KC], o)
        cp_h, o = at("cp_h", [P, KC], o)
        cs_h, o = at("cs_h", [P, NS, KC], o)
        csil, o = at("csil", [P, KC, TAIL + 1], o)
        adab, o = at("adab", [TAIL + 1, MOD], o)
        gmix, o = at("gmix", [TAIL + 1, 2, D], o)

        win, _ = at("win", [P, KC, DIN], XW)
        o = PERS
        modA, o = at("modA", [P, 2, D], o)
        bias, o = at("bias", [P, NH, 2 * P], o)
        prm, o = at("prm", [P, RC, 40], o)
        gb, o = at("gb", [P, 2 * RC], o)
        lam8, o = at("lam8", [P, RC, 2], o)
        ssq, o = at("ssq", [P, 2], o)
        rst, o = at("rst", [P, 4], o)
        ss10, o = at("ss10", [P, 16], o)
        r10, o = at("r10", [P, 32], o)
        sink, o = at("sink", [P, NH], o)
        mx, o = at("mx", [P, 2, 4, GQ], o)
        esum, o = at("esum", [P, 2, 2, GQ], o)
        hlast, o = at("hlast", [P, RC, 1], o)
        stt, o = at("stt", [P, RC, 36], o)
        xin, o = at("xin", [P, 2, D], o)
        o_hrow = o
        hrow, o = at("hrow", [P, D], o)
        o_hT = o
        hT, o = at("hT", [P, KC, P], o)
        o_xrb = o
        xrb, o = at("xrb", [P, RC, HALO + P], o)
        u, o = at("u", [P, RC, P], o)
        y_t, o = at("y_t", [P, RC, P], o)
        sq_t, o = at("sq_t", [P, RC, P], o)
        gts, o = at("gts", [P, 2 * RC, P], o)
        a_t, o = at("a_t", [P, RC, P], o)
        th_t, o = at("th_t", [P, RC, P], o)
        b_t, o = at("b_t", [P, RC, P], o)
        outr, o = at("outr", [P, RC, P], o)
        qkv, o = at("qkv", [P, QKV], o)
        qn, o = at("qn", [P, QD + KVD], o)
        qT, o = at("qT", [P, 5, P], o)
        kT, o = at("kT", [P, 2, P], o)
        vb, o = at("vb", [P, 2, KVD], o)
        o_sc = o
        sc, o = at("sc", [P, 2, GQ, 2 * P], o)
        o_PT = o
        PT, o = at("PT", [P, GQ, 2, P], o)
        endA = o
        lini, o = at("lini", [P, P, 2], endA, I32)
        zrow, o = at("zrow", [P, D], o)
        o = YW + 33 * KB
        gwt, o = at("gwt", [P, 2, RC, P], o)
        prm_r, o = at("prm_r", [40, R], o)
        stt_r, o = at("stt_r", [36, R], o)
        sqj, o = at("sqj", [P, D], o)
        hs_t, o = at("hs_t", [P, RC, P], o)
        orow, o = at("orow", [P, QD], o)
        oT, o = at("oT", [P, RC, P], o)
        qw, o = at("qw", [P, QD + KVD], o)
        assert o <= WK, o - WK

        wout, _ = at("wout", [P, KC, D], YW)
        o = XW
        wohi, o = at("wohi", [P, KC, D], o, R32)
        wolo, _ = at("wolo", [P, KC, D], YW, R32)
        ck8, o = at("ck8", [P, NS, KVD], o)
        vb8, o = at("vb8", [P, NS, KVD], o)
        kT8, o = at("kT8", [P, NS, P], o)
        kTn, o = at("kTn", [P, TAIL], o)
        qTs, o = at("qTs", [P, NS, 32], o)
        biasS, o = at("biasS", [P, 2, NKV, P + TAIL], o)
        orowS, o = at("orowS", [P, 2, KVD], o)
        oTs, o = at("oTs", [P, GQ, TAIL], o)
        sqB, o = at("sqB", [P, D], o)
        assert o <= YW, o - YW
        scS, _ = at("scS", [P, 2, NKV, P + TAIL], o_sc)
        PTs, _ = at("PTs", [P, 2 * NKV, P], o_PT)
        PTn, _ = at("PTn", [TAIL, 2 * NKV, P], o_hrow)
        distS, o = at("distS", [P, 2, P + TAIL], o_hT)
        penS, o = at("penS", [P, 2, P + TAIL], o)
        penT, o = at("penT", [P, 2, P + TAIL], o)
        mxS, o = at("mxS", [P, 6, 2, NKV], o)
        o = PERS
        iota, o = at("iota", [P, NE], o)
        mrun, o = at("mrun", [P, NE], o)
        msk_all, o = at("msk_all", [P, ALL, NE], o)
        pos_all, o = at("pos_all", [P, ALL, NE], o)
        tokf, o = at("tokf", [P, ALL], o)
        iotp, o = at("iotp", [P, 2], o)
        idxf, o = at("idxf", [P, 8], o)
        wgt, o = at("wgt", [P, 8], o)
        posk, o = at("posk", [P, 2, 2, 8], o)
        entry, o = at("entry", [P, 2, TOPK, 2], o, I32)
        dsti, o = at("dsti", [P, 2, 8], o, I32)
        keepC = o
        h2, o = at("h2", [P, D], o)
        h2T, o = at("h2T", [P, KC, P], o)
        sg, o = at("sg", [P, 2, F], o)
        actr, o = at("actr", [P, F], o)
        actT, o = at("actT", [P, 2, P], o)
        sho, o = at("sho", [P, 2, D], o)
        rt_s, o = at("rt_s", [P, NE], o)
        rt_b, o = at("rt_b", [P, NE], o)
        rt_m, o = at("rt_m", [P, NE], o)
        rt_8, o = at("rt_8", [P, NG, 8], o)
        rt_g, o = at("rt_g", [P, 4, 8], o)
        rt_u, o = at("rt_u", [P, 2, 8], o, U32)
        rt_oh, o = at("rt_oh", [P, TOPK, NE], o)
        rt_t, o = at("rt_t", [P, TOPK, NE], o)
        ssqB, o = at("ssqB", [P, 4], o)
        shgu, o = at("shgu", [P, KC, 2 * F], o)
        shd, o = at("shd", [P, 2, D], o)
        rw, o = at("rw", [P, KC, NE], o)
        modB, o = at("modB", [P, 3, D], o)
        rbias, o = at("rbias", [P, NE], o)
        mxhi, o = at("mxhi", [P, 2 * RC, P], o, R32)
        mxlo, o = at("mxlo", [P, 2 * RC, P], o, R32)
        o = YW + 4 * KC * D
        mixb, o = at("mixb", [P, 2, 2 * RC, P], o)
        xb, o = at("xb", [P, 2, D], o)
        x2, o = at("x2", [P, 2, D], o)
        assert o <= WK

        o = keepC + 4 * D
        cnt, o = at("cnt", [P, 8, NE], o)
        efst, o = at("efst", [1, 4 + NE], o)
        cnti, o = at("cnti", [P, 2, NE], o, I32)
        blkf, o = at("blkf", [P, 4, NE], o)
        bt_t, o = at("bt_t", [P, 2, NE], o)
        blki, o = at("blki", [P, 2, 4], o, I32)
        bsum, o = at("bsum", [P, 8, 2], o)

        WE = 3 * KC * F
        GU = 2 * KC * F
        wraw, o = at("wraw", [P, 2, WE], XW)
        whi, o = at("whi", [P, 2, WE], o, R32)
        xg, o = at("xg", [P, 2, D], o)
        sgD, o = at("sgD", [P, 2, F], o)
        actD, o = at("actD", [P, F], o)
        aThi, o = at("aThi", [P, 2, P], o, R32)
        aTlo, o = at("aTlo", [P, 2, P], o, R32)
        assert o <= WK, o - WK
        o = PERS
        wlo, o = at("wlo", [P, 2, WE], o, R32)
        xThi, o = at("xThi", [P, 2, KC, P], o, R32)
        xTlo, o = at("xTlo", [P, 2, KC, P], o, R32)
        ysb, o = at("ysb", [P, 2, D], o)
        dnt, o = at("dnt", [1, 2 * P], o, I32)
        dnf, o = at("dnf", [1, 5, 2 * P], o)
        lent, o = at("lent", [P, 2, 2], o, I32)
        six, o = at("six", [P, 2, 1], o, I32)
        tok_all, o = at("tok_all", [P, NBT], o, I32)
        w_all, o = at("w_all", [P, NBT], o)
        o = YW
        acc, o = at("acc", [P, 4, D], o)
        xe, o = at("xe", [P, 4, D], o)
        g2b, o = at("g2b", [P, 2, D], o)
        ye, o = at("ye", [P, 4, D], o)
        assert o <= WK

        psT = ctx.enter_context(nc.psum_tensor("psT", [P, 1024], F32))
        psP = ctx.enter_context(nc.psum_tensor("psP", [P, 1024], F32))
        psQ = ctx.enter_context(nc.psum_tensor("psQ", [P, 1024], F32))
        psS = ctx.enter_context(nc.psum_tensor("psS", [P, 1024], F32))

        names = """c_in norms_in ada_psum_ready mod_row_ready mod_bank_free csil_ready c_tanh prm_in prm_psum prm_ready
            sink_in qw_in gate_w_zero gate_w_in const_ready modA_in win_in tailmod_in ssq_ready rstd_ready
            h_ready hT_psum hT_ready xr_psum xr_ready conv_ready yr_psum y_ready gates_psum gates_sum gates_tanh
            loga_ready a_ready b2_ready bsqrt_ready gelu_in gelu_tanh outr_ready qkv1_psum qkv2_psum qkv_ready
            ss10_ready r10_ready qn_ready v_ready qkT_psum qkT_ready s_psum s_read m_ready p_ready pT_psum
            pT_ready o_psum o_ready oT_psum oT_ready lam_exp lam_one kwin_st small_psum small_ready small_st
            cachecp_st init_st smp_in ckT_psum ckT_ready smp_psum smp_act smp_dve smp_oT_st wB_in modB_in
            rbias_in mixed_psum x2_ready ssqB_ready rstdB_ready h2_ready h2T_psum h2T_ready router_psum rtanh
            shup_psum shtanh act_ready actT_ready shd_psum sh_ready pos_psum msk_ready tailmodB_in mrun_ready
            entry_ready cnt_psum blk_ready blk_st blkr_in w_gu_in w_dn_in hi_gu hi_dn lo_gu lo_dn lent_used
            eps_added pool_steps sp_steps b_hi b_lo xgT_psum xThi_ready xTlo_ready up_psum dtanh dact_ready
            dactT_psum aThi_ready aTlo_ready down_psum ysb_ready outr_st oT_st ye_ready g2_in add_st""".split()
        S = {n: sem(n) for n in names}
        slots2 = """ada_in mod_st x_in mix_in xB_in x2_st h2_st sh_st list_st lent_in gather_in""".split()
        S2 = {n: [sem(f"{n}0"), sem(f"{n}1")] for n in slots2}
        S4 = {n: [sem(f"{n}{k}") for k in range(4)] for n in ("xe_in", "out_st")}

        WO = 8
        CONST_BIAS, CONST_ROWS, CONST_B = 2, 3, 4
        SMP_S, SMP_PT, SMP_O, SMP_OT = 1, 2, 3, 4
        SMP_P, SMP_PT_OUT, SMP_OT_OUT = 1, 2, 3
        SMP_Q0, SMP_M, SMP_OROW = 1, 2, 3

        block = ctx.enter_context(nc.Block())
        NCH = MOD // 512
        ada_v = ada_w[0].rearrange("(p k) n -> p k n", k=KC)
        SMP = NT

        def bc(ap, n):
            return ap.unsqueeze(len(ap.shape)).to_broadcast(list(ap.shape) + [n])

        @block.sync
        def _(sp):
            sp.dma_start(cp_t[:], c_prompt[0].rearrange("(p k) -> p k", k=KC)).then_inc(S["c_in"], 16)
            sp.dma_start(cs_t[:], c_sample.rearrange("b (p k) -> p b k", k=KC)).then_inc(S["c_in"], 16)
            for s in range(2):
                sp.dma_start(ada_wt[:, s], ada_v[:, :, s * 512:(s + 1) * 512]).then_inc(S2["ada_in"][s], 16)
            sp.dma_start(xin[:, 0], x_prompt[0, 0:P]).then_inc(S2["x_in"][0], 16)
            sp.dma_start(xin[:, 1], x_prompt[0, P:2 * P]).then_inc(S2["x_in"][1], 16)

            def ada_pair(j):
                for s in range(2):
                    sp.wait_ge(S["ada_psum_ready"], 2 * j + s - 1)
                    sp.dma_start(ada_wt[:, s], ada_v[:, :, bass.ds(j * 1024 + s * 512, 512)]).then_inc(S2["ada_in"][s], 16)

            win_v = w_in[0].rearrange("(p k) n -> p k n", k=KC)
            sp.dma_start(win[:, 0:KC // 2], win_v[:, 0:KC // 2]).then_inc(S["win_in"], 16)
            with sp.Fori(1, 5) as j:
                ada_pair(j)
                sp.dma_start(win[:, bass.ds(j + 3, 1)], win_v[:, bass.ds(j + 3, 1)]).then_inc(S["win_in"], 16)
            ada_pair(NCH // 2 - 1)
            sp.wait_ge(S2["mod_st"][0], 16)
            sp.dma_start(modA[:], mod_d[TAIL:TAIL + 1, 0:2 * D].rearrange("a (m d) -> a m d", m=2)
                         .to_broadcast([P, 2, D])).then_inc(S["modA_in"], 16)
            sp.wait_ge(S["ada_psum_ready"], NCH)
            sp.dma_start(wout[:], w_out[0].rearrange("(c p) n -> p c n", p=P)).then_inc(S["wB_in"], 16)

            def step(i, par, nxt=True, proj=True, att=True, n=P):
                if nxt:
                    sp.wait_ge(S["h_ready"], i + 1)
                    sp.dma_start(xin[:, par], x_prompt[0, bass.ds((i + 2) * P, P)]).then_inc(S2["x_in"][par], 16)
                if proj:
                    sp.wait_ge(S["outr_ready"], i + 1)
                    sp.dma_start(mix_d[i, :, 0:RC, 0:n], outr[:, :, 0:n]).then_inc(S["outr_st"], 16)
                if att:
                    sp.wait_ge(S["oT_ready"], i)
                    sp.dma_start(mix_d[i - 1, :, RC:2 * RC, :], oT[:]).then_inc(S["oT_st"], 16)

            step(0, 0, att=False)
            step(1, 1)
            with sp.Fori(1, NT // 2 - 1) as j:
                for s in range(2):
                    step(2 * j + s, s)
            sp.wait_ge(S["h_ready"], NT - 1)
            sp.dma_start(xin[0:TAIL, 0], x_sample.rearrange("b t d -> (b t) d")).then_inc(S2["x_in"][0], 16)
            step(NT - 2, 0, nxt=False)
            sp.wait_ge(S["h_ready"], NT)
            sp.dma_start(modA[0:TAIL], mod_d[0:TAIL, 0:2 * D].rearrange("a (m d) -> a m d", m=2)).then_inc(S["tailmod_in"], 16)
            step(NT - 1, 1, nxt=False)
            sp.wait_ge(S["qn_ready"], NT)
            sp.dma_start(k_win_prompt[0, 0].rearrange("t h d -> t (h d)"), qn[:, QD:]).then_inc(S["kwin_st"], 16)
            sp.dma_start(v_win_prompt[0, 0].rearrange("t h d -> t (h d)"), qkv[:, QD + KVD:]).then_inc(S["kwin_st"], 16)
            sp.wait_ge(S["qkv2_psum"], NT + 1)
            sp.dma_start(ck8[:], cache_k_win[0].rearrange("b t h d -> t b (h d)")).then_inc(S["smp_in"], 16)
            sp.dma_start(vb8[:], cache_v_win[0].rearrange("b t h d -> t b (h d)")).then_inc(S["smp_in"], 16)
            step(NT, 0, nxt=False, n=TAIL)
            sp.wait_ge(S["qn_ready"], NT + 1)
            for out, src in ((k_win_sample, qn[0:TAIL, QD:]), (v_win_sample, qkv[0:TAIL, QD + KVD:])):
                for b in range(NS):
                    sp.dma_start(out[0, b, P - TS:P].rearrange("t h d -> t (h d)"), src[b * TS:(b + 1) * TS]).then_inc(S["kwin_st"], 16)
            sp.wait_ge(S["small_ready"], 1)
            for dst, a, n in ((conv_prompt[0, 0], 0, HALO), (rnn_prompt[0], HALO, 1),
                              (conv_sample[0].rearrange("b j r -> (b j) r"), HALO + 1, NS * HALO),
                              (rnn_sample[0], HALO + 1 + NS * HALO, NS)):
                sp.dma_start(dst, stt_r[a:a + n]).then_inc(S["small_st"], 16)
            sp.wait_ge(S["oT_st"], 16 * NT)
            sp.wait_ge(S["outr_st"], 16 * (NT + 1))
            sp.wait_ge(S["kwin_st"], 16 * (2 + 2 * NS))

            sp.wait_ge(S["small_st"], 64)

            def load_b(i, par, n=P, free=True):
                if free:
                    sp.wait_ge(S["x2_ready"], i - 1)
                sp.dma_start(mixb[:, par, :, 0:n], mix_d[i, :, :, 0:n]).then_inc(S2["mix_in"][par], 16)
                src = x_prompt[0, bass.ds(i * P, P)] if n == P else x_sample.rearrange("b t d -> (b t) d")
                sp.dma_start(xb[0:n, par], src).then_inc(S2["xB_in"][par], 16)

            def store_h2(i, par, n=P):
                sp.wait_ge(S["x2_ready"], i + 1)
                sp.dma_start(x2_d[bass.ds(i * P, n)], x2[0:n, par]).then_inc(S2["x2_st"][par], 16)
                sp.wait_ge(S["h2_ready"], i + 1)
                sp.dma_start(h2_d[bass.ds(i * P, n)], h2[0:n]).then_inc(S2["h2_st"][par], 16)

            def store_sh(i, par, n=P):
                sp.wait_ge(S["sh_ready"], i + 1)
                sp.dma_start(acc_d[bass.ds(i * P, n)], sho[0:n, par]).then_inc(S2["sh_st"][par], 16)

            load_b(0, 0, free=False)
            sp.wait_ge(S["init_st"], 48)
            sp.wait_ge(S["smp_act"], SMP_OT_OUT)
            sp.wait_ge(S2["mod_st"][1], 16)
            sp.dma_start(modB[:], mod_d[TAIL:TAIL + 1, 2 * D:5 * D].rearrange("a (m d) -> a m d", m=3)
                         .to_broadcast([P, 3, D])).then_inc(S["modB_in"], 16)
            sp.dma_start(rbias[:], router_bias.to_broadcast([P, NE])).then_inc(S["rbias_in"], 16)
            load_b(1, 1, free=False)
            sp.dma_start(shgu[:, :, 0:F], sh_w_gate[0].rearrange("(p k) f -> p k f", k=KC)).then_inc(S["wB_in"], 16)
            sp.dma_start(shgu[:, :, F:2 * F], sh_w_up[0].rearrange("(p k) f -> p k f", k=KC)).then_inc(S["wB_in"], 16)
            sp.dma_start(shd[:], sh_w_down[0].rearrange("(p j) d -> p j d", j=2)).then_inc(S["wB_in"], 16)
            sp.dma_start(rw[:], router_w[0].rearrange("(p k) e -> p k e", k=KC)).then_inc(S["wB_in"], 16)
            store_h2(0, 0)
            load_b(2, 0)
            store_h2(1, 1)
            with sp.Fori(1, NT // 2 - 1) as j:
                for s in range(2):
                    load_b(2 * j + s + 1, 1 - s)
                    store_sh(2 * j + s - 2, s)
                    store_h2(2 * j + s, s)
            load_b(NT - 1, 1)
            store_sh(NT - 4, 0)
            store_h2(NT - 2, 0)
            sp.wait_ge(S["x2_ready"], NT - 1)
            sp.wait_ge(S["smp_oT_st"], 16 * 2 * GQ)
            load_b(NT, 0, TAIL)
            store_sh(NT - 3, 1)
            store_h2(NT - 1, 1)
            sp.dma_start(modB[0:TAIL], mod_d[0:TAIL, 2 * D:5 * D].rearrange("a (m d) -> a m d", m=3)).then_inc(S["tailmodB_in"], 16)
            store_sh(NT - 2, 0)
            store_h2(NT, 0, TAIL)
            store_sh(NT - 1, 1)
            store_sh(NT, 0, TAIL)

            def load_gu(n, s, e=None):
                if e is None:
                    e = sp.value_load(blkr[0:1, bass.ds(n, 1), 3:4], min_val=0, max_val=NE - 1)
                for m, w in enumerate((exp_w_gate, exp_w_up)):
                    sp.dma_start(wraw[:, s, m * KC * F:(m + 1) * KC * F],
                                 w[0, bass.ds(e, 1)].rearrange("a (p k) f -> p (a k f)", k=KC)).then_inc(S["w_gu_in"], 16)
                return e

            def load_dn(e, s):
                sp.dma_start(wraw[:, s, GU:], exp_w_down[0, bass.ds(e, 1)].rearrange("a (p j) d -> p (a j d)", j=2)).then_inc(S["w_dn_in"], 16)

            sp.wait_ge(S["blk_ready"], 1)
            e0 = load_gu(0, 0, sp.value_load(nord[0:1, 1:2], min_val=0, max_val=NE - 1))
            sp.wait_ge(S["blk_ready"], 2)
            for h in range(2):
                sp.dma_start(blk_d[h * P:(h + 1) * P], blki[:, h]).then_inc(S["blk_st"], 16)
            sp.wait_ge(S["blk_st"], 32)
            sp.dma_start(blkr[:], blk_d.unsqueeze(0)).then_inc(S["blkr_in"], 16)
            sp.wait_ge(S["blkr_in"], 16)
            load_dn(e0, 0)
            sp.wait_ge(S["w_gu_in"], 32)
            e1 = load_gu(1, 1)
            sp.wait_ge(S["w_dn_in"], 16)
            load_dn(e1, 1)
            experts = sp.value_load(nord[0:1, 0:1], min_val=2, max_val=NE)
            with sp.Fori(1, NE // 2) as q:
                for s in range(2):
                    with sp.If(q * 2 + s < experts):
                        sp.wait_ge(S["w_gu_in"], q * 64 + s * 32)
                        sp.sem_inc(S["sp_steps"], 1)
                        sp.wait_ge(S["lo_gu"], q * 2 + s - 1)
                        e = load_gu(q * 2 + s, s)
                        sp.wait_ge(S["w_dn_in"], q * 32 + s * 16)
                        sp.sem_inc(S["sp_steps"], 1)
                        sp.wait_ge(S["lo_dn"], q * 2 + s - 1)
                        load_dn(e, s)

            y_out = y_prompt[0]

            def load_e(t, s, n=P, free=True):
                if free:
                    sp.wait_ge(S["ye_ready"], t - 3)
                sp.dma_start(xe[0:n, s], x2_d[bass.ds(t * P, n)]).then_inc(S4["xe_in"][s], 16)
                sp.dma_start(acc[0:n, s], acc_d[bass.ds(t * P, n)]).then_inc(S4["xe_in"][s], 16)

            last_pair = sp.value_load(nblk[0:1, 0:1], min_val=0, max_val=NB // 2 - 1)
            sp.wait_ge(S["add_st"], last_pair * 32 + 32)
            sp.dma_start(g2b[:, 0], mod_d[TAIL:TAIL + 1, 5 * D:].to_broadcast([P, D])).then_inc(S["g2_in"], 16)
            sp.dma_start(g2b[0:TAIL, 1], mod_d[0:TAIL, 5 * D:]).then_inc(S["g2_in"], 16)
            for s in range(4):
                load_e(s, s, free=False)
            with sp.Fori(1, NT // 4) as q:
                for s in range(4):
                    load_e(4 * q + s, s)
            load_e(NT, 0, TAIL)
            for s in range(4):
                sp.wait_ge(S4["out_st"][s], 16 * (NT // 4 + (s == 0)))
            for n in ("small_st", "cachecp_st"):
                sp.wait_ge(S[n], 64 if n == "small_st" else 32)

        @block.gpsimd
        def _(gp):
            nc.gpsimd.memset(ident[:], 0.0)
            nc.gpsimd.memset(tri[:], 1.0)
            nc.gpsimd.memset(ones[:], 1.0)
            nc.gpsimd.memset(mhalf[:], -0.5)
            nc.gpsimd.memset(epsc[:], EPS)
            nc.gpsimd.iota(hrow[:, 0:2 * P], [[-1, 2 * P]], base=P, channel_multiplier=1, allow_small_or_imprecise_dtypes=True)
            gp.drain()
            nc.gpsimd.affine_select(out=ident[:], in_=ident[:], compare_op=ALU.not_equal, fill=1.0, base=0,
                                    pattern=[[-1, P]], channel_multiplier=1)
            nc.gpsimd.affine_select(out=tri[:], in_=tri[:], compare_op=ALU.is_gt, fill=0.0, base=0,
                                    pattern=[[1, P]], channel_multiplier=-1)
            gp.drain().then_inc(S["const_ready"], 1)
            for h in range(NH):
                nc.gpsimd.tensor_scalar(bias[:, h], hrow[:, 0:2 * P], -(2.0 ** (-8.0 * (h + 1) / NH)), None, ALU.mult)
            gp.drain()
            nc.gpsimd.affine_select(out=bias[:], in_=bias[:], compare_op=ALU.is_ge, fill=NEG, base=P,
                                    pattern=[[0, NH], [-1, 2 * P]], channel_multiplier=1)
            gp.drain()
            nc.gpsimd.affine_select(out=bias[:], in_=bias[:], compare_op=ALU.is_ge, fill=NEG, base=0,
                                    pattern=[[0, NH], [1, 2 * P]], channel_multiplier=-1)
            gp.drain().then_inc(S["const_ready"], 1)
            nc.gpsimd.iota(pid[:, 0:1], [[1, 1]], base=0, channel_multiplier=1)
            nc.gpsimd.iota(jdist[:, 0:P], [[-1, P]], base=P, channel_multiplier=0, allow_small_or_imprecise_dtypes=True)
            nc.gpsimd.iota(jdist[:, P:], [[-1, TAIL]], base=0, channel_multiplier=0, allow_small_or_imprecise_dtypes=True)
            gp.drain().then_inc(S["const_ready"], 1)
            def rstd(i, par, n=P):
                gp.wait_ge(S["ssq_ready"], i + 1)
                nc.gpsimd.tensor_tensor(rst[0:n, 2:3], ssq[0:n, par:par + 1], epsc[0:n, 0:1], ALU.add)
                gp.drain()
                nc.gpsimd.tensor_tensor(rst[0:n, par:par + 1], rst[0:n, 2:3], mhalf[0:n, 0:1], ALU.pow).then_inc(S["rstd_ready"], 1)

            def r10_of(i, n=P):
                gp.wait_ge(S["ss10_ready"], i + 1)
                nc.gpsimd.tensor_tensor(r10[0:n, 16:16 + NH + NKV], ss10[0:n, 0:NH + NKV], epsc[0:n, 0:NH + NKV], ALU.add)
                gp.drain()
                nc.gpsimd.tensor_tensor(r10[0:n, 0:NH + NKV], r10[0:n, 16:16 + NH + NKV], mhalf[0:n, 0:NH + NKV],
                                        ALU.pow).then_inc(S["r10_ready"], 1)

            rstd(0, 0)
            gp.wait_ge(S2["mod_st"][1], 16)
            nc.gpsimd.memset(lini[:], 0)
            nc.gpsimd.memset(zrow[:], 0.0)
            gp.drain()
            nc.gpsimd.iota(lini[:, :, 0], [[1, P]], base=NTOK, channel_multiplier=0)
            gp.drain()
            gp.dma_start(list_d.rearrange("(p b c) a -> p b c a", p=P, c=P), lini[:].unsqueeze(1).to_broadcast([P, 9, P, 2])
                         ).then_inc(S["init_st"], 16)
            gp.dma_start(h2_d[NTOK:], zrow[:]).then_inc(S["init_st"], 16)
            gp.dma_start(acc_d[NTOK:], zrow[:]).then_inc(S["init_st"], 16)
            gp.dma_start(k_win_sample[0, :, 0:P - TS].rearrange("b t h d -> b (t h d)"),
                         cache_k_win[0, :, TS:P].rearrange("b t h d -> b (t h d)")).then_inc(S["cachecp_st"], 16)
            gp.dma_start(v_win_sample[0, :, 0:P - TS].rearrange("b t h d -> b (t h d)"),
                         cache_v_win[0, :, TS:P].rearrange("b t h d -> b (t h d)")).then_inc(S["cachecp_st"], 16)

            with gp.Fori(0, NT // 2 - 1) as j:
                for s in range(2):
                    rstd(2 * j + s + 1, 1 - s)
                    r10_of(2 * j + s)
            rstd(NT - 1, 1)
            r10_of(NT - 2)
            rstd(NT, 0, TAIL)
            r10_of(NT - 1)
            r10_of(NT, TAIL)

            gp.wait_ge(S["r10_ready"], NT + 1)
            gp.wait_ge(S["smp_psum"], SMP_S)
            nc.gpsimd.iota(iota[:], [[1, NE]], base=0, channel_multiplier=0, allow_small_or_imprecise_dtypes=True)
            nc.gpsimd.iota(tokf[:], [[P, ALL]], base=0, channel_multiplier=1, allow_small_or_imprecise_dtypes=True)
            nc.gpsimd.iota(iotp[:], [[P, 2]], base=0, channel_multiplier=1, allow_small_or_imprecise_dtypes=True)
            gp.drain().then_inc(S["const_ready"], 1)
            gp.wait_ge(S["init_st"], 48)
            gp.nop()

            def rstd_b(i, n=P):
                gp.wait_ge(S["ssqB_ready"], i + 1)
                nc.gpsimd.tensor_tensor(ssqB[0:n, 2:3], ssqB[0:n, 0:1], epsc[0:n, 0:1], ALU.add).then_inc(S["eps_added"], 1)
                gp.wait_ge(S["eps_added"], i + 1)
                nc.gpsimd.tensor_tensor(ssqB[0:n, 1:2], ssqB[0:n, 2:3], mhalf[0:n, 0:1], ALU.pow).then_inc(S["rstdB_ready"], 1)

            def take_wait():
                gp.sem_inc(S["pool_steps"], 1)

            def enlist(i, par, n=P):
                gp.wait_ge(S["entry_ready"], i + 1)
                take_wait()
                for k in range(TOPK):
                    nc.gpsimd.indirect_dma_start(list_d, bass.IndirectOffsetOnAxis(ap=dsti[0:n, par, k:k + 1], axis=0),
                                                 entry[0:n, par, k], None).then_inc(S2["list_st"][par], 16)

            rstd_b(0)
            rstd_b(1)
            with gp.Fori(1, NT // 2) as j:
                for s in range(2):
                    rstd_b(2 * j + s)
                    enlist(2 * j + s - 2, s)
            rstd_b(NT, TAIL)
            enlist(NT - 2, 0)
            enlist(NT - 1, 1)
            enlist(NT, 0, TAIL)

            def gather(b, s, half):
                gp.wait_ge(S2["lent_in"][s], 16 * half + 16)
                take_wait()
                nc.gpsimd.indirect_dma_start(xg[:, s], None, h2_d, bass.IndirectOffsetOnAxis(ap=lent[:, s, 0:1], axis=0)
                                             ).then_inc(S2["gather_in"][s], 16)

            def add_rows(b, s, first=False):
                if not first:
                    gp.wait_ge(S["add_st"], 16 * b)
                gp.wait_ge(S["ysb_ready"], b + 1)
                take_wait()
                nc.gpsimd.indirect_dma_start(acc_d, bass.IndirectOffsetOnAxis(ap=six[:, s], axis=0), ysb[:, s], None,
                                             compute_op=ALU.add).then_inc(S["add_st"], 16)

            for s in range(2):
                for par in range(2):
                    gp.wait_ge(S2["h2_st"][par], 16 * (NT // 2 + 1 - par))
                gather(s, s, 0)
            for b in range(2, 5):
                gp.wait_ge(S["xgT_psum"], b - 1)
                gather(b, b % 2, b // 2)
            for par in range(2):
                gp.wait_ge(S2["sh_st"][par], 16 * (NT // 2 + 1 - par))
            add_rows(0, 0, first=True)
            last_pair = gp.value_load(nblk[0:1, 0:1], min_val=0, max_val=NB // 2 - 1)
            with gp.Fori(1, NB // 2) as j:
                with gp.If(j < last_pair + 1):
                    for s in range(2):
                        gp.wait_ge(S["xgT_psum"], 2 * j + s + 2)
                        gather(2 * j + s + 3, 1 - s, j + 1 + s)
                        add_rows(2 * j + s - 1, 1 - s)
            add_rows(last_pair * 2 + 1, 1)

        @block.scalar
        def _(act):
            for a, n, src in ((0, HALO + 1, conv_w[0]), (4, 1, conv_b), (5, 1, gate_a_b), (6, 1, gate_x_b), (7, 1, lru_lambda),
                              (8, NS * HALO, state_conv[0].rearrange("b j r -> (b j) r")), (8 + NS * HALO, NS, state_rnn[0])):
                act.dma_start(prm_r[a:a + n], src).then_inc(S["prm_in"], 16)
            act.dma_start(adab[:], ada_b.to_broadcast([TAIL + 1, MOD])).then_inc(S["norms_in"], 16)
            act.dma_start(gmix[:, 0], norm_mix.to_broadcast([TAIL + 1, D])).then_inc(S["norms_in"], 16)
            act.dma_start(gmix[:, 1], norm_ffn.to_broadcast([TAIL + 1, D])).then_inc(S["norms_in"], 16)
            act.dma_start(sink[:], attn_sinks.to_broadcast([P, NH])).then_inc(S["sink_in"], 16)
            for h in range(NH):
                act.dma_start(qw[:, h * HD:(h + 1) * HD], q_norm.to_broadcast([P, HD])).then_inc(S["qw_in"], 16)
            for h in range(NKV):
                act.dma_start(qw[:, QD + h * HD:QD + (h + 1) * HD], k_norm.to_broadcast([P, HD])).then_inc(S["qw_in"], 16)
            act.wait_ge(S["c_in"], 32)
            nc.scalar.activation(cp_h[:], cp_t[:], ACT.Tanh, scale=0.5)
            nc.scalar.activation(cs_h[:], cs_t[:], ACT.Tanh, scale=0.5).then_inc(S["c_tanh"], 1)
            act.wait_ge(S["lam_exp"], 1)
            nc.scalar.activation(lam8[:, :, 1], lam8[:, :, 1], ACT.Exp, scale=-1.0).then_inc(S["lam_one"], 1)
            act.wait_ge(S["gate_w_zero"], 1)
            for g, w in enumerate((gate_a_w, gate_x_w)):
                for two in range(2):
                    act.dma_start(gwt[64 * two:64 * two + 64, g, :, 64 * two:64 * two + 64],
                                  w[0].rearrange("(c two) i j -> two i c j", two=2)[two]).then_inc(S["gate_w_in"], 16)
            act.wait_ge(S["mod_row_ready"], 4)
            act.dma_start(mod_d[:, 0:2 * D], adab[:, 0:2 * D]).then_inc(S2["mod_st"][0], 16)
            act.wait_ge(S["mod_row_ready"], NCH)
            act.dma_start(mod_d[:, 2 * D:], adab[:, 2 * D:]).then_inc(S2["mod_st"][1], 16)

            def sumsq(i, par, half, n=P):
                act.wait_ge(S2["x_in"][par], 16 * (half + 1))
                nc.scalar.activation(sqj[0:n], xin[0:n, par], ACT.Square, scale=D ** -0.5, accum_out=ssq[0:n, par:par + 1]).then_inc(S["ssq_ready"], 1)

            def hT_out(i, n=P):
                act.wait_ge(S["hT_psum"], i + 1)
                nc.scalar.activation(hT[:, :, 0:n], psT[:].rearrange("p (k t) -> p k t", k=KC)[:, :, 0:n], ACT.Copy).then_inc(S["hT_ready"], 1)

            def exps(n, h):
                act.wait_ge(S["m_ready"], 2 * n + h + 1)
                nc.scalar.activation(esum[:, h, 1], mx[:, h, 2], ACT.Exp)
                for g in range(GQ):
                    last = nc.scalar.activation(sc[:, h, g], sc[:, h, g], ACT.Exp, bias=mx[:, h, 1, g:g + 1],
                                                accum_out=esum[:, h, 0, g:g + 1])
                last.then_inc(S["p_ready"], 1)

            def pT_out(n, h, first=False):
                act.wait_ge(S["pT_psum"], 2 * n + h + 1)
                if not (first and h == 0):
                    act.wait_ge(S["o_psum"], 2 * n + h)
                nc.scalar.activation(PT[:].rearrange("p g b t -> p (g b t)"), psT[:], ACT.Copy).then_inc(S["pT_ready"], 1)

            def oT_out(n, first=False):
                act.wait_ge(S["oT_psum"], n + 1)
                if not first:
                    act.wait_ge(S["oT_st"], 16 * n)
                nc.scalar.activation(oT[:].rearrange("p c t -> p (c t)"), psS[:, 0:512], ACT.Copy).then_inc(S["oT_ready"], 1)

            def step(i, par, half, proj=True, att=True, nxt=True, first=False, n=P, n_next=P):
                a = i - 1
                if nxt:
                    sumsq(i + 1, 1 - par, half + par, n_next)
                if proj:
                    act.wait_ge(S["xr_psum"], i + 1)
                    if not (isinstance(i, int) and i == 0):
                        act.wait_ge(S["conv_ready"], i)
                    if n == P:
                        nc.scalar.activation(xrb[:, :, HALO:HALO + P], psP[:, 0:512].rearrange("p (c t) -> p c t", c=RC),
                                             ACT.Copy).then_inc(S["xr_ready"], 1)
                    else:
                        for c in range(RC):
                            last = nc.scalar.activation(
                                xrb[:, c, 0:NS * (TS + HALO)].rearrange("p (b t) -> p b t", b=NS)[:, :, HALO:],
                                psP[:, c * P:c * P + n].rearrange("p (b t) -> p b t", b=NS), ACT.Copy)
                        last.then_inc(S["xr_ready"], 1)
                if att:
                    act.wait_ge(S["qkT_psum"], a + 1)
                    nc.scalar.activation(qT[:, 0:4].rearrange("p c t -> p (c t)"), psT[:, 0:512], ACT.Copy)
                    nc.scalar.activation(kT[:, 1 - par], psT[:, 512:640], ACT.Copy).then_inc(S["qkT_ready"], 1)
                if proj:
                    act.wait_ge(S["yr_psum"], i + 1)
                    if not (isinstance(i, int) and i == 0):
                        act.wait_ge(S["outr_ready"], i)
                    yps = psP[:, 512:1024].rearrange("p (c t) -> p c t", c=RC)[:, :, 0:n]
                    nc.scalar.activation(y_t[:, :, 0:n], yps, ACT.Copy)
                    nc.scalar.activation(sq_t[:, :, 0:n], yps, ACT.Square).then_inc(S["y_ready"], 1)
                if att:
                    exps(a, 0)
                if proj:
                    act.wait_ge(S["gates_sum"], i + 1)
                    nc.scalar.activation(gts[:, :, 0:n], gts[:, :, 0:n], ACT.Tanh, scale=0.5).then_inc(S["gates_tanh"], 1)
                if att:
                    pT_out(a, 0, first)
                if proj:
                    act.wait_ge(S["loga_ready"], i + 1)
                    nc.scalar.activation(a_t[:, :, 0:n], b_t[:, :, 0:n], ACT.Exp)
                    nc.scalar.activation(th_t[:, :, 0:n], b_t[:, :, 0:n], ACT.Tanh).then_inc(S["a_ready"], 1)
                if att:
                    exps(a, 1)
                if proj:
                    act.wait_ge(S["gelu_in"], i + 1)
                    nc.scalar.activation(sq_t[:, :, 0:n], sq_t[:, :, 0:n], ACT.Tanh, scale=GELU_C).then_inc(S["gelu_tanh"], 1)
                if att:
                    pT_out(a, 1, first)
                if proj:
                    act.wait_ge(S["b2_ready"], i + 1)
                    nc.scalar.activation(b_t[:, :, 0:n], b_t[:, :, 0:n], ACT.Sqrt).then_inc(S["bsqrt_ready"], 1)
                    act.wait_ge(S["qkv2_psum"], i + 1)
                    if att:
                        act.wait_ge(S["v_ready"], i)
                        act.wait_ge(S["qn_ready"], i)
                    if n != P:
                        act.wait_ge(S["kwin_st"], 32)
                    nc.scalar.activation(qkv[0:n], psQ[0:n, 0:QKV], ACT.Copy).then_inc(S["qkv_ready"], 1)
                if nxt:
                    hT_out(i + 1, n_next)
                if att:
                    oT_out(a, first)

            sumsq(0, 0, 0)
            hT_out(0)
            act.wait_ge(S2["mod_st"][1], 16)
            step(0, 0, 0, att=False)
            step(1, 1, 0, first=True)
            with act.Fori(1, NT // 2 - 1) as j:
                for s in range(2):
                    step(2 * j + s, s, j)
            step(NT - 2, 0, NT // 2 - 1)
            step(NT - 1, 1, NT // 2 - 1, n_next=TAIL)
            step(NT, 0, NT // 2, nxt=False, n=TAIL)
            act.wait_ge(S["smp_dve"], SMP_Q0)
            act.wait_ge(S["qkT_psum"], NT + 1)
            nc.scalar.activation(kTn[:], psT[:, 4 * P:4 * P + TAIL], ACT.Copy)
            for g in range(GQ):
                last = nc.scalar.activation(qTs[:, :, g * TS:(g + 1) * TS], psT[:, g * P:g * P + TAIL].rearrange("p (b t) -> p b t", b=NS),
                                            ACT.Copy)
            last.then_inc(S["qkT_ready"], 1)
            def wout_hi(k0, k1):
                for k in range(k0, k1):
                    nc.scalar.activation(wohi[:, k], wout[:, k], ACT.Copy).then_inc(S["b_hi"], 1)

            act.wait_ge(S["wB_in"], 16)
            wout_hi(0, 2)
            act.wait_ge(S["ckT_psum"], 1)
            nc.scalar.activation(kT8[:].rearrange("p b t -> p (b t)"), psP[:], ACT.Copy).then_inc(S["ckT_ready"], 1)
            wout_hi(2, 4)
            act.wait_ge(S["smp_dve"], SMP_M)
            nc.scalar.activation(mxS[:, 4], mxS[:, 2], ACT.Exp)
            for half in range(2):
                for h in range(NKV):
                    last = nc.scalar.activation(scS[:, half, h], scS[:, half, h], ACT.Exp, bias=mxS[:, 1, half, h:h + 1],
                                                accum_out=mxS[:, 3, half, h:h + 1])
            last.then_inc(S["smp_act"], 1)
            wout_hi(4, 5)
            act.wait_ge(S["smp_psum"], SMP_PT)
            nc.scalar.activation(PTs[:].rearrange("p c t -> p (c t)"), psT[:, 0:512], ACT.Copy)
            nc.scalar.activation(PTn[:].rearrange("p c t -> p (c t)"), psT[0:TAIL, 512:1024], ACT.Copy).then_inc(S["smp_act"], 1)
            wout_hi(5, KC)
            act.wait_ge(S["smp_psum"], SMP_OT)
            for g in range(GQ):
                last = nc.scalar.activation(oTs[:, g].rearrange("p (b t) -> p b t", b=NS),
                                            psT[:, 0:2 * P].rearrange("p (b r) -> p b r", b=NS)[:, :, g * TS:(g + 1) * TS], ACT.Copy)
            last.then_inc(S["smp_act"], 1)
            act.wait_ge(S2["mix_in"][0], 16)
            nc.scalar.activation(mxhi[:], mixb[:, 0], ACT.Copy).then_inc(S["b_hi"], 1)
            act.wait_ge(S["smp_act"], SMP_OT_OUT)
            for g in range(GQ):
                for h in range(NKV):
                    head = h * GQ + g
                    act.dma_start(mix_d[NT, (head % 2) * HD:(head % 2) * HD + HD, RC + head // 2, 0:TAIL],
                                  oTs[h * HD:(h + 1) * HD, g]).then_inc(S["smp_oT_st"], 16)

            def mix_hi(i, par, half):
                act.wait_ge(S2["mix_in"][par], 16 * half + 16)
                nc.scalar.activation(mxhi[:], mixb[:, par], ACT.Copy).then_inc(S["b_hi"], 1)

            def step_b(i, par, half, d0=True, d1=True, d2=True, n0=P, n1=P, n2=P, st=None):
                if d2:
                    act.wait_ge(S["pos_psum"], i - 1)
                    nc.scalar.activation(actT[:, :, 0:n2], psP[:, 768:1024].rearrange("p (j t) -> p j t", j=2)[:, :, 0:n2], ACT.Copy)
                    nc.scalar.activation(pos_all[:, i - 2], psP[:, 640:640 + NE], ACT.Copy).then_inc(S["actT_ready"], 1)
                if d1:
                    act.wait_ge(S["h2T_psum"], i)
                    nc.scalar.activation(h2T[:, :, 0:n1], psT[:].rearrange("p (k t) -> p k t", k=KC)[:, :, 0:n1], ACT.Copy).then_inc(S["h2T_ready"], 1)
                    act.wait_ge(S["router_psum"], i)
                    nc.scalar.activation(rt_s[0:n1], psP[0:n1, 512:512 + NE], ACT.Tanh, scale=0.5).then_inc(S["rtanh"], 1)
                if d0:
                    act.wait_ge(S["x2_ready"], i + 1)
                    nc.scalar.activation(sqB[0:n0], x2[0:n0, par], ACT.Square, scale=D ** -0.5, accum_out=ssqB[0:n0, 0:1]).then_inc(S["ssqB_ready"], 1)
                    if n0 == P:
                        mix_hi(i + 1, 1 - par, half + par)
                if d1:
                    act.wait_ge(S["shup_psum"], i)
                    nc.scalar.activation(sg[0:n1, 0], psP[0:n1, 0:F], ACT.Tanh, scale=0.5).then_inc(S["shtanh"], 1)
                if d2:
                    act.wait_ge(S["shd_psum"], i - 1)
                    if st is not None:
                        act.wait_ge(S2["sh_st"][par], st)
                    nc.scalar.activation(sho[0:n2, par], psS[0:n2], ACT.Copy).then_inc(S["sh_ready"], 1)

            step_b(0, 0, 0, d1=False, d2=False)
            step_b(1, 1, 0, d2=False)
            step_b(2, 0, 1)
            step_b(3, 1, 1)
            with act.Fori(2, NT // 2) as j:
                for s in range(2):
                    step_b(2 * j + s, s, j, st=16 * j - 16)
            step_b(NT, 0, 0, n0=TAIL, st=8 * NT - 16)
            step_b(NT + 1, 1, 0, d0=False, n1=TAIL, st=8 * NT - 16)
            step_b(NT + 2, 0, 0, d0=False, d1=False, n2=TAIL, st=8 * NT)

            def x_hi(b, s):
                act.wait_ge(S["xgT_psum"], b + 1)
                nc.scalar.activation(xThi[:, s].rearrange("p k t -> p (k t)"), psT[:], ACT.Copy).then_inc(S["xThi_ready"], 1)

            def tanh_d(b, s):
                act.wait_ge(S["up_psum"], b + 1)
                nc.scalar.activation(sgD[:, s], psP[:, s * 512:s * 512 + F], ACT.Tanh, scale=0.5).then_inc(S["dtanh"], 1)

            def a_hi(b):
                act.wait_ge(S["dactT_psum"], b + 1)
                nc.scalar.activation(aThi[:].rearrange("p j t -> p (j t)"), psQ[:, 0:F], ACT.Copy).then_inc(S["aThi_ready"], 1)

            def gu_hi(n, b=None):
                act.wait_ge(S["w_gu_in"], n * 32 + 32)
                if b is not None:
                    act.wait_ge(S["up_psum"], b)
                sl = bass.ds(n % 2, 1)
                for c in range(4):
                    nc.scalar.activation(whi[:, sl, c * 1024:(c + 1) * 1024], wraw[:, sl, c * 1024:(c + 1) * 1024], ACT.Copy).then_inc(S["hi_gu"], 1)

            def dn_hi(n, b=None):
                act.wait_ge(S["w_dn_in"], n * 16 + 16)
                if b is not None:
                    act.wait_ge(S["down_psum"], b)
                sl = bass.ds(n % 2, 1)
                for c in range(4, 6):
                    nc.scalar.activation(whi[:, sl, c * 1024:(c + 1) * 1024], wraw[:, sl, c * 1024:(c + 1) * 1024], ACT.Copy).then_inc(S["hi_dn"], 1)

            def next_gu(b, first=False):
                n = act.value_load(blkr[0:1, bass.ds(b, 1), 2:3], min_val=0, max_val=NE - 1)
                with act.If(n > 0):
                    gu_hi(n, None if first else b)

            def next_dn(b, first=False):
                n = act.value_load(blkr[0:1, bass.ds(b, 1), 2:3], min_val=0, max_val=NE - 1)
                with act.If(n > 0):
                    dn_hi(n, None if first else b)

            def y_out(b, s, stored=None):
                act.wait_ge(S["down_psum"], b + 1)
                if stored is not None:
                    act.wait_ge(S["add_st"], stored)
                nc.scalar.activation(six[:, s], tok_all[:, bass.ds(b, 1)], ACT.Copy)
                nc.scalar.activation(ysb[:, s], psS[:], ACT.Copy, scale=w_all[:, bass.ds(b, 1)]).then_inc(S["ysb_ready"], 1)

            def load_list(b, s, half=0, free=True):
                row = act.value_load(blkr[0:1, bass.ds(b, 1), 1:2], min_val=0, max_val=NE * LB)
                if free:
                    act.wait_ge(S2["gather_in"][s], half * 16)
                    act.wait_ge(S["lent_used"], b - 1)
                act.dma_start(lent[:, s], list_d[bass.ds(row * P, P)]).then_inc(S2["lent_in"][s], 16)

            act.wait_ge(S["blkr_in"], 16)
            for par in range(2):
                act.wait_ge(S2["list_st"][par], 16 * TOPK * (NT // 2 + 1 - par))
            load_list(0, 0, free=False)
            load_list(1, 1, free=False)
            load_list(2, 0, 1)
            load_list(3, 1, 1)
            gu_hi(0)
            dn_hi(0)
            x_hi(0, 0)
            load_list(4, 0, 2)
            x_hi(1, 1)
            load_list(5, 1, 2)
            next_gu(0, first=True)
            tanh_d(0, 0)
            last_pair = act.value_load(nblk[0:1, 0:1], min_val=0, max_val=NB // 2 - 1)
            next_gu(1)
            a_hi(0)
            x_hi(2, 0)
            tanh_d(1, 1)
            next_gu(2)
            next_dn(0, first=True)
            y_out(0, 0)

            def d_step(b, s, half, stored):
                a_hi(b - 1)
                load_list(b + 4, s, half + 2)
                x_hi(b + 1, 1 - s)
                tanh_d(b, s)
                next_dn(b - 1)
                next_gu(b + 1)
                y_out(b - 1, 1 - s, stored)

            d_step(2, 0, 1, None)
            d_step(3, 1, 1, 16)
            with act.Fori(2, NB // 2) as j:
                with act.If(j < last_pair + 1):
                    for s in range(2):
                        d_step(2 * j + s, s, j, 32 * j + 16 * s - 32)
            a_hi(last_pair * 2 + 1)
            y_out(last_pair * 2 + 1, 1, last_pair * 32)

            def store_e(t, s, n=P):
                act.wait_ge(S["ye_ready"], t + 1)
                dst = y_prompt[0, bass.ds(t * P, P)] if n == P else y_sample.rearrange("b t d -> (b t) d")
                act.dma_start(dst, ye[0:n, s]).then_inc(S4["out_st"][s], 16)

            with act.Fori(0, NT // 4) as q:
                for s in range(4):
                    store_e(4 * q + s, s)
            store_e(NT, 0, TAIL)

        @block.vector
        def _(dve):
            V = nc.vector
            V.memset(gwt[:], 0.0).then_inc(S["gate_w_zero"], 1)
            dve.sem_inc(S["mod_bank_free"], 2)
            dve.wait_ge(S["c_tanh"], 1)
            V.scalar_tensor_tensor(cp_h[:], cp_h[:], 1.0, cp_t[:], ALU.add, ALU.mult)
            V.scalar_tensor_tensor(cs_h[:], cs_h[:], 1.0, cs_t[:], ALU.add, ALU.mult)
            dve.drain()
            for t in range(TS):
                V.tensor_scalar(csil[:, :, 0:TAIL].rearrange("p k (b t) -> p k b t", t=TS)[:, :, :, t],
                                cs_h[:].rearrange("p b k -> p k b"), 0.5, None, ALU.mult)
            V.tensor_scalar(csil[:, :, TAIL], cp_h[:], 0.5, None, ALU.mult).then_inc(S["csil_ready"], 1)
            dve.wait_ge(S["norms_in"], 48)
            def mod_row(n):
                dve.wait_ge(S["ada_psum_ready"], n + 1)
                sect, row = n * 512 // D, adab[:, n * 512:(n + 1) * 512]
                src = psT[0:TAIL + 1, (n % 2) * 512:(n % 2) * 512 + 512]
                if sect in (1, 4):
                    V.tensor_tensor(row, src, row, ALU.add)
                    dve.drain()
                    V.scalar_tensor_tensor(row, row, 1.0,
                                           gmix[:, sect // 4, (n % 2) * 512:(n % 2) * 512 + 512], ALU.add,
                                           ALU.mult).then_inc(S["mod_row_ready"], 1)
                else:
                    V.tensor_tensor(row, src, row, ALU.add).then_inc(S["mod_row_ready"], 1)
                dve.drain().then_inc(S["mod_bank_free"], 1)

            for n in range(4):
                mod_row(n)
            dve.wait_ge(S["prm_psum"], 1)
            V.tensor_copy(prm[:], psP[:, 0:RC * 40].rearrange("p (c n) -> p c n", n=40)).then_inc(S["prm_ready"], 1)
            dve.drain()
            V.tensor_copy(gb[:, 0:RC], prm[:, :, 5])
            V.tensor_copy(gb[:, RC:2 * RC], prm[:, :, 6])
            V.tensor_scalar(lam8[:, :, 0], prm[:, :, 7], -1.0, None, ALU.mult)
            dve.drain()
            V.tensor_tensor(lam8[:, :, 1], lam8[:, :, 0], prm[:, :, 7], ALU.max).then_inc(S["lam_exp"], 1)
            dve.wait_ge(S["const_ready"], CONST_ROWS)
            V.tensor_scalar(pid[:, 1:2], pid[:, 0:1], TS - 1, None, ALU.bitwise_and)
            V.tensor_scalar(pid[:, 2:3], pid[:, 0:1], 5, None, ALU.arith_shift_right)
            V.tensor_scalar(pid[:, 3:4], pid[:, 0:1], 2, None, ALU.arith_shift_right)
            for h in range(NH):
                V.memset(gtmp[:, 0, h:h + 1], -(2.0 ** (-8.0 * (h + 1) / NH)))
            dve.drain()
            V.tensor_scalar(pid[:, 4:5], pid[:, 3:4], GQ - 1, None, ALU.bitwise_and)
            V.tensor_copy(smc[:, 0:1], pid[:, 1:2])
            V.tensor_copy(smc[:, 10:11], pid[:, 2:3])
            dve.drain()
            V.tensor_copy(smc[:, 9:10], pid[:, 4:5])
            V.scalar_tensor_tensor(smc[:, 1:2], smc[:, 10:11], float(TS), smc[:, 0:1], ALU.mult, ALU.add)
            dve.drain()
            V.tensor_scalar(smc[:, 2:3], smc[:, 1:2], float(TS * NS // 2), None, ALU.add)
            for g in range(GQ):
                V.tensor_scalar(gsel[:, 0, g:g + 1], smc[:, 9:10], float(g), None, ALU.is_equal)
            dve.wait_ge(S["sink_in"], 16)
            dve.drain()
            gs = gsel[:, 0].unsqueeze(1).to_broadcast([P, NKV, GQ])
            for k, src in ((0, gtmp[:, 0]), (1, sink[:])):
                V.tensor_tensor(gtmp[:, k].rearrange("p (h g) -> p h g", h=NKV), src.rearrange("p (h g) -> p h g", h=NKV), gs, ALU.mult)
                dve.drain()
                V.tensor_reduce(smc[:, 3 + 2 * k:5 + 2 * k], gtmp[:, k].rearrange("p (h g) -> p h g", h=NKV), AX.X, ALU.add)
            dve.wait_ge(S["lam_one"], 1)
            e, z, w, s_ = lam8[:, :, 1], hs_t[:, :, 0], hs_t[:, :, 1], hs_t[:, :, 2]
            V.tensor_scalar(z, e, 2.0, None, ALU.add)
            dve.drain()
            V.reciprocal(z, z)
            dve.drain()
            V.tensor_tensor(z, z, e, ALU.mult)
            dve.drain()
            V.tensor_tensor(w, z, z, ALU.mult)
            V.memset(s_, 1.0 / 17.0)
            for c in (15.0, 13.0, 11.0, 9.0, 7.0, 5.0, 3.0, 1.0):
                dve.drain()
                V.tensor_tensor(s_, s_, w, ALU.mult)
                dve.drain()
                V.tensor_scalar(s_, s_, 1.0 / c, None, ALU.add)
            dve.drain()
            V.scalar_tensor_tensor(s_, s_, 2.0, z, ALU.mult, ALU.mult)
            V.tensor_scalar(lam8[:, :, 0], lam8[:, :, 0], 0.0, None, ALU.max)
            dve.drain()
            V.tensor_tensor(s_, s_, lam8[:, :, 0], ALU.add)
            dve.drain()
            V.tensor_scalar(lam8[:, :, 0], s_, -0.5 * LRU_C, None, ALU.mult)
            for n in range(4, NCH):
                mod_row(n)
            V.memset(xrb[:, :, 0:HALO], 0.0)
            V.memset(hlast[:], 0.0)
            dve.drain()

            def h_of(i, par, n=P, first=False):
                dve.wait_ge(S["rstd_ready"], i + 1)
                if not first:
                    dve.wait_ge(S["hT_psum"], i)
                V.scalar_tensor_tensor(hrow[0:n], xin[0:n, par], rst[0:n, par:par + 1], modA[0:n, 1], ALU.mult, ALU.mult)
                dve.drain()
                V.tensor_tensor(hrow[0:n], hrow[0:n], modA[0:n, 0], ALU.add).then_inc(S["h_ready"], 1)

            def conv(i):
                dve.wait_ge(S["xr_ready"], i + 1)
                for c in range(RC):
                    V.tensor_scalar(u[:, c], xrb[:, c, 0:P], prm[:, c, 0:1], prm[:, c, 4:5], ALU.mult, ALU.add)
                for t in range(1, HALO + 1):
                    dve.drain()
                    for c in range(RC):
                        V.scalar_tensor_tensor(u[:, c], xrb[:, c, t:t + P], prm[:, c, t:t + 1], u[:, c], ALU.mult, ALU.add)
                dve.drain()
                V.tensor_copy(xrb[:, :, 0:HALO], xrb[:, :, P:P + HALO])
                dve.drain().then_inc(S["conv_ready"], 1)

            def conv_tail(i):
                def view(ap, t0, n):
                    return ap[:, 0:NS * (TS + HALO)].rearrange("p (b t) -> p b t", b=NS)[:, :, t0:t0 + n]
                dve.wait_ge(S["xr_ready"], i + 1)
                uv = [u[:, c, 0:TAIL].rearrange("p (b t) -> p b t", b=NS) for c in range(RC)]
                for c in range(RC):
                    V.tensor_copy(view(xrb[:, c], 0, HALO), prm[:, c, 8:8 + NS * HALO].rearrange("p (b j) -> p b j", b=NS))
                dve.drain()
                for c in range(RC):
                    V.tensor_scalar(uv[c], view(xrb[:, c], 0, TS), prm[:, c, 0:1], prm[:, c, 4:5], ALU.mult, ALU.add)
                for t in range(1, HALO + 1):
                    dve.drain()
                    for c in range(RC):
                        V.scalar_tensor_tensor(uv[c], view(xrb[:, c], t, TS), prm[:, c, t:t + 1], uv[c], ALU.mult, ALU.add)
                for c in range(RC):
                    V.tensor_copy(stt[:, c, HALO + 1:HALO + 1 + NS * HALO].rearrange("p (b j) -> p b j", b=NS), view(xrb[:, c], TS, HALO))
                dve.drain().then_inc(S["conv_ready"], 1)

            def scores(n, h, first=False):
                dve.wait_ge(S["s_psum"], 2 * n + h + 1)
                hs = slice(GQ * h, GQ * h + GQ)
                s_in = psS[:].rearrange("p (g j) -> p g j", g=GQ)
                if first:
                    V.memset(sc[:, h, :, 0:P], NEG)
                    V.scalar_tensor_tensor(sc[:, h, :, P:], s_in[:, :, P:], HD ** -0.5, bias[:, hs, P:], ALU.mult, ALU.add)
                else:
                    V.scalar_tensor_tensor(sc[:, h], s_in, HD ** -0.5, bias[:, hs], ALU.mult, ALU.add)
                dve.drain().then_inc(S["s_read"], 1)
                V.tensor_reduce(mx[:, h, 0], sc[:, h], AX.X, ALU.max)
                dve.drain()
                V.tensor_tensor(mx[:, h, 0], mx[:, h, 0], sink[:, hs], ALU.max)
                dve.drain()
                V.tensor_scalar(mx[:, h, 1], mx[:, h, 0], -1.0, None, ALU.mult)
                V.tensor_tensor(mx[:, h, 2], sink[:, hs], mx[:, h, 0], ALU.subtract)
                dve.drain().then_inc(S["m_ready"], 1)

            def o_out(n, h):
                dve.wait_ge(S["o_psum"], 2 * n + h + 1)
                V.tensor_tensor(mx[:, h, 3], esum[:, h, 0], esum[:, h, 1], ALU.add)
                dve.drain()
                V.reciprocal(mx[:, h, 3], mx[:, h, 3])
                dve.drain()
                V.tensor_tensor(orow[:, 256 * h:256 * h + 256].rearrange("p (g d) -> p g d", g=GQ),
                                psQ[:, 768:1024].rearrange("p (g d) -> p g d", g=GQ), bc(mx[:, h, 3], HD),
                                ALU.mult).then_inc(S["o_ready"], 1)

            def step(i, par, proj=True, att=True, nxt=True, first=False, n=P, n_next=P):
                a = i - 1
                tail = n != P
                if proj:
                    (conv_tail if tail else conv)(i)
                if att:
                    if not first:
                        dve.wait_ge(S["o_psum"], 2 * a)
                    V.tensor_copy(vb[:, 1 - par], qkv[:, QD + KVD:]).then_inc(S["v_ready"], 1)
                    scores(a, 0, first)
                if nxt:
                    if n_next != P:
                        dve.wait_ge(S["tailmod_in"], 16)
                    h_of(i + 1, 1 - par, n_next)
                if proj:
                    dve.wait_ge(S["gates_psum"], i + 1)
                    V.tensor_tensor(gts[:, :, 0:n], psP[:].rearrange("p (c t) -> p c t", t=P)[:, :, 0:n], bc(gb[:], n),
                                    ALU.add).then_inc(S["gates_sum"], 1)
                    dve.wait_ge(S["y_ready"], i + 1)
                    V.tensor_scalar(sq_t[:, :, 0:n], sq_t[:, :, 0:n], GELU_A, 1.0, ALU.mult, ALU.add)
                    dve.drain()
                    V.tensor_tensor(sq_t[:, :, 0:n], sq_t[:, :, 0:n], y_t[:, :, 0:n], ALU.mult).then_inc(S["gelu_in"], 1)
                    dve.wait_ge(S["gates_tanh"], i + 1)
                    V.scalar_tensor_tensor(b_t[:, :, 0:n], gts[:, 0:RC, 0:n], 1.0, bc(lam8[:, :, 0], n), ALU.add,
                                           ALU.mult).then_inc(S["loga_ready"], 1)
                    V.scalar_tensor_tensor(gts[:, RC:, 0:n], gts[:, RC:, 0:n], 1.0, u[:, :, 0:n], ALU.add, ALU.mult)
                if att:
                    scores(a, 1, first)
                    o_out(a, 0)
                if proj:
                    dve.wait_ge(S["a_ready"], i + 1)
                    V.tensor_scalar(b_t[:, :, 0:n], th_t[:, :, 0:n], -1.0, 1.0, ALU.mult, ALU.add)
                    dve.drain()
                    V.reciprocal(b_t[:, :, 0:n], b_t[:, :, 0:n])
                    dve.drain()
                    V.scalar_tensor_tensor(b_t[:, :, 0:n], th_t[:, :, 0:n], -2.0, b_t[:, :, 0:n], ALU.mult,
                                           ALU.mult).then_inc(S["b2_ready"], 1)
                    dve.wait_ge(S["gelu_tanh"], i + 1)
                    V.scalar_tensor_tensor(sq_t[:, :, 0:n], sq_t[:, :, 0:n], 1.0, y_t[:, :, 0:n], ALU.add, ALU.mult)
                    dve.wait_ge(S["bsqrt_ready"], i + 1)
                    V.scalar_tensor_tensor(b_t[:, :, 0:n], gts[:, RC:, 0:n], 0.5, b_t[:, :, 0:n], ALU.mult, ALU.mult)
                    dve.drain()
                    if tail:
                        at_, bt_, ht_ = (x[:, :, 0:TAIL].rearrange("p c (b t) -> p c b t", b=NS) for x in (a_t, b_t, hs_t))
                        for t in range(TS):
                            prev = prm[:, :, 8 + NS * HALO:8 + NS * HALO + NS] if t == 0 else ht_[:, :, :, t - 1]
                            V.tensor_tensor(ht_[:, :, :, t], at_[:, :, :, t], prev, ALU.mult)
                            dve.drain()
                            V.tensor_tensor(ht_[:, :, :, t], ht_[:, :, :, t], bt_[:, :, :, t], ALU.add)
                            dve.drain()
                        V.tensor_copy(stt[:, :, HALO + 1 + NS * HALO:], ht_[:, :, :, TS - 1])
                    else:
                        for c in range(RC):
                            V.tensor_tensor_scan(hs_t[:, c], a_t[:, c], b_t[:, c], hlast[:, c], ALU.mult, ALU.add)
                        dve.drain()
                        V.tensor_copy(hlast[:], hs_t[:, :, P - 1:P])
                    if att:
                        dve.wait_ge(S["outr_st"], 16 * i)
                    V.scalar_tensor_tensor(outr[:, :, 0:n], sq_t[:, :, 0:n], 0.5, hs_t[:, :, 0:n], ALU.mult, ALU.mult)
                    dve.drain().then_inc(S["outr_ready"], 1)
                if att:
                    o_out(a, 1)
                if proj:
                    dve.wait_ge(S["qkv_ready"], i + 1)
                    if att:
                        dve.wait_ge(S["qkT_psum"], i)
                    if tail:
                        dve.wait_ge(S["kwin_st"], 32)
                    q3 = qkv[0:n, 0:QD + KVD].rearrange("p (h d) -> p h d", d=HD)
                    n3 = qn[0:n].rearrange("p (h d) -> p h d", d=HD)
                    V.scalar_tensor_tensor(qn[0:n], qkv[0:n, 0:QD + KVD], 1.0 / HD, qkv[0:n, 0:QD + KVD], ALU.mult, ALU.mult)
                    dve.drain()
                    V.tensor_reduce(ss10[0:n, 0:NH + NKV], n3, AX.X, ALU.add).then_inc(S["ss10_ready"], 1)
                    dve.wait_ge(S["r10_ready"], i + 1)
                    V.tensor_tensor(q3, q3, bc(r10[0:n, 0:NH + NKV], HD), ALU.mult)
                    dve.drain()
                    for v in range(NKV):
                        V.tensor_tensor(qn[0:n, 0:QD].rearrange("p (g v d) -> p v g d", v=NKV, g=GQ)[:, v],
                                        qkv[0:n, v * GQ * HD:(v + 1) * GQ * HD].rearrange("p (g d) -> p g d", g=GQ),
                                        qw[0:n, v * GQ * HD:(v + 1) * GQ * HD].rearrange("p (g d) -> p g d", g=GQ), ALU.mult)
                    V.tensor_tensor(qn[0:n, QD:], qkv[0:n, QD:QD + KVD], qw[0:n, QD:], ALU.mult).then_inc(S["qn_ready"], 1)

            dve.wait_ge(S["modA_in"], 16)
            dve.wait_ge(S["sink_in"], 16)
            dve.wait_ge(S["const_ready"], CONST_BIAS)
            dve.wait_ge(S["qw_in"], 16 * (NH + NKV))
            h_of(0, 0, first=True)
            dve.wait_ge(S2["mod_st"][1], 16)
            step(0, 0, att=False)
            step(1, 1, first=True)
            with dve.Fori(1, NT // 2 - 1) as j:
                for s in range(2):
                    step(2 * j + s, s)
            step(NT - 2, 0)
            step(NT - 1, 1, n_next=TAIL)
            V.tensor_copy(stt[:, :, 0:HALO], xrb[:, :, 0:HALO])
            V.tensor_copy(stt[:, :, HALO:HALO + 1], hlast[:])
            dve.drain()
            step(NT, 0, nxt=False, n=TAIL)
            dve.wait_ge(S["smp_in"], 32)
            V.memset(qTs[:], 0.0).then_inc(S["smp_dve"], 1)
            V.tensor_scalar(distS[:, :, 0:P], jdist[:, 0:P].unsqueeze(1).to_broadcast([P, 2, P]), smc[:, 0:1], None, ALU.add)
            for half in range(2):
                V.tensor_scalar(distS[:, half, P:], jdist[:, P:], smc[:, 1 + half:2 + half], None, ALU.add)
            dve.drain()
            V.tensor_scalar(penS[:, :, 0:P], distS[:, :, 0:P], float(P), NEG, ALU.is_gt, ALU.mult)
            V.tensor_scalar(penS[:, :, P:], distS[:, :, P:], smc[:, 0:1], NEG, ALU.is_gt, ALU.mult)
            V.tensor_scalar(penT[:], distS[:], 0.0, NEG, ALU.is_lt, ALU.mult)
            dve.drain()
            V.tensor_tensor(penS[:], penS[:], penT[:], ALU.add)
            dve.drain()
            for h in range(NKV):
                V.scalar_tensor_tensor(biasS[:, :, h], distS[:], smc[:, 3 + h:4 + h], penS[:], ALU.mult, ALU.add)
            dve.wait_ge(S["small_psum"], 1)
            V.tensor_copy(stt_r[:], psQ[0:36, 0:512]).then_inc(S["small_ready"], 1)
            dve.drain()
            def wout_lo(k0, k1):
                for k in range(k0, k1):
                    dve.wait_ge(S["b_hi"], k + 1)
                    last = V.tensor_tensor(wolo[:, k], wout[:, k], wohi[:, k].bitcast(F32), ALU.subtract)
                return last

            wout_lo(0, 2)
            dve.wait_ge(S["smp_psum"], SMP_S)
            sS = psS[:].rearrange("p (h a j) -> p a h j", a=2, h=NKV)[:, :, :, 0:P + TAIL]
            for half in range(2):
                V.scalar_tensor_tensor(scS[:, half], sS[:, half], HD ** -0.5, biasS[:, half], ALU.mult, ALU.add)
            dve.drain()
            V.tensor_reduce(mxS[:, 0], scS[:], AX.X, ALU.max)
            dve.drain()
            snk = smc[:, 5:7].unsqueeze(1).to_broadcast([P, 2, NKV])
            V.tensor_tensor(mxS[:, 0], mxS[:, 0], snk, ALU.max)
            dve.drain()
            V.tensor_scalar(mxS[:, 1], mxS[:, 0], -1.0, None, ALU.mult)
            V.tensor_tensor(mxS[:, 2], snk, mxS[:, 0], ALU.subtract)
            dve.drain().then_inc(S["smp_dve"], 1)
            wout_lo(2, 4)
            dve.wait_ge(S["smp_act"], SMP_P)
            V.tensor_tensor(mxS[:, 5], mxS[:, 3], mxS[:, 4], ALU.add)
            dve.drain()
            V.reciprocal(mxS[:, 5], mxS[:, 5])
            dve.drain()
            wout_lo(4, 5)
            dve.wait_ge(S["smp_psum"], SMP_O)
            V.tensor_tensor(orowS[:].rearrange("p a (h d) -> p (a h) d", h=NKV), psQ[:, 768:1024].rearrange("p (c d) -> p c d", c=2 * NKV),
                            bc(mxS[:, 5].rearrange("p a h -> p (a h)"), HD), ALU.mult).then_inc(S["smp_dve"], 1)

            wout_lo(5, KC).then_inc(S["b_lo"], 1)
            dve.wait_ge(S["b_hi"], WO + 1)
            V.tensor_tensor(mxlo[:], mixb[:, 0], mxhi[:].bitcast(F32), ALU.subtract).then_inc(S["b_lo"], 1)
            dve.wait_ge(S["modB_in"], 16)
            dve.wait_ge(S["rbias_in"], 16)
            dve.wait_ge(S["const_ready"], CONST_B)
            V.memset(mrun[:], 0.0)
            V.memset(msk_all[:, NT], 0.0)
            dve.drain().then_inc(S["mrun_ready"], 1)

            def x2_of(i, par, half, n=P, st=None):
                dve.wait_ge(S["mixed_psum"], i + 1)
                dve.wait_ge(S2["xB_in"][par], 16 * half + 16)
                if st is not None:
                    dve.wait_ge(S2["x2_st"][par], st)
                V.tensor_tensor(x2[0:n, par], psQ[0:n], modB[0:n, 0], ALU.mult)
                dve.drain()
                V.tensor_tensor(x2[0:n, par], x2[0:n, par], xb[0:n, par], ALU.add)
                dve.drain().then_inc(S["x2_ready"], 1)

            def mix_lo(i, par):
                dve.wait_ge(S["b_hi"], WO + i + 1)
                V.tensor_tensor(mxlo[:], mixb[:, par], mxhi[:].bitcast(F32), ALU.subtract).then_inc(S["b_lo"], 1)

            def h2_of(i, par, half, n=P, first=False):
                dve.wait_ge(S["rstdB_ready"], i + 1)
                if not first:
                    dve.wait_ge(S2["h2_st"][1 - par], 16 * (half + par))
                    dve.wait_ge(S["h2T_psum"], i)
                V.scalar_tensor_tensor(h2[0:n], x2[0:n, par], ssqB[0:n, 1:2], modB[0:n, 2], ALU.mult, ALU.mult)
                dve.drain()
                V.tensor_tensor(h2[0:n], h2[0:n], modB[0:n, 1], ALU.add).then_inc(S["h2_ready"], 1)

            def shared_act(i, n=P):
                dve.wait_ge(S["shtanh"], i + 1)
                V.scalar_tensor_tensor(sg[0:n, 1], sg[0:n, 0], 1.0, psP[0:n, 0:F], ALU.add, ALU.mult)
                dve.drain()
                V.scalar_tensor_tensor(actr[0:n], sg[0:n, 1], 0.5, psP[0:n, F:2 * F], ALU.mult, ALU.mult).then_inc(S["act_ready"], 1)

            def route(t, n=P):
                dve.wait_ge(S["rtanh"], t + 1)
                V.tensor_scalar(rt_s[0:n], rt_s[0:n], 0.5, 0.5, ALU.mult, ALU.add)
                dve.drain()
                V.tensor_tensor(rt_b[0:n], rt_s[0:n], rbias[0:n], ALU.add)
                dve.drain()
                for g in range(NG):
                    V.max(rt_8[0:n, g], rt_b[0:n, g * GE:(g + 1) * GE])
                dve.drain()
                V.tensor_tensor(rt_g[0:n, 0], rt_8[0:n, :, 0], rt_8[0:n, :, 1], ALU.add)
                dve.drain()
                V.max(rt_g[0:n, 1], rt_g[0:n, 0])
                dve.drain()
                V.max_index(rt_u[0:n, 0], rt_g[0:n, 1], rt_g[0:n, 0])
                dve.drain()
                V.tensor_copy(rt_g[0:n, 2], rt_u[0:n, 0])
                dve.drain()
                g4 = rt_t[0:n, 0, 0:NG * TG].rearrange("p (g k) -> p g k", g=NG)
                V.tensor_tensor(g4, bc(iota[0:n, 0:NG], TG), rt_g[0:n, 2, 0:TG].unsqueeze(1).to_broadcast([n, NG, TG]), ALU.is_equal)
                dve.drain()
                V.tensor_reduce(rt_g[0:n, 3], g4, AX.X, ALU.add)
                dve.drain()
                V.tensor_scalar(rt_g[0:n, 0], rt_g[0:n, 3], -1.0, -NEG, ALU.add, ALU.mult)
                b3 = rt_b[0:n].rearrange("p (g e) -> p g e", g=NG)
                m3 = rt_m[0:n].rearrange("p (g e) -> p g e", g=NG)
                V.tensor_tensor(m3, b3, bc(rt_g[0:n, 3], GE), ALU.mult)
                dve.drain()
                V.tensor_tensor(m3, m3, bc(rt_g[0:n, 0], GE), ALU.add)
                dve.drain()
                V.max(rt_8[0:n, 0], rt_m[0:n])
                dve.drain()
                V.max_index(rt_u[0:n, 1], rt_8[0:n, 0], rt_m[0:n])
                dve.drain()
                V.tensor_copy(idxf[0:n], rt_u[0:n, 1])
                dve.drain()
                V.tensor_tensor(rt_oh[0:n], iota[0:n].unsqueeze(1).to_broadcast([n, TOPK, NE]), bc(idxf[0:n, 0:TOPK], NE), ALU.is_equal)
                dve.drain()
                V.tensor_tensor(rt_t[0:n], rt_oh[0:n], rt_s[0:n].unsqueeze(1).to_broadcast([n, TOPK, NE]), ALU.mult)
                V.tensor_reduce(msk_all[0:n, t], rt_oh[0:n].rearrange("p k e -> p e k"), AX.X, ALU.add).then_inc(S["msk_ready"], 1)
                dve.drain()
                V.tensor_reduce(wgt[0:n, 0:TOPK], rt_t[0:n], AX.X, ALU.add)
                dve.drain()
                V.tensor_reduce(rt_g[0:n, 1, 0:1], wgt[0:n, 0:TOPK], AX.X, ALU.add)
                dve.drain()
                V.reciprocal(rt_g[0:n, 1, 1:2], rt_g[0:n, 1, 0:1])
                dve.drain()
                V.tensor_scalar(wgt[0:n, 0:TOPK], wgt[0:n, 0:TOPK], rt_g[0:n, 1, 1:2], ROUTE_SCALE, ALU.mult, ALU.mult)
                dve.drain()

            def add_mask(t):
                dve.wait_ge(S["pos_psum"], t + 1)
                V.tensor_tensor(mrun[:], mrun[:], msk_all[:, t], ALU.add)
                dve.drain().then_inc(S["mrun_ready"], 1)

            def entries(t, par, st, n=P):
                dve.wait_ge(S["actT_ready"], t + 1)
                V.tensor_tensor(rt_t[0:n], rt_oh[0:n], pos_all[0:n, t].unsqueeze(1).to_broadcast([n, TOPK, NE]), ALU.mult)
                dve.drain()
                if st is not None:
                    dve.wait_ge(S2["list_st"][par], st)
                V.tensor_reduce(posk[0:n, par, 0, 0:TOPK], rt_t[0:n], AX.X, ALU.add)
                V.tensor_scalar(posk[0:n, par, 1, 0:TOPK], idxf[0:n, 0:TOPK], float(LB * P), None, ALU.mult)
                V.tensor_copy(entry[0:n, par, :, 0], tokf[0:n, bass.ds(t, 1)].to_broadcast([n, TOPK]))
                V.tensor_copy(entry[0:n, par, :, 1].bitcast(F32), wgt[0:n, 0:TOPK])
                dve.drain()
                V.tensor_tensor(posk[0:n, par, 0, 0:TOPK], posk[0:n, par, 0, 0:TOPK], posk[0:n, par, 1, 0:TOPK], ALU.add)
                dve.drain()
                V.tensor_copy(dsti[0:n, par, 0:TOPK], posk[0:n, par, 0, 0:TOPK])
                dve.drain().then_inc(S["entry_ready"], 1)

            def step_b(i, par, half, d0=True, d1=True, d2=True, n0=P, n1=P, n2=P, st=None, lst=None):
                if d2:
                    add_mask(i - 2)
                if d0:
                    x2_of(i, par, half, n0, st)
                if d2:
                    entries(i - 2, par, lst, n2)
                if d0 and n0 == P:
                    mix_lo(i + 1, 1 - par)
                if d1:
                    route(i - 1, n1)
                    shared_act(i - 1, n1)
                if d0:
                    h2_of(i, par, half, n0, first=isinstance(i, int) and i == 0)

            LT = 16 * TOPK
            step_b(0, 0, 0, d1=False, d2=False)
            step_b(1, 1, 0, d2=False)
            step_b(2, 0, 1, st=16)
            step_b(3, 1, 1, st=16)
            with dve.Fori(2, NT // 2) as j:
                for s in range(2):
                    step_b(2 * j + s, s, j, st=16 * j, lst=LT * j - LT)
            dve.wait_ge(S["tailmodB_in"], 16)
            step_b(NT, 0, NT // 2, n0=TAIL, st=8 * NT, lst=LT * (NT // 2 - 1))
            step_b(NT + 1, 1, 0, d0=False, n1=TAIL, lst=LT * (NT // 2 - 1))
            step_b(NT + 2, 0, 0, d0=False, d1=False, n2=TAIL, lst=LT * (NT // 2))

            dve.wait_ge(S["cnt_psum"], 1)
            V.tensor_scalar(cnt[:, 0], psP[:, 0:NE], float(P - 1), None, ALU.add)
            dve.drain()
            V.tensor_copy(cnti[:, 0], cnt[:, 0])
            dve.drain()
            V.tensor_scalar(cnti[:, 1], cnti[:, 0], 7, None, ALU.arith_shift_right)
            dve.drain()
            V.tensor_copy(cnt[:, 1], cnti[:, 1])
            dve.drain()
            V.tensor_tensor_scan(cnt[:, 2], ones[:, 0:NE], cnt[:, 1], 0.0, ALU.mult, ALU.add)
            dve.drain()
            V.tensor_tensor(cnt[:, 3], cnt[:, 2], cnt[:, 1], ALU.subtract)
            V.tensor_scalar(cnt[:, 5], iota[:], float(LB), None, ALU.mult)
            V.tensor_scalar(cnt[:, 6], cnt[:, 1], 1.0, None, ALU.min)
            dve.drain()
            V.tensor_tensor_scan(cnt[:, 7], ones[:, 0:NE], cnt[:, 6], 0.0, ALU.mult, ALU.add)
            dve.drain()
            V.tensor_scalar(efst[0:1, 4:4 + NE], cnt[0:1, 7], 0.0, None, ALU.is_le)
            for h in range(2):
                V.tensor_scalar(blkf[:, h], cnt[:, 2], iotp[:, h:h + 1], None, ALU.is_le)
                V.tensor_scalar(blkf[:, 2 + h], cnt[:, 3], iotp[:, h:h + 1], None, ALU.is_le)
                V.tensor_scalar(bt_t[:, h], cnt[:, 3], iotp[:, h:h + 1], None, ALU.is_equal)
            V.tensor_tensor(cnt[:, 5], cnt[:, 5], cnt[:, 3], ALU.subtract)
            dve.drain()
            V.tensor_reduce(efst[0:1, 1:2], efst[0:1, 4:4 + NE], AX.X, ALU.add)
            dve.drain()
            V.tensor_copy(nord[0:1, 1:2], efst[0:1, 1:2])
            dve.drain().then_inc(S["blk_ready"], 1)
            V.tensor_scalar(cnt[0:1, 4, 0:1], cnt[0:1, 2, NE - 1:NE], -1.0, None, ALU.add)
            V.tensor_scalar(cnt[:, 4, 1:2], cnt[:, 7, NE - 1:NE], -1.0, None, ALU.add)
            V.tensor_copy(nord[0:1, 0:1], cnt[0:1, 7, NE - 1:NE])
            V.tensor_scalar(cnt[:, 0], cnt[:, 7], iotp[:, 0:1], None, ALU.is_le)
            V.tensor_tensor(bt_t[:], bt_t[:], cnt[:, 6].unsqueeze(1).to_broadcast([P, 2, NE]), ALU.mult)
            V.tensor_tensor(blkf[:, 2:4], blkf[:, 2:4], blkf[:, 0:2], ALU.subtract)
            dve.drain()
            V.tensor_copy(nblk[0:1, 1:2], cnt[0:1, 4, 0:1])
            V.tensor_reduce(bsum[:, 0], bt_t[:], AX.X, ALU.add)
            V.memset(bsum[:, 1], 0.0)
            V.tensor_scalar(cnt[:, 7], cnt[:, 7], -1.0, None, ALU.add)
            dve.drain()
            V.tensor_reduce(bsum[:, 1, 0:1], cnt[:, 0], AX.X, ALU.add)
            V.tensor_tensor(bt_t[:], blkf[:, 2:4], cnt[:, 7].unsqueeze(1).to_broadcast([P, 2, NE]), ALU.mult)
            V.tensor_scalar(nblk[0:1, 0:1], nblk[0:1, 1:2], 1, None, ALU.arith_shift_right)
            V.tensor_scalar(bsum[:, 2], iotp[:], -1.0, float(NE * LB), ALU.mult, ALU.add)
            V.tensor_scalar(bsum[:, 3], blkf[:, 0:2, NE - 1], cnt[:, 4, 1:2], None, ALU.mult)
            dve.drain()
            V.tensor_reduce(bsum[:, 4], bt_t[:], AX.X, ALU.add)
            V.tensor_tensor(blkf[:, 2:4], blkf[:, 2:4], cnt[:, 5].unsqueeze(1).to_broadcast([P, 2, NE]), ALU.mult)
            V.tensor_tensor(bsum[:, 2], bsum[:, 2], blkf[:, 0:2, NE - 1], ALU.mult)
            V.tensor_scalar(bsum[:, 1], bsum[:, 1], float(NE - 1), None, ALU.min)
            dve.drain()
            V.tensor_tensor(bsum[:, 4], bsum[:, 4], bsum[:, 3], ALU.add)
            V.tensor_reduce(bsum[:, 5], blkf[:, 2:4], AX.X, ALU.add)
            V.tensor_tensor(bsum[:, 2], bsum[:, 2], iotp[:], ALU.add)
            V.tensor_copy(blki[:, :, 3], bsum[:, 1])
            dve.drain()
            V.tensor_scalar(bsum[:, 6], bsum[:, 4], cnt[:, 4, 1:2], None, ALU.is_lt)
            V.scalar_tensor_tensor(bsum[:, 7], bsum[:, 4], 1.0, bsum[:, 0], ALU.add, ALU.mult)
            V.tensor_tensor(bsum[:, 5], bsum[:, 5], bsum[:, 2], ALU.add)
            V.tensor_copy(blki[:, :, 0], bsum[:, 4])
            dve.drain()
            V.tensor_tensor(bsum[:, 6], bsum[:, 6], bsum[:, 7], ALU.mult)
            V.tensor_copy(blki[:, :, 1], bsum[:, 5])
            dve.drain()
            V.tensor_copy(blki[:, :, 2], bsum[:, 6])
            dve.drain().then_inc(S["blk_ready"], 1)

            def act_d(b, s, free=True):
                dve.wait_ge(S["dtanh"], b + 1)
                if free:
                    dve.wait_ge(S["dactT_psum"], b)
                V.scalar_tensor_tensor(sgD[:, s], sgD[:, s], 1.0, psP[:, s * 512:s * 512 + F], ALU.add, ALU.mult)
                dve.drain()
                V.scalar_tensor_tensor(actD[:], sgD[:, s], 0.5, psP[:, s * 512 + F:s * 512 + 2 * F], ALU.mult, ALU.mult).then_inc(S["dact_ready"], 1)

            def keep_entries(b, s, half):
                dve.wait_ge(S2["lent_in"][s], 16 * half + 16)
                V.tensor_copy(tok_all[:, bass.ds(b, 1)], lent[:, s, 0:1])
                V.tensor_copy(w_all[:, bass.ds(b, 1)], lent[:, s, 1:2].bitcast(F32)).then_inc(S["lent_used"], 1)

            def x_lo(b, s):
                dve.wait_ge(S["xThi_ready"], b + 1)
                V.tensor_tensor(xTlo[:, s].rearrange("p k t -> p (k t)"), psT[:], xThi[:, s].bitcast(F32).rearrange("p k t -> p (k t)"),
                                ALU.subtract).then_inc(S["xTlo_ready"], 1)

            def a_lo(b):
                dve.wait_ge(S["aThi_ready"], b + 1)
                V.tensor_tensor(aTlo[:].rearrange("p j t -> p (j t)"), psQ[:, 0:F], aThi[:].bitcast(F32).rearrange("p j t -> p (j t)"),
                                ALU.subtract).then_inc(S["aTlo_ready"], 1)

            def lower(n, c0, c1, hi, per, done):
                sl = bass.ds(n % 2, 1)
                for c in range(c0, c1):
                    dve.wait_ge(S[hi], n * per + c - c0 + 1)
                    last = V.tensor_tensor(wlo[:, sl, c * 1024:(c + 1) * 1024], wraw[:, sl, c * 1024:(c + 1) * 1024],
                                           whi[:, sl, c * 1024:(c + 1) * 1024].bitcast(F32), ALU.subtract)
                last.then_inc(S[done], 1)

            def next_gu(b):
                n = dve.value_load(blkr[0:1, bass.ds(b, 1), 2:3], min_val=0, max_val=NE - 1)
                with dve.If(n > 0):
                    lower(n, 0, 4, "hi_gu", 4, "lo_gu")

            def next_dn(b):
                n = dve.value_load(dnt[0:1, bass.ds(b, 1)], min_val=0, max_val=NE - 1)
                with dve.If(n > 0):
                    lower(n, 4, 6, "hi_dn", 2, "lo_dn")

            dve.wait_ge(S["blkr_in"], 16)
            V.tensor_copy(dnf[:, 0], blkr[:, :, 2])
            V.tensor_copy(dnf[:, 1], blkr[:, :, 0])
            V.memset(dnf[:, 4], 0.0)
            dve.drain()
            V.tensor_tensor(dnf[:, 2, 1:], dnf[:, 1, 1:], dnf[:, 1, :-1], ALU.not_equal)
            dve.drain()
            V.tensor_scalar(dnf[:, 3, 1:], dnf[:, 2, 1:], -1.0, 1.0, ALU.mult, ALU.add)
            V.tensor_tensor(dnf[:, 4, 1:], dnf[:, 0, :-1], dnf[:, 2, 1:], ALU.mult)
            dve.drain()
            V.tensor_tensor(dnf[:, 3, 1:-1], dnf[:, 0, :-2], dnf[:, 3, 1:-1], ALU.mult)
            dve.drain()
            V.tensor_tensor(dnf[:, 4, 2:], dnf[:, 4, 2:], dnf[:, 3, 1:-1], ALU.add)
            dve.drain()
            V.tensor_copy(dnt[:], dnf[:, 4])
            dve.drain()
            for b in range(4):
                keep_entries(b, b % 2, b // 2)
            lower(0, 0, 4, "hi_gu", 4, "lo_gu")
            lower(0, 4, 6, "hi_dn", 2, "lo_dn")
            x_lo(0, 0)
            x_lo(1, 1)
            next_gu(0)
            act_d(0, 0, free=False)
            last_pair = dve.value_load(nblk[0:1, 0:1], min_val=0, max_val=NB // 2 - 1)
            next_gu(1)
            a_lo(0)
            keep_entries(4, 0, 2)
            x_lo(2, 0)
            next_dn(1)
            act_d(1, 1)
            next_gu(2)
            for s in range(2):
                a_lo(1 + s)
                keep_entries(5 + s, 1 - s, 2 + s)
                x_lo(3 + s, 1 - s)
                next_dn(2 + s)
                act_d(2 + s, s)
                next_gu(3 + s)
            with dve.Fori(2, NB // 2) as j:
                with dve.If(j < last_pair + 1):
                    for s in range(2):
                        a_lo(2 * j + s - 1)
                        keep_entries(2 * j + s + 3, 1 - s, j + 1 + s)
                        x_lo(2 * j + s + 1, 1 - s)
                        next_dn(2 * j + s)
                        act_d(2 * j + s, s)
                        next_gu(2 * j + s + 1)
            a_lo(last_pair * 2 + 1)

            def out_e(t, s, q, n=P, stored=True, g=0):
                dve.wait_ge(S4["xe_in"][s], 32 * q + 32)
                V.tensor_tensor(acc[0:n, s], acc[0:n, s], g2b[0:n, g], ALU.mult)
                dve.drain()
                if stored:
                    dve.wait_ge(S4["out_st"][s], 16 * q)
                V.tensor_tensor(ye[0:n, s], acc[0:n, s], xe[0:n, s], ALU.add).then_inc(S["ye_ready"], 1)

            dve.wait_ge(S["g2_in"], 32)
            for s in range(4):
                out_e(s, s, 0, stored=False)
            with dve.Fori(1, NT // 4) as q:
                for s in range(4):
                    out_e(4 * q + s, s, q)
            out_e(NT, 0, NT // 4, n=TAIL, g=1)

        @block.tensor
        def _(pe):
            T = nc.tensor
            pe.wait_ge(S["const_ready"], 1)
            pe.wait_ge(S["csil_ready"], 1)
            def ada_chunks(j):
                for s in range(2):
                    pe.wait_ge(S2["ada_in"][s], 16 * j + 16)
                    pe.wait_ge(S["mod_bank_free"], 2 * j + s + 1)
                    for k in range(KC):
                        last = T.matmul(psT[0:TAIL + 1, s * 512:s * 512 + 512], csil[:, k], ada_wt[:, s, k], start=k == 0, stop=k == KC - 1)
                    last.then_inc(S["ada_psum_ready"], 1)

            ada_chunks(0)
            pe.wait_ge(S["prm_in"], 16 * 7)
            for c in range(RC):
                last = T.transpose(psP[:, c * 40:(c + 1) * 40], prm_r[:, c * P:(c + 1) * P], ident[0:40, 0:40])
            last.then_inc(S["prm_psum"], 1)
            with pe.Fori(1, NCH // 2) as j:
                ada_chunks(j)
            pe.wait_ge(S["gate_w_in"], 64)

            def h_transpose(i, n=P, first=False):
                pe.wait_ge(S["h_ready"], i + 1)
                if not first:
                    pe.wait_ge(S["hT_ready"], i)
                hv = hrow[0:n].rearrange("p (m k) -> p k m", k=KC)
                for k in range(KC):
                    last = T.transpose(psT[:, k * P:k * P + n], hv[:, k], ident[0:n, 0:n])
                last.then_inc(S["hT_psum"], 1)

            def branch(i, bank, col, n, done, chunks=range(RC)):
                for c in chunks:
                    for k in range(KC):
                        last = T.matmul(psP[:, bank * 512 + c * P:bank * 512 + c * P + n], win[:, k, col + c * P:col + (c + 1) * P],
                                        hT[:, k, 0:n], start=k == 0, stop=k == KC - 1)
                if done is not None:
                    last.then_inc(done, 1)

            def qkv_part(i, c0, c1, n, done):
                for k in range(KC):
                    last = T.matmul(psQ[0:n, c0:c1], hT[:, k, 0:n], win[:, k, 2 * R + c0:2 * R + c1], start=k == 0, stop=k == KC - 1)
                last.then_inc(done, 1)

            def qk_transpose(a, n=P):
                pe.wait_ge(S["qn_ready"], a + 1)
                for g in range(GQ):
                    T.transpose(psT[:, g * P:g * P + n], qn[0:n, g * P:(g + 1) * P], ident[0:n, 0:n])
                T.transpose(psT[:, 4 * P:4 * P + n], qn[0:n, QD:], ident[0:n, 0:n]).then_inc(S["qkT_psum"], 1)

            def qk(n, h, cur, first=False):
                rows = slice(HD * h, HD * h + HD)
                for g in range(GQ):
                    for where, slot in ((0, 1 - cur), (1, cur)):
                        if first and where == 0:
                            continue
                        last = T.matmul(psS[:, g * 256 + where * P:g * 256 + where * P + P], qT[rows, g], kT[rows, slot], start=True, stop=True)
                last.then_inc(S["s_psum"], 1)

            def p_transpose(n, h):
                pe.wait_ge(S["p_ready"], 2 * n + h + 1)
                for g in range(GQ):
                    for b in range(2):
                        last = T.transpose(psT[:, (2 * g + b) * P:(2 * g + b + 1) * P], sc[:, h, g, b * P:(b + 1) * P], ident[:])
                last.then_inc(S["pT_psum"], 1)

            def pv(n, h, cur, first=False):
                pe.wait_ge(S["pT_ready"], 2 * n + h + 1)
                for g in range(GQ):
                    for b, slot in ((0, 1 - cur), (1, cur)):
                        if first and b == 0:
                            continue
                        last = T.matmul(psQ[:, 768 + g * HD:768 + (g + 1) * HD], PT[:, g, b], vb[:, slot, HD * h:HD * h + HD],
                                        start=b == 0 or first, stop=b == 1)
                last.then_inc(S["o_psum"], 1)

            def o_transpose(n):
                pe.wait_ge(S["o_ready"], 2 * n + 2)
                for c in range(RC):
                    last = T.transpose(psS[:, c * P:(c + 1) * P], orow[:, c * P:(c + 1) * P], ident[:])
                last.then_inc(S["oT_psum"], 1)

            def step(i, par, proj=True, att=True, nxt=True, first=False, n=P, n_next=P):
                a, cur = i - 1, 1 - par
                if proj:
                    pe.wait_ge(S["hT_ready"], i + 1)
                    if att:
                        pe.wait_ge(S["gates_sum"], i)
                    branch(i, 0, 0, n, S["xr_psum"])
                if att:
                    qk_transpose(a)
                if proj:
                    branch(i, 1, R, n, None, range(0, 2))
                if att:
                    pe.wait_ge(S["qkT_ready"], a + 1)
                    if not first:
                        pe.wait_ge(S["oT_ready"], a)
                    qk(a, 0, cur, first)
                if proj:
                    branch(i, 1, R, n, S["yr_psum"], range(2, 4))
                    pe.wait_ge(S["conv_ready"], i + 1)
                    pe.wait_ge(S["xr_ready"], i + 1)
                    pe.wait_ge(S["y_ready"], i + 1)
                    for g in range(2):
                        for c in range(RC):
                            last = T.matmul(psP[:, (g * RC + c) * P:(g * RC + c) * P + n], gwt[:, g, c], u[:, c, 0:n], start=True, stop=True)
                    last.then_inc(S["gates_psum"], 1)
                if att:
                    p_transpose(a, 0)
                    pe.wait_ge(S["s_read"], 2 * a + 1)
                    qk(a, 1, cur, first)
                    pe.wait_ge(S["v_ready"], a + 1)
                    if not first:
                        pe.wait_ge(S["o_ready"], 2 * a)
                    pv(a, 0, cur, first)
                if proj:
                    if att:
                        pe.wait_ge(S["qkv_ready"], i)
                    qkv_part(i, 0, 512, n, S["qkv1_psum"])
                if att:
                    pe.wait_ge(S["pT_ready"], 2 * a + 1)
                    p_transpose(a, 1)
                if proj:
                    if att:
                        pe.wait_ge(S["o_ready"], 2 * a + 1)
                    qkv_part(i, 512, QKV, n, S["qkv2_psum"])
                if nxt:
                    if att:
                        pe.wait_ge(S["pT_ready"], 2 * a + 2)
                    h_transpose(i + 1, n_next)
                if att:
                    pe.wait_ge(S["o_ready"], 2 * a + 1)
                    if proj:
                        pe.wait_ge(S["qkv_ready"], i + 1)
                    pv(a, 1, cur, first)
                    o_transpose(a)

            pe.wait_ge(S["prm_ready"], 1)
            pe.wait_ge(S["mod_row_ready"], NCH)
            h_transpose(0, first=True)
            pe.wait_ge(S["win_in"], 80)
            step(0, 0, att=False)
            step(1, 1, first=True)
            with pe.Fori(1, NT // 2 - 1) as j:
                for s in range(2):
                    step(2 * j + s, s)
            step(NT - 2, 0)
            step(NT - 1, 1, n_next=TAIL)
            step(NT, 0, nxt=False, n=TAIL)
            qk_transpose(NT, TAIL)
            pe.wait_ge(S["outr_ready"], NT + 1)
            pe.wait_ge(S["qkv_ready"], NT + 1)
            for c in range(RC):
                last = T.transpose(psQ[0:36, c * P:(c + 1) * P], stt[:, c], ident[:])
            last.then_inc(S["small_psum"], 1)
            pe.wait_ge(S["smp_in"], 32)
            pe.wait_ge(S["gates_sum"], NT + 1)
            for b in range(NS):
                last = T.transpose(psP[:, b * P:(b + 1) * P], ck8[:, b], ident[:])
            last.then_inc(S["ckT_psum"], 1)
            pe.wait_ge(S["qkT_ready"], NT + 1)
            pe.wait_ge(S["ckT_ready"], 1)
            pe.wait_ge(S["oT_ready"], NT)
            for b in range(NS):
                half, q = divmod(b, 4)
                for h in range(NKV):
                    rows, col = slice(HD * h, HD * h + HD), h * 512 + half * 256
                    T.matmul(psS[32 * q:32 * q + 32, col:col + P], qTs[rows, b], kT8[rows, b], start=True, stop=True)
                    last = T.matmul(psS[32 * q:32 * q + 32, col + P:col + P + TAIL], qTs[rows, b], kTn[rows], start=True, stop=True)
            last.then_inc(S["smp_psum"], 1)
            pe.wait_ge(S["smp_act"], SMP_P)
            for c in range(2 * NKV):
                half, h = divmod(c, NKV)
                T.transpose(psT[:, c * P:(c + 1) * P], scS[:, half, h, 0:P], ident[:])
                last = T.transpose(psT[0:TAIL, 512 + c * P:512 + (c + 1) * P], scS[:, half, h, P:], ident[:])
            last.then_inc(S["smp_psum"], 1)
            pe.wait_ge(S["smp_act"], SMP_PT_OUT)
            pe.wait_ge(S["o_ready"], 2 * NT)
            for b in range(NS):
                half, q = divmod(b, 4)
                for h in range(NKV):
                    c = half * NKV + h
                    out = psQ[32 * q:32 * q + 32, 768 + c * HD:768 + (c + 1) * HD]
                    T.matmul(out, PTs[:, c, 32 * q:32 * q + 32], vb8[:, b, HD * h:HD * h + HD], start=True, stop=False)
                    last = T.matmul(out, PTn[:, c, 32 * q:32 * q + 32], qkv[0:TAIL, QD + KVD + HD * h:QD + KVD + HD * h + HD],
                                    start=False, stop=True)
            last.then_inc(S["smp_psum"], 1)
            pe.wait_ge(S["smp_dve"], SMP_OROW)
            for half in range(2):
                last = T.transpose(psT[:, half * P:(half + 1) * P], orowS[:, half], ident[:])
            last.then_inc(S["smp_psum"], 1)
            pe.wait_ge(S["small_ready"], 1)
            pe.wait_ge(S["smp_act"], SMP_OT_OUT)

            def mixed(i, par, h, half, n, first=False):
                if h == 0:
                    pe.wait_ge(S["b_lo"], i + 2)
                    if not first:
                        pe.wait_ge(S["x2_ready"], i)
                for c in range(2 * RC):
                    for x, w in ((mxhi, wohi), (mxhi, wolo), (mxlo, wohi)):
                        last = T.matmul(psQ[0:n, h * 512:h * 512 + 512], x[:, c, 0:n], w[:, c, h * 512:h * 512 + 512],
                                        start=c == 0 and x is mxhi and w is wohi, stop=c == 2 * RC - 1 and x is mxlo)
                if h == 1:
                    last.then_inc(S["mixed_psum"], 1)

            def step_b(i, par, half, d0=True, d1=True, d2=True, n0=P, n1=P, n2=P, first0=False, first1=False):
                if d0:
                    mixed(i, par, 0, half, n0, first0)
                if d2:
                    pe.wait_ge(S["act_ready"], i - 1)
                    pe.wait_ge(S["rtanh"], i - 1)
                    av = actr[0:n2].rearrange("p (m j) -> p j m", j=2)
                    for jj in range(2):
                        T.transpose(psP[:, 768 + jj * P:768 + jj * P + n2], av[:, jj], ident[0:n2, 0:n2])
                    pe.wait_ge(S["msk_ready"], i - 1)
                    pe.wait_ge(S["mrun_ready"], i - 1)
                    T.matmul(psP[:, 640:640 + NE], tri[:], msk_all[:, i - 2], start=True, stop=False)
                    T.matmul(psP[:, 640:640 + NE], ones[:], mrun[:], start=False, stop=True).then_inc(S["pos_psum"], 1)
                if d1:
                    pe.wait_ge(S["h2_ready"], i)
                    if not first1:
                        pe.wait_ge(S["h2T_ready"], i - 1)
                    hv = h2[0:n1].rearrange("p (m k) -> p k m", k=KC)
                    for k in range(KC):
                        last = T.transpose(psT[:, k * P:k * P + n1], hv[:, k], ident[0:n1, 0:n1])
                    last.then_inc(S["h2T_psum"], 1)
                if d0:
                    mixed(i, par, 1, half, n0)
                if d2:
                    pe.wait_ge(S["actT_ready"], i - 1)
                    if not (isinstance(i, int) and i == 2):
                        pe.wait_ge(S["sh_ready"], i - 2)
                    for h in range(2):
                        for jj in range(2):
                            last = T.matmul(psS[0:n2, h * 512:h * 512 + 512], actT[:, jj, 0:n2], shd[:, jj, h * 512:h * 512 + 512],
                                            start=jj == 0, stop=jj == 1)
                    last.then_inc(S["shd_psum"], 1)
                if d1:
                    if first1:
                        pe.wait_ge(S["wB_in"], 16 * 5)
                    pe.wait_ge(S["h2T_ready"], i)
                    if not first1:
                        pe.wait_ge(S["act_ready"], i - 1)
                    for k in range(KC):
                        last = T.matmul(psP[0:n1, 512:512 + NE], h2T[:, k, 0:n1], rw[:, k], start=k == 0, stop=k == KC - 1)
                    last.then_inc(S["router_psum"], 1)
                    for k in range(KC):
                        last = T.matmul(psP[0:n1, 0:2 * F], h2T[:, k, 0:n1], shgu[:, k], start=k == 0, stop=k == KC - 1)
                    last.then_inc(S["shup_psum"], 1)

            step_b(0, 0, 0, d1=False, d2=False, first0=True)
            step_b(1, 1, 0, d2=False, first1=True)
            step_b(2, 0, 1)
            step_b(3, 1, 1)
            with pe.Fori(2, NT // 2) as j:
                for s in range(2):
                    step_b(2 * j + s, s, j)
            step_b(NT, 0, NT // 2, n0=TAIL)
            step_b(NT + 1, 1, 0, d0=False, n1=TAIL)
            step_b(NT + 2, 0, 0, d0=False, d1=False, n2=TAIL)
            pe.wait_ge(S["mrun_ready"], ALL + 1)
            pe.wait_ge(S["act_ready"], ALL)
            T.matmul(psP[:, 0:NE], ones[:], mrun[:], start=True, stop=True).then_inc(S["cnt_psum"], 1)

            def x_tr(b, s, pairs):
                pe.wait_ge(S2["gather_in"][s], pairs)
                xv = xg[:, s].rearrange("p (m k) -> p k m", k=KC)
                for k in range(KC):
                    last = T.transpose(psT[:, k * P:(k + 1) * P], xv[:, k], ident[:])
                last.then_inc(S["xgT_psum"], 1)

            def up(b, s, free=True):
                n = pe.value_load(blkr[0:1, bass.ds(b, 1), 0:1], min_val=0, max_val=NE - 1)
                pe.wait_ge(S["lo_gu"], n + 1)
                pe.wait_ge(S["xTlo_ready"], b + 1)
                if free:
                    pe.wait_ge(S["dact_ready"], b - 1)
                slot = bass.ds(n % 2, 1)
                for k in range(KC):
                    for x, w in ((xThi, whi), (xThi, wlo), (xTlo, whi)):
                        wk = w[:, slot, 0:GU].rearrange("p a (m c) -> p a m c", m=2)[:, :, :, k * F:(k + 1) * F]
                        last = T.matmul(psP[:, s * 512:s * 512 + 2 * F], x[:, s, k], wk,
                                        start=k == 0 and x is xThi and w is whi, stop=k == KC - 1 and x is xTlo)
                last.then_inc(S["up_psum"], 1)

            def a_tr(b):
                pe.wait_ge(S["dact_ready"], b + 1)
                av = actD[:].rearrange("p (m j) -> p j m", j=2)
                for jj in range(2):
                    last = T.transpose(psQ[:, jj * P:(jj + 1) * P], av[:, jj], ident[:])
                last.then_inc(S["dactT_psum"], 1)

            def down(b, free=True):
                n = pe.value_load(blkr[0:1, bass.ds(b, 1), 0:1], min_val=0, max_val=NE - 1)
                pe.wait_ge(S["lo_dn"], n + 1)
                pe.wait_ge(S["aTlo_ready"], b + 1)
                if free:
                    pe.wait_ge(S["ysb_ready"], b)
                slot = bass.ds(n % 2, 1)
                for h in range(2):
                    for jj in range(2):
                        col = GU + jj * D + h * 512
                        for x, w in ((aThi, whi), (aThi, wlo), (aTlo, whi)):
                            last = T.matmul(psS[:, h * 512:h * 512 + 512], x[:, jj], w[:, slot, col:col + 512],
                                            start=jj == 0 and x is aThi and w is whi, stop=jj == 1 and x is aTlo)
                last.then_inc(S["down_psum"], 1)

            pe.wait_ge(S["blkr_in"], 16)
            x_tr(0, 0, 16)
            up(0, 0, free=False)
            pe.wait_ge(S["xTlo_ready"], 1)
            x_tr(1, 1, 16)
            up(1, 1, free=False)
            a_tr(0)
            pe.wait_ge(S["xTlo_ready"], 2)
            x_tr(2, 0, 32)
            down(0, free=False)
            last_pair = pe.value_load(nblk[0:1, 0:1], min_val=0, max_val=NB // 2 - 1)
            with pe.Fori(1, NB // 2) as j:
                with pe.If(j < last_pair + 1):
                    for s in range(2):
                        b = 2 * j + s
                        up(b, s)
                        a_tr(b - 1)
                        x_tr(b + 1, 1 - s, 16 * (j + 1 + s))
                        down(b - 1)
            a_tr(last_pair * 2 + 1)
            down(last_pair * 2 + 1)


_INS = ["x_prompt", "x_sample", "c_prompt", "c_sample", "cache_k_win", "cache_v_win", "state_conv",
        "state_rnn", "ada_w", "ada_b", "norm_mix", "w_in", "conv_w", "conv_b", "gate_a_w", "gate_a_b",
        "gate_x_w", "gate_x_b", "lru_lambda", "q_norm", "k_norm", "attn_sinks", "w_out", "norm_ffn",
        "router_w", "router_bias", "exp_w_gate", "exp_w_up", "exp_w_down", "sh_w_gate", "sh_w_up",
        "sh_w_down"]
_OUTS = [(1, 2048, 1024), (8, 4, 1024), (1, 1, 128, 2, 64), (1, 1, 128, 2, 64), (1, 1, 3, 512), (1, 1, 512),
         (1, 8, 128, 2, 64), (1, 8, 128, 2, 64), (1, 8, 3, 512), (1, 8, 512)]


def kernel(**inputs):
    import numpy as _np
    import concourse.bacc as _bacc
    from concourse import mybir as _mybir
    from concourse.bass_utils import run_bass_kernel_spmd as _run

    nc = _bacc.Bacc("TRN2", target_bir_lowering=False, num_devices=1)
    arrays, args = {}, []
    for name in _INS:
        a = _np.ascontiguousarray(inputs[name])
        arrays[f"in_{name}_dram"] = a
        args.append(nc.dram_tensor(f"in_{name}_dram", a.shape, _mybir.dt.from_np(a.dtype), kind="ExternalInput").ap())
    for i, shape in enumerate(_OUTS):
        args.append(nc.dram_tensor(f"out_{i}_dram", shape, _mybir.dt.float32, kind="ExternalOutput").ap())
    program(nc, *args)
    r = _run(nc, [arrays], core_ids=[0])
    return tuple(r.results[0][f"out_{i}_dram"] for i in range(len(_OUTS)))
```
